# Optimizing a Trainium2 kernel written in Bass

```python
import math
import jax, jax.numpy as jnp
from jax import lax
import numpy as np

D_MODEL = 1024
BATCH = 1
SEQ = 512
DEPTH = 1

POOL_WINDOWS = (2, 4, 8, 16)
N_POOL_GROUPS = len(POOL_WINDOWS)
POOL_GROUP_DIM = D_MODEL // 8
POOL_WIDTH = N_POOL_GROUPS * POOL_GROUP_DIM

SSD_WIDTH = D_MODEL
SSD_HEAD_DIM = 64
SSD_HEADS = SSD_WIDTH // SSD_HEAD_DIM
SSD_GROUPS = 2
HEADS_PER_GROUP = SSD_HEADS // SSD_GROUPS
SSD_STATE = 128
SSD_CONV = 4
SSD_CHUNK = 128
CONV_DIM = SSD_WIDTH + 2 * SSD_GROUPS * SSD_STATE

MIX_WIDTH = POOL_WIDTH + SSD_WIDTH
IN_PROJ_DIM = POOL_WIDTH + SSD_WIDTH + CONV_DIM + SSD_HEADS

PEER_HEADS = 8
PEER_TOPK = 16
N_KEYS = 128
N_EXPERTS = N_KEYS * N_KEYS
D_KEY = 256
PEER_BLOCK = 128

N_MOD = 6
EPS = 1e-6


def rmsnorm(x, g):
    xf = x.astype(jnp.float32)
    y = xf * lax.rsqrt(jnp.mean(xf * xf, axis=-1, keepdims=True) + EPS)
    return (y * g.astype(jnp.float32)).astype(x.dtype)

def modulate(h, shift, scale):
    return h * (1 + scale[:, None, :]) + shift[:, None, :]

def pool_mixer(u, pool_w, pool_b, pool_scale):
    Bsz, S, _ = u.shape
    ug = u.astype(jnp.float32).reshape(Bsz, S, N_POOL_GROUPS, POOL_GROUP_DIM)
    cs = jnp.cumsum(ug, axis=1)
    t = jnp.arange(S)
    pooled = []
    for gi, w in enumerate(POOL_WINDOWS):
        csg = cs[:, :, gi]
        cs_pad = jnp.pad(csg, ((0, 0), (w, 0), (0, 0)))
        win_sum = cs_pad[:, w:] - cs_pad[:, :S]
        count = jnp.minimum(t + 1, w).astype(jnp.float32)[None, :, None]
        pooled.append(win_sum / count)
    pooled = jnp.stack(pooled, axis=2)
    mixed = pooled - ug
    y = jnp.einsum("bsgc,gcd->bsgd", mixed, pool_w.astype(jnp.float32)) + pool_b.astype(jnp.float32)
    y = y * pool_scale.astype(jnp.float32)
    return y.reshape(Bsz, S, POOL_WIDTH).astype(u.dtype)

def ssd_chunked(xdt, a, b, c):
    Bsz, S, G, R, P = xdt.shape
    N = b.shape[-1]
    L = SSD_CHUNK
    nc = S // L
    xdt = xdt.reshape(Bsz, nc, L, G, R, P)
    b = b.reshape(Bsz, nc, L, G, N)
    c = c.reshape(Bsz, nc, L, G, N)
    a = a.reshape(Bsz, nc, L, G, R).transpose(0, 3, 4, 1, 2)
    a_cs = jnp.cumsum(a, axis=-1)

    causal = jnp.tril(jnp.ones((L, L), dtype=bool))
    seg = a_cs[..., :, None] - a_cs[..., None, :]
    decay = jnp.exp(jnp.where(causal, seg, -jnp.inf))
    cb = jnp.einsum("bclgn,bcsgn->bcgls", c, b)
    y_diag = jnp.einsum("bcgls,bgrcls,bcsgrp->bclgrp", cb, decay, xdt)

    decay_to_end = jnp.exp(a_cs[..., -1:] - a_cs)
    states = jnp.einsum("bclgn,bgrcl,bclgrp->bcgrpn", b, decay_to_end, xdt)
    chunk_decay = jnp.exp(a_cs[..., -1])

    def step(h, inp):
        st, dec = inp
        return h * dec[..., None, None] + st, h

    h0 = jnp.zeros((Bsz, G, R, P, N), jnp.float32)
    _, h_prev = lax.scan(step, h0, (jnp.moveaxis(states, 1, 0), jnp.moveaxis(chunk_decay, -1, 0)))
    y_off = jnp.einsum("bclgn,cbgrpn,bgrcl->bclgrp", c, h_prev, jnp.exp(a_cs))
    return (y_diag + y_off).reshape(Bsz, S, G, R, P)

def ssd_mixer(z, xbc, dt_raw, conv_w, conv_b, dt_bias, a_log, d_skip, ssd_norm):
    Bsz, S, _ = xbc.shape
    dtype = xbc.dtype
    xf = xbc.astype(jnp.float32)
    conv = lax.conv_general_dilated(
        xf, conv_w.astype(jnp.float32).reshape(SSD_CONV, 1, CONV_DIM),
        window_strides=(1,), padding=[(SSD_CONV - 1, 0)],
        dimension_numbers=("NWC", "WIO", "NWC"), feature_group_count=CONV_DIM)
    conv = jax.nn.silu(conv + conv_b.astype(jnp.float32))
    xs = conv[..., :SSD_WIDTH].reshape(Bsz, S, SSD_GROUPS, HEADS_PER_GROUP, SSD_HEAD_DIM)
    bs = conv[..., SSD_WIDTH:SSD_WIDTH + SSD_GROUPS * SSD_STATE].reshape(Bsz, S, SSD_GROUPS, SSD_STATE)
    cs = conv[..., SSD_WIDTH + SSD_GROUPS * SSD_STATE:].reshape(Bsz, S, SSD_GROUPS, SSD_STATE)

    dt = jax.nn.softplus(dt_raw.astype(jnp.float32) + dt_bias.astype(jnp.float32))
    dt = dt.reshape(Bsz, S, SSD_GROUPS, HEADS_PER_GROUP)
    A = -jnp.exp(a_log.astype(jnp.float32)).reshape(SSD_GROUPS, HEADS_PER_GROUP)
    y = ssd_chunked(xs * dt[..., None], dt * A, bs, cs)
    y = y + xs * d_skip.astype(jnp.float32).reshape(SSD_GROUPS, HEADS_PER_GROUP)[..., None]
    y = y.reshape(Bsz, S, SSD_WIDTH) * jax.nn.silu(z.astype(jnp.float32))
    return rmsnorm(y, ssd_norm).astype(dtype)

def peer(h, w_query, sub_keys1, sub_keys2, expert_down, expert_up):
    Bsz, S, D = h.shape
    T = Bsz * S
    hf = h.reshape(T, D)
    q = (hf @ w_query).reshape(T, PEER_HEADS, 2, D_KEY // 2)
    s1 = jnp.einsum("thk,hnk->thn", q[:, :, 0], sub_keys1).astype(jnp.float32)
    s2 = jnp.einsum("thk,hnk->thn", q[:, :, 1], sub_keys2).astype(jnp.float32)
    v1, i1 = lax.top_k(s1, PEER_TOPK)
    v2, i2 = lax.top_k(s2, PEER_TOPK)
    cand = (v1[..., :, None] + v2[..., None, :]).reshape(T, PEER_HEADS, PEER_TOPK * PEER_TOPK)
    cand_idx = (i1[..., :, None] * N_KEYS + i2[..., None, :]).reshape(T, PEER_HEADS, PEER_TOPK * PEER_TOPK)
    top_s, pos = lax.top_k(cand, PEER_TOPK)
    idx = jnp.take_along_axis(cand_idx, pos, axis=-1)
    gates = jax.nn.softmax(top_s, axis=-1).astype(h.dtype)

    nb = T // PEER_BLOCK

    def block_fn(args):
        hb, ib, gb = args
        u = expert_down[ib]
        act = jax.nn.gelu(jnp.einsum("td,thkd->thk", hb, u), approximate=False)
        v = expert_up[ib]
        return jnp.einsum("thk,thkd->td", gb * act, v)

    out = lax.map(block_fn, (hf.reshape(nb, PEER_BLOCK, D),
                             idx.reshape(nb, PEER_BLOCK, PEER_HEADS, PEER_TOPK),
                             gates.reshape(nb, PEER_BLOCK, PEER_HEADS, PEER_TOPK)))
    return out.reshape(Bsz, S, D)

def first_inputs(seed: int = 0) -> dict:
    key = jax.random.key(seed)
    ks = jax.random.split(key, 24)

    def nrm(k, shape, s):
        return jax.random.normal(k, shape, jnp.float32) * s

    x = nrm(ks[0], (BATCH, SEQ, D_MODEL), 1.0)
    c = nrm(ks[1], (BATCH, D_MODEL), 1.0)
    w_ada = nrm(ks[2], (DEPTH, D_MODEL, N_MOD * D_MODEL), 0.5 * D_MODEL ** -0.5)
    b_ada = nrm(ks[3], (DEPTH, N_MOD * D_MODEL), 0.02)
    norm_mix = 1.0 + nrm(ks[4], (DEPTH, D_MODEL), 0.02)
    norm_ffn = 1.0 + nrm(ks[5], (DEPTH, D_MODEL), 0.02)
    w_in = nrm(ks[6], (DEPTH, D_MODEL, IN_PROJ_DIM), D_MODEL ** -0.5)
    pool_w = nrm(ks[7], (DEPTH, N_POOL_GROUPS, POOL_GROUP_DIM, POOL_GROUP_DIM), POOL_GROUP_DIM ** -0.5)
    pool_b = nrm(ks[8], (DEPTH, N_POOL_GROUPS, POOL_GROUP_DIM), 0.02)
    pool_scale = 1.0 + nrm(ks[9], (DEPTH, N_POOL_GROUPS, POOL_GROUP_DIM), 0.1)
    conv_w = nrm(ks[10], (DEPTH, SSD_CONV, CONV_DIM), SSD_CONV ** -0.5)
    conv_b = nrm(ks[11], (DEPTH, CONV_DIM), 0.02)
    dt0 = jnp.exp(jax.random.uniform(ks[12], (DEPTH, SSD_HEADS), jnp.float32,
                                     minval=math.log(1e-3), maxval=math.log(1e-1)))
    dt_bias = dt0 + jnp.log(-jnp.expm1(-dt0))
    a_log = jnp.log(jax.random.uniform(ks[13], (DEPTH, SSD_HEADS), jnp.float32, minval=1.0, maxval=16.0))
    d_skip = 1.0 + nrm(ks[14], (DEPTH, SSD_HEADS), 0.1)
    ssd_norm = 1.0 + nrm(ks[15], (DEPTH, SSD_WIDTH), 0.02)
    w_out = nrm(ks[16], (DEPTH, MIX_WIDTH, D_MODEL), MIX_WIDTH ** -0.5)
    w_query = nrm(ks[17], (DEPTH, D_MODEL, PEER_HEADS * D_KEY), D_MODEL ** -0.5)
    sub_keys1 = nrm(ks[18], (DEPTH, PEER_HEADS, N_KEYS, D_KEY // 2), (D_KEY // 2) ** -0.5)
    sub_keys2 = nrm(ks[19], (DEPTH, PEER_HEADS, N_KEYS, D_KEY // 2), (D_KEY // 2) ** -0.5)
    expert_down = nrm(ks[20], (DEPTH, N_EXPERTS, D_MODEL), D_MODEL ** -0.5)
    expert_up = nrm(ks[21], (DEPTH, N_EXPERTS, D_MODEL), PEER_HEADS ** -0.5)
    norm_final = 1.0 + nrm(ks[22], (D_MODEL,), 0.02)
    return {"x": x, "c": c, "w_ada": w_ada, "b_ada": b_ada, "norm_mix": norm_mix, "norm_ffn": norm_ffn,
            "w_in": w_in, "pool_w": pool_w, "pool_b": pool_b, "pool_scale": pool_scale,
            "conv_w": conv_w, "conv_b": conv_b, "dt_bias": dt_bias, "a_log": a_log, "d_skip": d_skip,
            "ssd_norm": ssd_norm, "w_out": w_out, "w_query": w_query, "sub_keys1": sub_keys1,
            "sub_keys2": sub_keys2, "expert_down": expert_down, "expert_up": expert_up,
            "norm_final": norm_final}

def first_block(x, c, w_ada, b_ada, norm_mix, norm_ffn, w_in, pool_w, pool_b, pool_scale,
              conv_w, conv_b, dt_bias, a_log, d_skip, ssd_norm, w_out, w_query, sub_keys1,
              sub_keys2, expert_down, expert_up, norm_final):
    Bsz = x.shape[0]
    c_act = jax.nn.silu(c)
    s_z = POOL_WIDTH
    s_xbc = POOL_WIDTH + SSD_WIDTH
    s_dt = POOL_WIDTH + SSD_WIDTH + CONV_DIM
    for l in range(DEPTH):
        mod = (c_act @ w_ada[l] + b_ada[l]).reshape(Bsz, N_MOD, D_MODEL)
        shift_m, scale_m, gate_m, shift_f, scale_f, gate_f = [mod[:, i] for i in range(N_MOD)]

        h = modulate(rmsnorm(x, norm_mix[l]), shift_m, scale_m)
        proj = h @ w_in[l]
        y_pool = pool_mixer(proj[..., :s_z], pool_w[l], pool_b[l], pool_scale[l])
        y_ssd = ssd_mixer(proj[..., s_z:s_xbc], proj[..., s_xbc:s_dt], proj[..., s_dt:],
                          conv_w[l], conv_b[l], dt_bias[l], a_log[l], d_skip[l], ssd_norm[l])
        y = jnp.concatenate([y_pool, y_ssd], axis=-1) @ w_out[l]
        x = x + gate_m[:, None, :] * y

        h = modulate(rmsnorm(x, norm_ffn[l]), shift_f, scale_f)
        y = peer(h, w_query[l], sub_keys1[l], sub_keys2[l], expert_down[l], expert_up[l])
        x = x + gate_f[:, None, :] * y
    return rmsnorm(x, norm_final)


N_META = 16
CHUNK = 64
N_PAD = CHUNK - N_META
GLA_HEADS = 4
GLA_DK = 128
GLA_DV = 256
GLA_KEY = GLA_HEADS * GLA_DK
GLA_VAL = GLA_HEADS * GLA_DV
GATE_RANK = 16
GATE_TAU = 16.0
SSM_WIDTH = D_MODEL
SSM_GROUP = 16
SSM_GROUPS = SSM_WIDTH // SSM_GROUP
SSM_STATE = 64
D_FF = 4 * D_MODEL

Q_END = GLA_KEY
K_END = Q_END + GLA_KEY
V_END = K_END + GLA_VAL
R_END = V_END + GLA_VAL
A_END = R_END + GATE_RANK
U_END = A_END + SSM_WIDTH
G1_END = U_END + D_MODEL
IN_WIDTH = G1_END + D_MODEL


def rmsnorm_2(x, g):
    xf = x.astype(jnp.float32)
    ms = jnp.mean(xf * xf, axis=-1, keepdims=True)
    return (xf * lax.rsqrt(ms + EPS) * g.astype(jnp.float32)).astype(x.dtype)

def gla_chunked(q, k, v, log_a):
    bsz, p, h, dk = q.shape
    dv = v.shape[-1]
    nc = p // CHUNK

    def to_chunks(t):
        return t.reshape(bsz, nc, CHUNK, h, t.shape[-1]).transpose(1, 0, 3, 2, 4)

    qc, kc, vc = to_chunks(q), to_chunks(k), to_chunks(v)
    b = jnp.cumsum(to_chunks(log_a).astype(jnp.float32), axis=3)
    b_ref = b[:, :, :, CHUNK // 2:CHUNK // 2 + 1, :]
    q_in = qc * jnp.exp(b - b_ref)
    k_in = kc * jnp.exp(b_ref - b)
    mask = jnp.tril(jnp.ones((CHUNK, CHUNK), dtype=bool))
    scores = jnp.where(mask, jnp.einsum('nbhid,nbhjd->nbhij', q_in, k_in), 0.0)
    o_intra = jnp.einsum('nbhij,nbhjv->nbhiv', scores, vc.astype(jnp.float32))

    b_last = b[:, :, :, -1:, :]
    q_inter = qc * jnp.exp(b)
    k_state = kc * jnp.exp(b_last - b)
    decay_chunk = jnp.exp(b_last[:, :, :, 0, :])

    def step(state, inp):
        qi, ks, vv, dc = inp
        o = jnp.einsum('bhid,bhdv->bhiv', qi, state)
        new_state = dc[..., None] * state + jnp.einsum('bhjd,bhjv->bhdv', ks, vv.astype(jnp.float32))
        return new_state, o

    s0 = jnp.zeros((bsz, h, dk, dv), jnp.float32)
    _, o_inter = lax.scan(step, s0, (q_inter, k_state, vc, decay_chunk))
    o = (o_intra + o_inter).transpose(1, 0, 3, 2, 4).reshape(bsz, p, h, dv)
    return o.astype(v.dtype)

def _complex_combine(e1, e2):
    a1r, a1i, b1r, b1i = e1
    a2r, a2i, b2r, b2i = e2
    return (a2r * a1r - a2i * a1i,
            a2r * a1i + a2i * a1r,
            a2r * b1r - a2i * b1i + b2r,
            a2r * b1i + a2i * b1r + b2i)

def s5_ssm(u, a_re, a_im, log_step, b_re, b_im, c_re, c_im, d_skip):
    bsz, p, _ = u.shape
    g, n, hg = SSM_GROUPS, SSM_STATE, SSM_GROUP
    ar = a_re.astype(jnp.float32)
    ai = a_im.astype(jnp.float32)
    dt = jnp.exp(log_step.astype(jnp.float32))[:, None]
    mag = jnp.exp(ar * dt)
    lam_re, lam_im = mag * jnp.cos(ai * dt), mag * jnp.sin(ai * dt)
    zr, zi = lam_re - 1.0, lam_im
    den = ar * ar + ai * ai
    fr = (zr * ar + zi * ai) / den
    fi = (zi * ar - zr * ai) / den
    br, bi = b_re.astype(jnp.float32), b_im.astype(jnp.float32)
    bb_re = fr[..., None] * br - fi[..., None] * bi
    bb_im = fr[..., None] * bi + fi[..., None] * br
    cr, ci = c_re.astype(jnp.float32), c_im.astype(jnp.float32)

    nc = p // CHUNK
    uc = u.reshape(bsz, nc, CHUNK, g, hg).transpose(1, 0, 2, 3, 4)
    lam_b_re = jnp.broadcast_to(lam_re, (bsz, CHUNK, g, n))
    lam_b_im = jnp.broadcast_to(lam_im, (bsz, CHUNK, g, n))

    def step(carry, u_blk):
        h_re, h_im = carry
        uf = u_blk.astype(jnp.float32)
        bu_re = jnp.einsum('bcgh,gnh->bcgn', uf, bb_re)
        bu_im = jnp.einsum('bcgh,gnh->bcgn', uf, bb_im)
        acc_re, acc_im, x_re, x_im = lax.associative_scan(
            _complex_combine, (lam_b_re, lam_b_im, bu_re, bu_im), axis=1)
        s_re = x_re + acc_re * h_re[:, None] - acc_im * h_im[:, None]
        s_im = x_im + acc_re * h_im[:, None] + acc_im * h_re[:, None]
        y = jnp.einsum('bcgn,ghn->bcgh', s_re, cr) - jnp.einsum('bcgn,ghn->bcgh', s_im, ci)
        return (s_re[:, -1], s_im[:, -1]), y

    carry0 = (jnp.zeros((bsz, g, n), jnp.float32), jnp.zeros((bsz, g, n), jnp.float32))
    _, y = lax.scan(step, carry0, uc)
    y = y.transpose(1, 0, 2, 3, 4).reshape(bsz, p, g * hg)
    return (y + d_skip.astype(jnp.float32) * u.astype(jnp.float32)).astype(u.dtype)

def second_inputs(seed: int = 0) -> dict:
    key = jax.random.key(seed)
    ks = jax.random.split(key, 24)
    nrm = lambda k, shape, s: jax.random.normal(k, shape, jnp.float32) * s
    gain = lambda k, shape: 1.0 + 0.05 * jax.random.normal(k, shape, jnp.float32)
    L = DEPTH
    x = jax.random.normal(ks[0], (BATCH, SEQ, D_MODEL), jnp.float32)
    meta_tokens = nrm(ks[1], (N_META, D_MODEL), 1.0)
    g_mix_pre = gain(ks[2], (L, D_MODEL))
    w_in = nrm(ks[3], (L, D_MODEL, IN_WIDTH), D_MODEL ** -0.5)
    w_gate_up = nrm(ks[4], (L, GATE_RANK, GLA_KEY), GATE_RANK ** -0.5)
    b_gate = 1.0 + 0.5 * jax.random.normal(ks[5], (L, GLA_KEY), jnp.float32)
    gla_norm_g = gain(ks[6], (L, GLA_HEADS, GLA_DV))
    w_o_gla = nrm(ks[7], (L, GLA_VAL, D_MODEL), GLA_VAL ** -0.5)
    n_idx = jnp.arange(SSM_STATE, dtype=jnp.float32)
    a_re = -0.5 + 0.01 * jax.random.normal(ks[8], (L, SSM_GROUPS, SSM_STATE), jnp.float32)
    a_im = jnp.broadcast_to(jnp.pi * n_idx, (L, SSM_GROUPS, SSM_STATE)) + 0.0
    log_step = jax.random.uniform(ks[9], (L, SSM_GROUPS), jnp.float32,
                                  minval=float(np.log(1e-3)), maxval=float(np.log(1e-1)))
    b_re = nrm(ks[10], (L, SSM_GROUPS, SSM_STATE, SSM_GROUP), (2 * SSM_GROUP) ** -0.5)
    b_im = nrm(ks[11], (L, SSM_GROUPS, SSM_STATE, SSM_GROUP), (2 * SSM_GROUP) ** -0.5)
    c_re = nrm(ks[12], (L, SSM_GROUPS, SSM_GROUP, SSM_STATE), (2 * SSM_STATE) ** -0.5)
    c_im = nrm(ks[13], (L, SSM_GROUPS, SSM_GROUP, SSM_STATE), (2 * SSM_STATE) ** -0.5)
    d_skip = nrm(ks[14], (L, SSM_WIDTH), 1.0)
    w_glu = nrm(ks[15], (L, SSM_WIDTH, 2 * D_MODEL), SSM_WIDTH ** -0.5)
    b_glu = nrm(ks[16], (L, 2 * D_MODEL), 0.02)
    w_out = nrm(ks[17], (L, D_MODEL, D_MODEL), D_MODEL ** -0.5)
    g_mix_post = gain(ks[18], (L, D_MODEL))
    g_ffn_pre = gain(ks[19], (L, D_MODEL))
    w_ff1 = nrm(ks[20], (L, D_MODEL, D_FF), D_MODEL ** -0.5)
    w_ff2 = nrm(ks[21], (L, D_FF, D_MODEL), D_FF ** -0.5)
    g_ffn_post = gain(ks[22], (L, D_MODEL))
    return {"x": x, "meta_tokens": meta_tokens, "g_mix_pre": g_mix_pre, "w_in": w_in,
            "w_gate_up": w_gate_up, "b_gate": b_gate, "gla_norm_g": gla_norm_g, "w_o_gla": w_o_gla,
            "a_re": a_re, "a_im": a_im, "log_step": log_step, "b_re": b_re, "b_im": b_im,
            "c_re": c_re, "c_im": c_im, "d_skip": d_skip, "w_glu": w_glu, "b_glu": b_glu,
            "w_out": w_out, "g_mix_post": g_mix_post, "g_ffn_pre": g_ffn_pre, "w_ff1": w_ff1,
            "w_ff2": w_ff2, "g_ffn_post": g_ffn_post}

def second_block(x, meta_tokens, g_mix_pre, w_in, w_gate_up, b_gate, gla_norm_g, w_o_gla,
              a_re, a_im, log_step, b_re, b_im, c_re, c_im, d_skip, w_glu, b_glu,
              w_out, g_mix_post, g_ffn_pre, w_ff1, w_ff2, g_ffn_post):
    bsz, seq, dm = x.shape
    meta = jnp.broadcast_to(meta_tokens.astype(x.dtype)[None], (bsz, N_META, dm))
    h = jnp.concatenate([meta, x], axis=1)
    p = N_PAD + N_META + seq

    def pad(t):
        return jnp.pad(t, ((0, 0), (N_PAD, 0), (0, 0)))

    def heads(t, d):
        return t.reshape(bsz, p, GLA_HEADS, d)

    for l in range(DEPTH):
        xn = rmsnorm_2(h, g_mix_pre[l])
        proj = xn @ w_in[l]
        q = proj[..., :Q_END]
        k = proj[..., Q_END:K_END]
        v = proj[..., K_END:V_END]
        r = proj[..., V_END:R_END]
        a_low = proj[..., R_END:A_END]
        u = proj[..., A_END:U_END]
        z_gla = proj[..., U_END:G1_END]
        z_ssm = proj[..., G1_END:]

        log_a = jax.nn.log_sigmoid((a_low @ w_gate_up[l] + b_gate[l]).astype(jnp.float32)) / GATE_TAU
        o = gla_chunked(heads(pad(q), GLA_DK) * (GLA_DK ** -0.5), heads(pad(k), GLA_DK),
                        heads(pad(v), GLA_DV), heads(pad(log_a), GLA_DK))[:, N_PAD:]
        o = rmsnorm_2(o, gla_norm_g[l]).reshape(bsz, N_META + seq, GLA_VAL) * jax.nn.silu(r)
        y_gla = o @ w_o_gla[l]

        y_s = s5_ssm(pad(u), a_re[l], a_im[l], log_step[l], b_re[l], b_im[l],
                     c_re[l], c_im[l], d_skip[l])[:, N_PAD:]
        g_s = jax.nn.gelu(y_s)
        glu = g_s @ w_glu[l] + b_glu[l]
        y_ssm = glu[..., :D_MODEL] * jax.nn.sigmoid(glu[..., D_MODEL:])

        mixed = jax.nn.sigmoid(z_gla) * y_gla + jax.nn.sigmoid(z_ssm) * y_ssm
        h = h + rmsnorm_2(mixed @ w_out[l], g_mix_post[l])

        hn = rmsnorm_2(h, g_ffn_pre[l])
        f = jnp.square(jax.nn.relu(hn @ w_ff1[l])) @ w_ff2[l]
        h = h + rmsnorm_2(f, g_ffn_post[l])

    return h[:, N_META:]


def setup_inputs(seed=0):
    out = dict(first_inputs(seed))
    for name, value in second_inputs(seed + 1).items():
        if name != "x":
            out[name + "_2"] = value
    return out


def reference(
    x, c, w_ada, b_ada, norm_mix, norm_ffn, w_in, pool_w, pool_b, pool_scale, conv_w, conv_b,
    dt_bias, a_log, d_skip, ssd_norm, w_out, w_query, sub_keys1, sub_keys2, expert_down,
    expert_up, norm_final, meta_tokens_2, g_mix_pre_2, w_in_2, w_gate_up_2, b_gate_2,
    gla_norm_g_2, w_o_gla_2, a_re_2, a_im_2, log_step_2, b_re_2, b_im_2, c_re_2, c_im_2,
    d_skip_2, w_glu_2, b_glu_2, w_out_2, g_mix_post_2, g_ffn_pre_2, w_ff1_2, w_ff2_2,
    g_ffn_post_2,
):
    x = first_block(
        x, c, w_ada, b_ada, norm_mix, norm_ffn, w_in, pool_w, pool_b, pool_scale, conv_w,
        conv_b, dt_bias, a_log, d_skip, ssd_norm, w_out, w_query, sub_keys1, sub_keys2,
        expert_down, expert_up, norm_final,
    )
    return second_block(
        x, meta_tokens_2, g_mix_pre_2, w_in_2, w_gate_up_2, b_gate_2, gla_norm_g_2, w_o_gla_2,
        a_re_2, a_im_2, log_step_2, b_re_2, b_im_2, c_re_2, c_im_2, d_skip_2, w_glu_2, b_glu_2,
        w_out_2, g_mix_post_2, g_ffn_pre_2, w_ff1_2, w_ff2_2, g_ffn_post_2,
    )


_drawn_inputs = setup_inputs


def setup_inputs(seed=0):
    import zlib

    import numpy as np

    out = dict(_drawn_inputs(seed))
    spreads = {}
    factors = {'norm_mix': 4.142,
     'norm_ffn': 4.466,
     'pool_b': 7.705,
     'conv_b': 4.951,
     'ssd_norm': 5.695,
     'a_re_2': 8.0,
     'b_re_2': 3.555,
     'b_im_2': 3.54,
     'c_re_2': 3.595,
     'c_im_2': 3.537,
     'b_glu_2': 4.681}
    for name, (base, spread) in spreads.items():
        noise = np.random.default_rng([zlib.crc32(name.encode()), seed]).standard_normal(out[name].shape)
        drawn = base * np.exp(spread * noise) if base else spread * noise
        out[name] = __import__('jax').numpy.asarray(drawn.astype(out[name].dtype))
    for name, factor in factors.items():
        out[name] = (out[name] * factor).astype(out[name].dtype)
    return out
```

```python
import numpy as np
from contextlib import ExitStack, contextmanager

import concourse.bass as bass
from concourse import mybir

F32 = mybir.dt.float32
F32R = mybir.dt.float32r
U32 = mybir.dt.uint32
ALU = mybir.AluOpType
ACT = mybir.ActivationFunctionType
AX = mybir.AxisListType

P = 128
D, T = 1024, 512
KT = D // P
EPS = 1e-6

POOL_G = 4
HEADS, HD = 16, 64
CH = 128
NCH = T // CH
PH, TOPK, NKEY = 8, 16, 128
SLOTS = PH * TOPK

META = 16
T2 = T + META
GLH, DV = 4, 256
GC = 64
GCH = [(0, META)] + [(META + GC * c, GC) for c in range(T // GC)]
S5G, S5H, S5N = 64, 16, 64
SB = 8
NB = T2 // SB
GP = P // S5H

ER = 4
EROUNDS = NKEY // ER
SPLIT_ORDER = [("d", 0), ("d", 1), ("u", 0), ("u", 1), ("d", 2), ("u", 2), ("d", 3), ("u", 3)]

CONST = {}
_at = 0
for _n, _w in [("ident", P), ("causal", P), ("ones", P), ("swap", P), ("iota", P), ("iota16", 16), ("mask64", T2),
               ("mask128", T), ("invcnt", POOL_G * 16), ("cidx", NB), ("cmask", NB), ("kk", SB + 1), ("sgn", 1),
               ("nsgn", 1)]:
    CONST[_n] = (_at, _w)
    _at += _w
NCONST = _at

PAR = {}
_at = 0
for _n, _w in [("norm_mix", 8), ("norm_ffn", 8), ("norm_final", 8), ("ssd_norm", 8), ("b_ada", 48), ("pool_b", 4),
               ("pool_scale", 4), ("conv_w", 48), ("conv_b", 12), ("d_skip", 8), ("g_mix_pre", 8), ("g_mix_post", 8),
               ("g_ffn_pre", 8), ("g_ffn_post", 8), ("gla_norm", 8), ("b_gate", 4), ("d_skip_2", 8), ("b_glu", 16)]:
    PAR[_n] = (_at, _w)
    _at += _w
NPAR = _at

TWO_PI = 2.0 * np.pi
MAGIC = 12582912.0
C1 = 6.28125
C2 = float(np.float32(TWO_PI - 6.28125))
PI_IN = 3.1415925

STAGES = {
    "in": (24, 8, 1, T), "out": (8, 12, 1, T), "query": (16, 8, 1, T),
    "in2": (40, 8, 1, T2), "r2": (8, 8, 1, T2), "ogla": (8, 8, 1, T2), "glu": (16, 8, 1, T2),
    "out2": (8, 8, 1, T2), "ff1": (32, 8, 1, T2), "ff2": (8, 16, 2, T2),
}
NSLOT, SLOT = 4, 2048


SHARED = {
    "act_events": [("cact", 1), ("sq1", 1), ("rt1", 1), ("dt_raw", 1), ("conv_out", 12), ("dt_e", 1), ("eacs", 1),
                   ("cdec", 1), ("dte", 3), ("btok", 2), ("dec_e", 16), ("sq2", 1), ("rt2", 1), ("sq3", 1), ("rt3", 1),
                   ("e_g", 128), ("sq4", 1), ("rt4", 1), ("sq5", 1), ("rt5", 1), ("alow", 1), ("ln_e", 1), ("ge1", 1),
                   ("ge2", 1), ("ge3", 1), ("ge4", 1), ("sq6", 1), ("rt6", 4), ("s5_e", 8), ("gs", 8), ("sq7", 1),
                   ("rt7", 1), ("sq8", 1), ("rt8", 1), ("sq9", 1), ("rt9", 1)],
    "act_1": [("sc_set", 16), ("s5_cs", 16)],
    "act_2": [("gate_e", 4), ("s5_W", 16)],
    "act_3": [("slots_T", 8), ("s5_K", 16)],
    "act_4": [("vtok", 9), ("s5_S", 8)],
    "act_5": [("o_set", 9), ("s5_y", 8)],
    "pe_events": [("ss1", 1), ("dt_mm", 1), ("btok_mm", 2), ("cb_mm", 2), ("xs_mm", 8), ("st_mm", 6),
                  ("ss2", 1), ("pool_mm", 4), ("ss3", 1), ("ss4", 1), ("ss5", 1), ("alow_mm", 1), ("gate_mm", 4),
                  ("ss6", 4), ("ss7", 1), ("ss8", 1), ("ss9", 1)],
    "pe_1": [("row_mm", 16), ("sc_mm", 4), ("gla_tr", 9), ("s5_Wmm", 8)],
    "pe_2": [("diag_mm", 16), ("slots_mm", 4), ("gla_sc", 9), ("s5_Kmm", 8)],
    "pe_3": [("yoff_mm", 6), ("e_u", 128), ("gla_o", 9), ("s5_Smm", 8)],
    "pe_4": [("yt_mm", 8), ("e_y", 256), ("gla_st", 8), ("s5_Zmm", 16)],
    "pe_5": [("acol_mm", 1), ("s5_ymm", 8)],
    "dma_1": [("x_in", 16), ("T_in", 1024)],
    "dve_events": [("pads", 1), ("h_ready", 8), ("conv_acc", 12), ("pooled", 4), ("dt_x", 1), ("acs", 1), ("aend_x", 1),
                   ("acol_set", 1), ("xdt", 8), ("cbm", 2), ("hst", 6), ("ymix", 8), ("pool_out", 4), ("x1_ready", 1),
                   ("h2_ready", 8), ("hsplit", 1), ("xf_ready", 8), ("h2in", 8), ("xn_ready", 8), ("gate_lin", 4), ("gd", 1),
                   ("gq", 4), ("gla_done", 1), ("o_ready", 8), ("ogla_out", 1), ("s5_x", 2), ("s5_out", 8),
                   ("mixed", 1), ("h_mid", 8), ("hn_ready", 8), ("ff1_out", 1), ("h_end", 8), ("fin", 1)],
    "dve_1": [("dte_x", 3), ("seg", 16), ("sc_free", 4), ("ktok", 9), ("s5_WT", 8)],
    "dve_2": [("xdte", 3), ("mdec", 16), ("gate_x", 4), ("sm", 9), ("s5_ang", 8)],
    "dve_3": [("yoff", 6), ("sel", 4), ("st", 32), ("s5_V9", 8)],
    "dve_4": [("ytok", 8), ("b_hot", 128), ("s5_w", 8)],
    "dve_5": [("yt_ready", 8), ("e_w", 128), ("s5_H", 8)],
}
PLACE = {}
for _s, _names in SHARED.items():
    _at = 0
    for _n, _w in _names:
        assert _n not in PLACE
        PLACE[_n] = (_s, _at)
        _at += _w


class Sems:

    def __init__(self, nc, ctx):
        self.nc, self.ctx, self.made = nc, ctx, {}

    def __getitem__(self, name):
        name = PLACE.get(name, (name, 0))[0]
        if name not in self.made:
            self.made[name] = self.ctx.enter_context(self.nc.semaphore(name))
        return self.made[name]

    def base(self, name):
        return PLACE.get(name, (name, 0))[1]


FREE = "free"


class Turn:

    def __init__(self, eng, sems, own):
        self.eng, self.sems, self.own = eng, sems, own
        self.base, self.k, self.per, self.i = {}, {}, {}, None

    def do(self, ins, sem=None):
        if sem == FREE:
            return
        sem = sem or self.own
        ins.then_inc(self.sems[sem], 1)
        if self.i is None:
            self.base[sem] = self.base.get(sem, 0) + 1
            self.eng.wait_ge(self.sems[sem], self.sems.base(sem) + self.base[sem])
        else:
            self.k[sem] = self.k.get(sem, 0) + 1
            self.eng.wait_ge(self.sems[sem], self.i * self.per[sem] + (self.sems.base(sem) + self.base.get(sem, 0) + self.k[sem]))

    def wait(self, sem, value):
        self.eng.wait_ge(self.sems[sem], self.sems.base(sem) + value)

    @contextmanager
    def loop(self, n, **per):
        with self.eng.Fori(0, n) as i:
            self.i, self.per, self.k = i, per, {}
            yield i
            assert self.k == per, (self.k, per)
        self.i = None
        for sem, m in per.items():
            self.base[sem] = self.base.get(sem, 0) + m * n


def build(nc, io):
    ctx = ExitStack()
    with ctx:
        def sb(name, shape, dt=F32):
            return ctx.enter_context(nc.sbuf_tensor(name, shape, dt))

        S = Sems(nc, ctx)

        ARENA = 49408
        at = (nc.sbuf_base + 31) // 32 * 32
        A = nc.alloc_sbuf_tensor_at("arena", [P, ARENA], F32, offset=at)
        sb("fence", [P, ARENA + 8])
        PS = ctx.enter_context(nc.psum_tensor("psum", [P, 4096], F32))
        cst = sb("cst", [P, NCONST])
        par = sb("par", [P, NPAR])
        mod = sb("mod", [P, 48])
        gsc = sb("gsc", [P, 16])
        RS = sb("rs", [P, T2])
        w16 = sb("w16", [P, 256])
        small = sb("small", [P, 336])
        tick = sb("tick", [P, 8])

        RING = 0
        X = NSLOT * SLOT
        XW = KT * T2
        H = X + XW
        R0 = H + XW

        def reg(off, n, parts=P):
            return A[0:parts, off:off + n]

        parts_r = {}

        def as_r(off, n, size):
            for o in range(off, off + n, size):
                parts_r[o] = (size, nc.alloc_sbuf_tensor_at(f"arena_r{o}", [P, size], F32R, offset=at + 4 * o))

        def rr(off, n):
            o = max(o for o in parts_r if o <= off)
            assert off + n <= o + parts_r[o][0]
            return parts_r[o][1][:, off - o:off - o + n]

        def con(name, parts=P):
            a, w = CONST[name]
            return cst[0:parts, a:a + w]

        def pr(name, j=None):
            a, w = PAR[name]
            return par[:, a:a + w] if j is None else par[:, a + j:a + j + 1]

        def bank(b, w=512, parts=P):
            return PS[0:parts, b * 512:b * 512 + w]

        def pair(b, parts=P):
            return PS[0:parts, b * 1024:(b + 1) * 1024].rearrange("p (h x) -> p h x", h=2)[:, :, 0:T2 // 2]

        def halves(ap):
            return ap.rearrange("p (h x) -> p h x", h=2)

        def bc(ap, shape):
            return ap.broadcast_to(shape)

        ident = con("ident")
        ones = con("ones")
        causal = con("causal")

        XRAW = R0
        XRW = 4 + T
        CONV = XRAW + 12 * XRW
        Z = CONV + 12 * T
        YMIX = Z + 8 * T
        POOLU = YMIX + 12 * T
        PUW = 16 + T
        PTMP = POOLU + 4 * PUW
        SEL = PTMP + 2 * PUW
        XDTE = SEL + 2048
        CBM = XDTE + 3072
        assert CBM + 1024 <= ARENA
        XDT = XRAW
        MB_ = XRAW + 4096
        PWT = CBM + 1024
        assert PWT + 512 <= ARENA
        YTOK = POOLU
        HST = H
        BTOK = H + 3072
        ADA = POOLU
        CACT = YMIX
        DTB = YMIX + 4 * T
        QT = R0
        KEYS = QT + 16 * T
        SC = KEYS + 2048
        CAND = SC + 2048
        OH = CAND + 2048
        OH2 = OH + 2048
        PV = OH2 + 2048
        PUI = PV + 256
        PIF = PUI + 256
        TV = PIF + 256
        TU = TV + 128
        TF = TU + 3 * 128
        SELX = TF + 2 * 128
        GSTG = R0
        I1T, I2T, GT = X, X + T, X + 2 * T
        OA, OB = RING + 4096, RING + 5120
        YACC = R0
        GRING = YACC + 8 * T
        ACTB = GRING + ER * T
        WHI, WLO = ACTB + ER * T, ACTB + 2 * ER * T
        HHI = WLO + ER * T
        DHI, DLO = HHI + 8 * T, HHI + 8 * T + 2048
        UHI, ULO = DLO + 2048, DLO + 2048 + 4096
        assert ULO + 4096 <= ARENA
        for o_, n_, size_ in ((H, 8 * T, 2 * T), (WHI, 2 * ER * T, T), (HHI, 8 * T, 2 * T),
                              (DHI, 4096, 1024), (UHI, 8192, 1024)):
            as_r(o_, n_, size_)
        PROJ = R0
        PQ, PK, PVV, PU, PZG, PZS = (PROJ + T2 * n for n in (0, 4, 8, 16, 24, 32))
        TMP = PROJ + 40 * T2
        LA, DD, EE, QIN, KIN = (TMP + 4 * T2 * n for n in range(5))
        DEC = TMP + 20 * T2
        assert DEC + 36 <= ARENA
        KTOK, VTOK, ST, SM = DD, DD + 512, DD + 1536, LA
        RR = QIN
        UALL, YALL = PROJ, PROJ + 8 * T2
        Y8 = PROJ
        S5P = TMP
        WT, V9, WW, TT_, KALL = (S5P + 4096 + n for n in (0, 1152, 2304, 3328, 4352))
        COS, SIN, SS, S2 = (S5P + 4096 + 5376 + 528 * n for n in range(4))
        RSX = COS
        assert S2 + 528 <= ARENA
        XN = H
        ANG, ANG2 = XN, XN + 528
        S5A = XN + 1056
        DT5, AR5, TH5, PH5, MG1, MG8, SN1, CS1, FR, FI = (S5A + 192 + 64 * n for n in range(10))
        BBP = S5A + 192 + 640
        LR, LI, LMG = BBP + 128, BBP + 128 + 576, RSX
        T5 = LI + 576
        assert T5 + 576 <= XN + XW
        FF = R0
        MO = R0 + 32 * T2
        MO2 = R0

        acol = small[:, 0:64]
        dtcol = small[:, 64:128]
        aend = small[:, 128:192]
        cdec = small[:, 192:256]
        eacs = small[:, 256:320]
        dtecol = small[:, 320:336]

        def wslot(s, kt, mcols=P):
            return reg(RING + s * SLOT, kt * mcols).rearrange("p (k m) -> p k m", k=kt)

        units, tiles, arr = {}, {}, {}
        u = t = 0
        a = [0] * NSLOT
        for name, (nt, kt, parts, w) in STAGES.items():
            if name == "in2":
                pass
            units[name], tiles[name], arr[name] = u, t, list(a)
            u += nt * parts
            t += nt
            a = [x + nt * parts // NSLOT for x in a]
        UNITS = u

        def load_stage(sp, name):
            nt, kt, parts, w = STAGES[name]
            src = io["w_" + name]
            n = kt * P
            first = name == "in"
            if first:
                for s in range(NSLOT):
                    sp.dma_start(reg(RING + s * SLOT, n), src[s]).then_inc(S[f"w_in{s}"], 16)
            with sp.Fori(1 if first else 0, nt * parts // NSLOT) as i:
                for s in range(NSLOT):
                    sp.wait_ge(S["unit_done"], S.base("unit_done") + i * NSLOT + (units[name] + s - 3))
                    sp.dma_start(reg(RING + s * SLOT, n), src[bass.ds(i * NSLOT + s, 1)].rearrange("o p n -> (o p) n"))\
                      .then_inc(S[f"w_in{s}"], 16)

        def stage_products(pe, name, rhs):
            nt, kt, parts, w = STAGES[name]
            cols = [(0, w)] if w <= 512 else [(0, w // 2), (w // 2, w // 2)]
            with pe.Fori(0, nt // 4) as i:
                for j in range(4):
                    for p in range(parts):
                        v = j * parts + p
                        s = v % NSLOT
                        pe.wait_ge(S[f"w_in{s}"], S.base(f"w_in{s}") + i * (16 * parts) + 16 * (arr[name][s] + v // NSLOT + 1))
                        if p == 0:
                            pe.wait_ge(S["bank_free"], S.base("bank_free") + i * 4 + (tiles[name] + j + 1))
                        for k in range(kt):
                            for h, (c0, cw) in enumerate(cols):
                                last = nc.tensor.matmul(bank(2 * j + h, cw), wslot(s, kt)[:, k, :],
                                                        rhs(p * kt + k, c0, cw), start=(p == 0 and k == 0),
                                                        stop=(p == parts - 1 and k == kt - 1))
                        last.then_inc(S["unit_done"], 1)

        def evacuate(tn, name, first, n, op):
            parts = STAGES[name][2]
            with tn.loop(n // 4, bank_free=4) as i:
                for j in range(4):
                    tn.wait("unit_done", i * (4 * parts) + (units[name] + parts * (first + j + 1)))
                    op(j, i)

        def ev(tn, name, first):
            tn.base["bank_free"] = 4 + tiles[name] + first

        block = ctx.enter_context(nc.Block())

        @block.sync
        def _(sp):
            load_stage(sp, "in")
            load_stage(sp, "out")
            load_stage(sp, "query")

            def tile(src, i, r):
                return src[r] if i is None else src[bass.ds(i * ER + r, 1)].rearrange("o p n -> (o p) n")

            def load_down(i):
                for r in range(ER):
                    if i is not None:
                        sp.wait_ge(S["d_lo"], S.base("d_lo") + i * ER + (r - 3))
                    sp.dma_start(reg(RING + r * 1024, 1024), tile(io["down"], i, r)).then_inc(S[f"down_in{r}"], 16)

            def load_gates(i):
                for r in range(ER):
                    if i is not None:
                        sp.wait_ge(S["e_w"], S.base("e_w") + i * ER + (r - 3))
                    sp.dma_start(reg(GRING + r * T, T), tile(io["gates"], i, r)).then_inc(S[f"g_in{r}"], 16)

            def load_up(i):
                for r in range(ER):
                    if i is not None:
                        sp.wait_ge(S["u_lo"], S.base("u_lo") + i * ER + (r - 3))
                    sp.dma_start(reg(RING + 4096 + r * 1024, 1024), tile(io["up"], i, r)).then_inc(S[f"up_in{r}"], 16)

            sp.wait_ge(S["unit_done"], S.base("unit_done") + units["query"] + 16)
            load_down(None)
            for tb in range(4):
                sp.wait_ge(S["g_evac"], S.base("g_evac") + 2 + 32 * (tb + 1))
                sp.dma_start(io["gates"][:, :, tb * P:(tb + 1) * P].rearrange("j i t -> i j t"),
                             reg(GSTG + (tb % 2) * 16384, 16384).rearrange("p (j t) -> p j t", j=P))\
                  .then_inc(S[f"g_stored{tb % 2}"], 16)
            sp.wait_ge(S["g_stored0"], S.base("g_stored0") + 32)
            sp.wait_ge(S["g_stored1"], S.base("g_stored1") + 32)
            load_gates(None)
            load_up(None)
            with sp.Fori(1, EROUNDS) as i:
                load_down(i)
                load_gates(i)
                load_up(i)
            sp.wait_ge(S["e_y"], S.base("e_y") + EROUNDS * 8)
            for name in ("in2", "r2", "ogla", "glu", "out2", "ff1", "ff2"):
                load_stage(sp, name)

        @block.gpsimd
        def _(pool):
            def alone(sem, value):
                pool.wait_ge(S["small_in"], 48)
                pool.wait_ge(S[sem], S.base(sem) + value)

            pool.dma_start(cst[:, :], io["consts"]).then_inc(S["small_in"], 16)
            pool.dma_start(par[:, :], io["params"]).then_inc(S["small_in"], 16)
            pool.dma_start(reg(CACT, D), io["c"].broadcast_to([P, D])).then_inc(S["c_in"], 16)
            pool.dma_start(w16[:, :], io["w16"]).then_inc(S["small_in"], 16)
            pool.dma_start(reg(X, KT * T).rearrange("p (k t) -> p k t", k=KT), io["xT"].rearrange("(k p) t -> p k t", p=P))\
                .then_inc(S["x_in"], 16)
            for m in range(8):
                pool.dma_start(reg(ADA + m * 1024, 1024), io["w_ada"][m]).then_inc(S[f"ada_in{m}"], 16)
            with pool.Fori(1, 6) as i:
                for m in range(8):
                    alone("mod_done", i * 8 + (m - 7))
                    pool.dma_start(reg(ADA + m * 1024, 1024), io["w_ada"][bass.ds(i * 8 + m, 1)]
                                   .rearrange("o p n -> (o p) n")).then_inc(S[f"ada_in{m}"], 16)
            pool.wait_ge(S["mod_done"], S.base("mod_done") + 48)
            pool.dma_start(reg(SEL, 2048, 16), io["sel"]).then_inc(S["sel_in"], 16)
            pool.dma_start(small[0:16, 320:322], io["dtal"]).then_inc(S["sel_in"], 16)
            pool.dma_start(reg(PWT, 512).rearrange("p (g d) -> p g d", g=4), io["pool_w"].rearrange("g c d -> c g d"))\
                .then_inc(S["poolw_in"], 16)

            pool.wait_ge(S["h2_ready"], S.base("h2_ready") + 8)
            pool.dma_start(reg(KEYS, 2048), io["keys"]).then_inc(S["keys_in"], 16)
            pool.dma_start(io["spill"], reg(X, KT * T)).then_inc(S["spilled"], 16)
            with pool.Fori(0, 64) as i:
                for u_ in range(2):
                    pool.wait_ge(S["b_hot"], S.base("b_hot") + i * 2 + (u_ + 1))
                    b3 = reg(OB + u_ * 512, 512).rearrange("p (t i) -> p t i", t=4)
                    nc.gpsimd.tensor_tensor(b3, b3, bc(A[:, bass.ds(i * 8 + (GT + 4 * u_), 4)].unsqueeze(2), [P, 4, P]),
                                            ALU.mult).then_inc(S["b_gated"], 1)
            pool.wait_ge(S["g_mm"], S.base("g_mm") + 2 + 128)
            pool.wait_ge(S["spilled"], S.base("spilled") + 16)
            pool.dma_start(reg(X, KT * T), io["spill"]).then_inc(S["unspilled"], 16)

            def low(raw, hi, lo, ready, done, i, r):
                pool.wait_ge(S[ready], S.base(ready) + i * ER + (r + 1))
                nc.gpsimd.tensor_tensor(rr(lo, 1024), reg(raw, 1024), rr(hi, 1024).bitcast(F32), ALU.subtract)\
                    .then_inc(S[done], 1)
            with pool.Fori(0, EROUNDS) as i:
                for kind, r in SPLIT_ORDER:
                    if kind == "d":
                        low(RING + r * 1024, DHI + (r % 2) * 1024, DLO + (r % 2) * 1024, "d_hi", "d_lo", i, r)
                    else:
                        low(RING + 4096 + r * 1024, UHI + r * 1024, ULO + r * 1024, "u_hi", "u_lo", i, r)

            pool.wait_ge(S["xf_ready"], S.base("xf_ready") + 8)
            pool.dma_start(A[:, X:X + XW].rearrange("p (k t) -> p k t", k=KT)[:, :, 0:META],
                           io["metaT"].rearrange("(k p) t -> p k t", p=P)).then_inc(S["meta_in"], 16)
            pool.dma_start(reg(DEC + 40, 512, 16), io["w_gate_up"]).then_inc(S["gate_in"], 16)
            pool.wait_ge(S["gla_done"], S.base("gla_done") + 1)
            pool.dma_start(io["u_d"].rearrange("t p x -> p t x"),
                           reg(PU, 8 * T2).rearrange("p (t x) -> p t x", t=8)).then_inc(S["u_out"], 16)
            pool.wait_ge(S["u_out"], S.base("u_out") + 16)
            ud = io["u_d"].rearrange("t (m h) (s c) -> s h (t m) c", h=S5H, s=SB)
            for s in range(SB):
                q = SB - 1 - s
                pool.dma_start(A[q * S5H:(q + 1) * S5H, UALL:UALL + S5G * NB].rearrange("p (g c) -> p g c", g=S5G),
                               ud[s]).then_inc(S["uall_in"], 16)
            pool.wait_ge(S["ogla_out"], S.base("ogla_out") + 1)
            pool.dma_start(reg(S5P, 4096), io["s5bc"]).then_inc(S["s5p_in"], 16)
            pool.dma_start(reg(S5A, 192), io["s5a"]).then_inc(S["s5p_in"], 16)
            for i in range(8):
                pool.wait_ge(S["s5_K"], S.base("s5_K") + i * 2 + 2)
                for s in range(SB):
                    q = SB - 1 - s
                    pool.dma_start(
                        A[q * S5H:(q + 1) * S5H, TT_:TT_ + 1024].rearrange("p (g m) -> p g m", g=GP)[:, :, s * S5H:P],
                        A[0:S5H, KALL:KALL + 1024].rearrange("p (g m) -> p g m", g=GP)[:, :, 0:P - s * S5H])\
                        .then_inc(S["T_in"], 16)
            pool.wait_ge(S["s5_y"], S.base("s5_y") + 8)
            yd = io["y_d"].rearrange("t (m h) (s c) -> s h (t m) c", h=S5H, s=SB)
            for s in range(SB):
                pool.dma_start(yd[s], A[s * S5H:(s + 1) * S5H, YALL:YALL + S5G * NB]
                               .rearrange("p (g c) -> p g c", g=S5G)).then_inc(S["y_out"], 16)
            pool.wait_ge(S["y_out"], S.base("y_out") + 16 * SB)
            pool.dma_start(reg(Y8, 8 * T2).rearrange("p (t x) -> p t x", t=8),
                           io["y_d"].rearrange("t p x -> p t x")).then_inc(S["y8_in"], 16)
            pool.wait_ge(S["fin"], S.base("fin") + 1)
            pool.dma_start(io["out"].rearrange("(k p) t -> p k t", p=P),
                           A[:, X:X + XW].rearrange("p (k t) -> p k t", k=KT)[:, :, META:T2]).then_inc(S["stored"], 16)
            pool.wait_ge(S["stored"], S.base("stored") + 16)

        @block.scalar
        def _(act):
            tn = Turn(act, S, "act_own")
            do, wait = tn.do, tn.wait
            sc = nc.scalar

            def act_(out, in_, f, sem=None, **kw):
                do(sc.activation(out, in_, f, **kw), sem)

            def norm_root(out, src_bank, sem, scale=1.0 / D):
                act_(out, src_bank, ACT.Sqrt, sem, scale=scale, bias=EPS)

            wait("small_in", 48)
            wait("c_in", 16)
            act_(reg(CACT, D), reg(CACT, D), ACT.Silu, "cact")
            wait("x_in", 16)
            act_(reg(H, KT * T), reg(X, KT * T), ACT.Square, "sq1")
            wait("ss1", 1)
            norm_root(RS[:, 0:T], bank(7), "rt1")

            wait("h_ready", 8)
            wait("pads", 1)
            wait("dt_mm", 1)
            act_(A[0:16, DTB:DTB + T], bank(7, 512, 16), ACT.Copy, "dt_raw")
            ev(tn, "in", 0)
            evacuate(tn, "in", 0, 12, lambda j, i: act_(
                A[:, bass.ds(i * (4 * XRW) + (XRAW + j * XRW + 4), T)], bank(2 * j), ACT.Copy, "bank_free"))
            evacuate(tn, "in", 12, 8, lambda j, i: act_(
                A[:, bass.ds(i * (4 * T) + (Z + j * T), T)], bank(2 * j), ACT.Silu, "bank_free"))
            for m in range(12):
                wait("conv_acc", m + 1)
                act_(reg(CONV + m * T, T), reg(CONV + m * T, T), ACT.Silu, "conv_out", bias=pr("conv_b", m))
            wait("mod_done", 48)
            evacuate(tn, "in", 20, 4, lambda j, i: act_(
                A[:, bass.ds(i * 0 + (POOLU + j * PUW + 16), T)], bank(2 * j), ACT.Copy, "bank_free"))

            wait("dt_x", 1)
            act_(A[0:16, DTB + T:DTB + 2 * T], A[0:16, DTB:DTB + T], ACT.Abs)
            act_(A[0:16, DTB + T:DTB + 2 * T], A[0:16, DTB + T:DTB + 2 * T], ACT.Exp, scale=-1.0)
            act_(small[0:16, 323:324], small[0:16, 321:322], ACT.Exp, "dt_e")

            wait("acol_set", 1)
            act_(eacs, acol, ACT.Exp, "eacs")
            act_(cdec, aend, ACT.Exp, "cdec")
            for c in range(3):
                wait("dte_x", c + 1)
                act_(dtecol, dtecol, ACT.Exp, "dte")
            wait("btok_mm", 2)
            act_(reg(BTOK, 512), bank(4), ACT.Copy, "btok")
            act_(reg(BTOK + 512, 512), bank(5), ACT.Copy, "btok")
            for h in range(HEADS):
                wait("seg", h + 1)
                m = reg(MB_ + (h % 2) * T, T)
                act_(m, m, ACT.Relu, scale=-1.0)
                act_(m, m, ACT.Exp, "dec_e", scale=-1.0)
            wait("yt_ready", 8)
            act_(reg(XRAW, 8 * T), reg(YMIX + 4 * T, 8 * T), ACT.Square, "sq2")
            wait("ss2", 1)
            norm_root(RS[:, 0:T], bank(7), "rt2")

            wait("x1_ready", 1)
            act_(reg(H, KT * T), reg(X, KT * T), ACT.Square, "sq3")
            wait("ss3", 1)
            norm_root(RS[:, 0:T], bank(7), "rt3")
            ev(tn, "query", 0)
            evacuate(tn, "query", 0, 16, lambda j, i: act_(
                A[:, bass.ds(i * (4 * T) + (QT + j * T), T)], bank(2 * j), ACT.Copy, "bank_free"))

            with tn.loop(4, act_own=1, sc_set=4, gate_e=1, slots_T=2) as i:
                wait("sc_mm", i + 1)
                wait("sc_free", i)
                for b in range(4):
                    act_(reg(SC + b * 512, 512), bank(b), ACT.Copy, "sc_set")
                wait("gate_x", i + 1)
                act_(reg(SELX + 256, 128), reg(SELX + 256, 128), ACT.Exp, "gate_e")
                wait("slots_mm", i + 1)
                wait("spilled", 16)
                act_(A[:, bass.ds(i * P + I1T, P)], bank(4)[:, 0:P], ACT.Copy)
                act_(A[:, bass.ds(i * P + I2T, P)], bank(4)[:, P:2 * P], ACT.Copy, "slots_T")
                act_(A[:, bass.ds(i * P + GT, P)], bank(4)[:, 2 * P:3 * P], ACT.Copy, "slots_T")

            tn.base["g_evac"] = 2
            for tb in range(4):
                if tb >= 2:
                    wait(f"g_stored{tb % 2}", 16)
                with tn.loop(16, g_evac=2) as i:
                    for u_ in range(2):
                        wait("g_mm", i * 2 + (2 + tb * 32 + u_ + 1))
                        stg = reg(GSTG + (tb % 2) * 16384, 16384).rearrange("p (j t) -> p t j", j=P)
                        act_(stg[:, bass.ds(i * 8 + 4 * u_, 4), :],
                             bank(u_).rearrange("p (t j) -> p t j", t=4), ACT.Copy, "g_evac")

            wait("g_stored0", 32)
            wait("g_stored1", 32)
            with tn.loop(EROUNDS, e_g=ER, d_hi=ER, u_hi=ER) as i:
                def gelu(r):
                    wait("e_u", i * ER + (r + 1))
                    wait("e_w", i * ER)
                    act_(reg(ACTB + r * T, T), bank(r), ACT.Gelu, "e_g")
                n = 0
                for kind, r in SPLIT_ORDER:
                    if kind == "d":
                        wait(f"down_in{r}", i * 16 + 16)
                        wait("e_u", i * ER + (r - 1))
                        act_(rr(DHI + (r % 2) * 1024, 1024), reg(RING + r * 1024, 1024), ACT.Copy, "d_hi")
                    else:
                        wait(f"up_in{r}", i * 16 + 16)
                        wait("e_y", i * 8)
                        act_(rr(UHI + r * 1024, 1024), reg(RING + 4096 + r * 1024, 1024), ACT.Copy, "u_hi")
                        if r:
                            gelu(r - 1)
                gelu(3)

            wait("xf_ready", 8)
            act_(reg(H, KT * T), reg(YACC, KT * T), ACT.Square, "sq4")
            wait("ss4", 1)
            norm_root(RS[:, 0:T], bank(7), "rt4")

            wait("h2in", 8)
            wait("meta_in", 16)
            act_(reg(XN, XW), reg(X, XW), ACT.Square, "sq5")
            wait("ss5", 1)
            norm_root(halves(RS[:, 0:T2]), pair(3), "rt5")
            wait("alow_mm", 1)
            act_(halves(A[0:16, EE:EE + T2]), pair(3, 16), ACT.Copy, "alow")
            E4, L4 = reg(EE, 4 * T2), reg(LA, 4 * T2)
            wait("gate_lin", 4)
            act_(E4, L4, ACT.Abs)
            act_(E4, E4, ACT.Exp, scale=-1.0)
            act_(E4, E4, ACT.Ln, "ln_e", bias=1.0)
            ev(tn, "in2", 0)
            evacuate(tn, "in2", 0, 16, lambda j, i: act_(
                halves(A[:, bass.ds(i * (4 * T2) + (PROJ + j * T2), T2)]), pair(j), ACT.Copy, "bank_free"))
            wait("gd", 1)
            act_(E4, L4, ACT.Exp, "ge1")
            wait("gq", 1)
            act_(E4, L4, ACT.Exp, "ge2", scale=-1.0)
            wait("gq", 2)
            act_(E4, reg(DD, 4 * T2), ACT.Exp, "ge3")
            wait("gq", 3)
            act_(E4, L4, ACT.Exp)
            act_(reg(DEC, 36), reg(DEC, 36), ACT.Exp, "ge4")

            def ev_u(j, i):
                dst = A[:, bass.ds(i * (4 * T2) + (PU + j * T2), T2)].rearrange("p (s c) -> p c s", s=SB)
                for h in range(2):
                    src = bank(2 * j + h, T2 // 2).rearrange("p (c s) -> p c s", s=SB)
                    act_(dst[:, h * NB // 2:(h + 1) * NB // 2, :], src, ACT.Copy, "bank_free" if h else None)
            with tn.loop(2, bank_free=4, act_own=4) as i:
                for j in range(4):
                    wait("unit_done", i * 4 + (units["in2"] + 16 + j + 1))
                    ev_u(j, i)
            evacuate(tn, "in2", 24, 16, lambda j, i: act_(
                halves(A[:, bass.ds(i * (4 * T2) + (PZG + j * T2), T2)]), pair(j), ACT.Sigmoid, "bank_free"))

            for c, (t0, L) in enumerate(GCH):
                wait("gla_tr", c + 1)
                act_(reg(VTOK, 1024, L), PS[0:L, 512:1536], ACT.Copy, "vtok")
                wait("gla_o", c + 1)
                o = A[:, PVV:PVV + 8 * T2].rearrange("p (m t) -> p m t", m=8)[:, :, t0:t0 + L]
                act_(o, bank(4).rearrange("p (m t) -> p m t", m=8)[:, :, 0:L], ACT.Copy, "o_set")
            act_(reg(QIN, 8 * T2), reg(PVV, 8 * T2), ACT.Square, "sq6")
            wait("ss6", 4)
            for h in range(GLH):
                norm_root(halves(reg(LA + h * T2, T2)), pair(h), "rt6", scale=1.0 / DV)
            ev(tn, "r2", 0)
            evacuate(tn, "r2", 0, 8, lambda j, i: act_(
                halves(A[:, bass.ds(i * (4 * T2) + (RR + j * T2), T2)]), pair(j), ACT.Silu, "bank_free"))

            wait("s5p_in", 32)
            act_(reg(DT5, 64), reg(S5A + 128, 64), ACT.Exp, "s5_e")
            wait("s5_x", 1)
            act_(reg(MG1, 64), reg(AR5, 64), ACT.Exp, "s5_e")
            act_(reg(MG8, 64), reg(AR5, 64), ACT.Exp, "s5_e", scale=float(SB))
            act_(reg(SN1, 64), reg(SN1, 64), ACT.Sin, "s5_e")
            act_(reg(CS1, 64), reg(CS1, 64), ACT.Sin, "s5_e")
            wait("s5_x", 2)
            act_(reg(LMG, 576), reg(LMG, 576), ACT.Exp, "s5_e")
            act_(reg(LR, 576), reg(LR, 576), ACT.Sin, "s5_e")
            act_(reg(LI, 576), reg(LI, 576), ACT.Sin, "s5_e")
            with tn.loop(8, s5_cs=2, s5_W=2, s5_K=2, s5_S=1, s5_y=1) as i:
                wait("s5_ang", i + 1)
                act_(reg(SIN, 528), reg(ANG, 528), ACT.Sin, "s5_cs")
                act_(reg(COS, 528), reg(ANG2, 528), ACT.Sin, "s5_cs")
                wait("s5_Wmm", i + 1)
                act_(reg(WW, 512), bank(0), ACT.Copy, "s5_W")
                act_(reg(WW + 512, 512), bank(1), ACT.Copy, "s5_W")
                wait("s5_Kmm", i + 1)
                wait("T_in", i * (16 * SB))
                act_(reg(KALL, 512, 16), bank(2, 512, 16), ACT.Copy, "s5_K")
                act_(reg(KALL + 512, 512, 16), bank(3, 512, 16), ACT.Copy, "s5_K")
                wait("s5_Smm", i + 1)
                act_(halves(reg(SS, 528)), pair(2), ACT.Copy, "s5_S")
                wait("s5_ymm", i + 1)
                act_(halves(A[:, bass.ds(i * 528 + YALL, 528)]), pair(2), ACT.Copy, "s5_y")
            for m in range(8):
                wait("s5_out", m + 1)
                act_(reg(PU + m * T2, T2).rearrange("p (c s) -> p s c", s=SB),
                     reg(Y8 + m * T2, T2).rearrange("p (s c) -> p s c", s=SB), ACT.Gelu_apprx_tanh, "gs")
            ev(tn, "glu", 0)
            wait("gs", 8)
            evacuate(tn, "glu", 0, 8, lambda j, i: act_(
                halves(A[:, bass.ds(i * (4 * T2) + (YALL + j * T2), T2)]), pair(j), ACT.Identity, "bank_free",
                bias=par[:, bass.ds(i * 4 + (PAR["b_glu"][0] + j), 1)]))
            evacuate(tn, "glu", 8, 8, lambda j, i: act_(
                halves(A[:, bass.ds(i * (4 * T2) + (Y8 + j * T2), T2)]), pair(j), ACT.Sigmoid, "bank_free",
                bias=par[:, bass.ds(i * 4 + (PAR["b_glu"][0] + 8 + j), 1)]))
            ev(tn, "out2", 0)
            evacuate(tn, "out2", 0, 8, lambda j, i: act_(
                halves(A[:, bass.ds(i * (4 * T2) + (MO + j * T2), T2)]), pair(j), ACT.Copy, "bank_free"))
            act_(reg(XN, XW), reg(MO, XW), ACT.Square, "sq7")
            wait("ss7", 1)
            norm_root(halves(RS[:, 0:T2]), pair(3), "rt7")
            wait("h_mid", 8)
            act_(reg(XN, XW), reg(X, XW), ACT.Square, "sq8")
            wait("ss8", 1)
            norm_root(halves(RS[:, 0:T2]), pair(3), "rt8")
            ev(tn, "ff1", 0)
            evacuate(tn, "ff1", 0, 32, lambda j, i: act_(
                halves(A[:, bass.ds(i * (4 * T2) + (FF + j * T2), T2)]), pair(j), ACT.Relu, "bank_free"))
            ev(tn, "ff2", 0)
            evacuate(tn, "ff2", 0, 8, lambda j, i: act_(
                halves(A[:, bass.ds(i * (4 * T2) + (MO + j * T2), T2)]), pair(j), ACT.Copy, "bank_free"))
            act_(reg(XN, XW), reg(MO, XW), ACT.Square, "sq9")
            wait("ss9", 1)
            norm_root(halves(RS[:, 0:T2]), pair(3), "rt9")

        @block.tensor
        def _(pe):
            mm = nc.tensor.matmul

            def w_(sem, v):
                pe.wait_ge(S[sem], S.base(sem) + v)

            def tok(off, w=T):
                return lambda k, c0, cw: A[:, off + k * w + c0:off + k * w + c0 + cw]

            def sumsq(src, n, w, out, sem, start=True):
                cols = [(0, w)] if w <= 512 else [(0, w // 2), (w // 2, w // 2)]
                for h, (c0, cw) in enumerate(cols):
                    for k in range(n):
                        last = mm(bank(out + h, cw), ones, reg(src + k * w + c0, cw), start=(k == 0), stop=(k == n - 1))
                last.then_inc(S[sem], 1)

            def drained(name):
                w_("bank_free", 4 + tiles[name] + STAGES[name][0])

            def T_(out, in_, n):
                return nc.tensor.transpose(out, in_, cst[0:n, 0:n])

            w_("small_in", 48)

            def ssd_diag(h):
                w_("mdec", h + 1)
                w_("xdt", 8)
                for c in range(NCH):
                    last = mm(bank(2 + c)[:, (h % 8) * HD:(h % 8 + 1) * HD], reg(MB_ + (h % 2) * T + c * CH, CH),
                              reg(XDT + c * 1024 + h * HD, HD), start=True, stop=True)
                last.then_inc(S["diag_mm"], 1)

            w_("sq1", 1)
            sumsq(H, 8, T, 7, "ss1")
            w_("h_ready", 8)
            for k in range(KT):
                last = mm(bank(7, 512, 16), w16[:, k * 16:(k + 1) * 16], reg(H + k * T, T), start=(k == 0), stop=(k == 7))
            last.then_inc(S["dt_mm"], 1)
            stage_products(pe, "in", tok(H))
            drained("in")

            w_("acs", 1)
            for c in range(NCH):
                T_(bank(6)[:, c * 16:(c + 1) * 16], RS[0:16, c * CH:(c + 1) * CH], 16)
                T_(bank(6)[:, 64 + c * 16:80 + c * 16], A[0:16, DTB + 2 * T + c * CH:DTB + 2 * T + (c + 1) * CH], 16)
            w_("aend_x", 1)
            mm(bank(6)[:, 128:192], cst[0:16, CONST["ones"][0]:CONST["ones"][0] + P], small[0:16, 0:64], start=True,
               stop=True).then_inc(S["acol_mm"], 1)
            w_("conv_out", 12)
            for g in range(2):
                for c in range(NCH):
                    last = T_(bank(4 + g)[:, c * P:(c + 1) * P], reg(CONV + (8 + g) * T + c * CH, CH), P)
                last.then_inc(S["btok_mm"], 1)
            for g in range(2):
                for c in range(NCH):
                    last = mm(bank(2 + g)[:, c * P:(c + 1) * P], reg(CONV + (8 + g) * T + c * CH, CH),
                              reg(CONV + (10 + g) * T + c * CH, CH), start=True, stop=True)
                last.then_inc(S["cb_mm"], 1)
            for c in range(NCH):
                w_("xdt", 2 * c)
                for m in range(8):
                    last = T_(bank(m // 4)[:, (m % 4) * P:(m % 4 + 1) * P], reg(CONV + m * T + c * CH, CH), P)
                    if m % 4 == 3:
                        last.then_inc(S["xs_mm"], 1)
            w_("btok", 2)
            for c in range(3):
                w_("xdte", c + 1)
                w_("hst", 2 * c)
                for g in range(2):
                    mm(bank(4 + g), reg(BTOK + g * 512 + c * P, P), reg(XDTE + c * 1024 + g * 512, 512), start=True,
                       stop=True).then_inc(S["st_mm"], 1)
            w_("hst", 6)
            w_("cbm", 2)
            w_("sel_in", 32)
            for g in range(2):
                w_("yt_ready", 4 * g)
                for h in range(8 * g, 8 * g + 8):
                    if h >= 2:
                        w_("seg", h - 1)
                    mm(bank(h % 2), A[0:16, SEL + h * P:SEL + (h + 1) * P], RS[0:16, 0:T], start=True,
                       stop=True).then_inc(S["row_mm"], 1)
                    if h % 8:
                        ssd_diag(h - 1)
                ssd_diag(8 * g + 7)
                for c in range(1, NCH):
                    w_("yoff", g * 3 + c - 1)
                    mm(bank(6), reg(CONV + (10 + g) * T + c * CH, CH), reg(HST + (c - 1) * 1024 + g * 512, 512),
                       start=True, stop=True).then_inc(S["yoff_mm"], 1)
                for m in range(4):
                    w_("ytok", 4 * (g + 1))
                    if m >= 2:
                        w_("yt_ready", 4 * g + m - 1)
                    for c in range(NCH):
                        last = T_(bank(m % 2)[:, c * P:(c + 1) * P], reg(YTOK + c * 512 + m * P, P), P)
                    last.then_inc(S["yt_mm"], 1)
            w_("sq2", 1)
            sumsq(XRAW, 8, T, 7, "ss2")
            w_("poolw_in", 16)
            w_("pooled", 4)
            w_("yt_ready", 8)
            for g in range(POOL_G):
                if g >= 2:
                    w_("pool_out", g - 1)
                mm(bank(2 * (g % 2)), reg(PWT + g * P, P), reg(YMIX + g * T, T), start=True, stop=True)                    .then_inc(S["pool_mm"], 1)
            w_("pool_out", 4)
            w_("ymix", 8)
            stage_products(pe, "out", tok(YMIX))
            w_("sq3", 1)
            sumsq(H, 8, T, 7, "ss3")
            w_("h2_ready", 8)
            stage_products(pe, "query", tok(H))
            drained("query")

            w_("keys_in", 16)

            def scores(tb):
                w_("sc_set", 4 * tb)
                for hh in range(16):
                    last = mm(bank(hh // 4)[:, (hh % 4) * P:(hh % 4 + 1) * P], reg(QT + hh * T + tb * P, P),
                              reg(KEYS + hh * P, P), start=True, stop=True)
                last.then_inc(S["sc_mm"], 1)

            scores(0)
            for tb in range(4):
                if tb < 3:
                    scores(tb + 1)
                w_("sel", tb + 1)
                w_("slots_T", 2 * tb)
                for n in range(3):
                    last = T_(bank(4)[:, n * P:(n + 1) * P], reg(SELX + n * P, P), P)
                last.then_inc(S["slots_mm"], 1)
            w_("slots_T", 8)
            with pe.Fori(0, 64) as i:
                for u_ in range(2):
                    pe.wait_ge(S["b_gated"], S.base("b_gated") + i * 2 + (u_ + 1))
                    pe.wait_ge(S["g_evac"], S.base("g_evac") + i * 2 + (u_ + 1))
                    for t in range(4):
                        last = mm(bank(u_)[:, t * P:(t + 1) * P], reg(OA + u_ * 512 + t * P, P),
                                  reg(OB + u_ * 512 + t * P, P), start=True, stop=True)
                    last.then_inc(S["g_mm"], 1)
            w_("g_evac", 130)

            w_("hsplit", 1)
            with pe.Fori(0, EROUNDS) as i:
                for r in range(ER):
                    w_("d_lo", i * ER + (r + 1))
                    w_("e_w", i * ER)
                    hi, lo = DHI + (r % 2) * 1024, DLO + (r % 2) * 1024
                    for k in range(KT):
                        for n, (a_, b_) in enumerate(((hi, HHI), (hi, H), (lo, HHI))):
                            last = mm(bank(r), rr(a_ + k * P, P), rr(b_ + k * T, T), start=(k == 0 and n == 0),
                                      stop=(k == 7 and n == 2))
                    last.then_inc(S["e_u"], 1)
                for d in range(KT):
                    w_("e_acc", i * 8 + (d + 1))
                    for r in range(ER):
                        if d == 0:
                            w_("u_lo", i * ER + (r + 1))
                            w_("e_w", i * ER + (r + 1))
                        for n, (a_, b_) in enumerate(((UHI, WHI), (UHI, WLO), (ULO, WHI))):
                            last = mm(bank(4 + d % 4), rr(a_ + r * 1024 + d * P, P), rr(b_ + r * T, T),
                                      start=(r == 0 and n == 0), stop=(r == ER - 1 and n == 2))
                    last.then_inc(S["e_y"], 1)

            w_("sq4", 1)
            w_("e_acc", 4 + 8 * EROUNDS)
            sumsq(H, 8, T, 7, "ss4")

            w_("sq5", 1)
            sumsq(XN, 8, T2, 6, "ss5")
            w_("xn_ready", 8)
            for h in range(2):
                for k in range(KT):
                    last = mm(bank(6 + h, 264, 16), w16[:, 128 + k * 16:144 + k * 16],
                              reg(XN + k * T2 + h * 264, 264), start=(k == 0), stop=(k == 7))
            last.then_inc(S["alow_mm"], 1)
            w_("alow", 1)
            w_("gate_in", 16)
            for m in range(GLH):
                for h in range(2):
                    last = mm(bank(2 * m + h, 264), A[0:16, DEC + 40 + m * P:DEC + 40 + (m + 1) * P],
                              A[0:16, EE + h * 264:EE + (h + 1) * 264], start=True, stop=True)
                last.then_inc(S["gate_mm"], 1)
            w_("gate_lin", 4)
            stage_products(pe, "in2", tok(XN, T2))
            drained("in2")

            w_("gq", 4)
            for c, (t0, L) in enumerate(GCH):
                w_("ktok", c)
                w_("vtok", c)
                for h in range(GLH):
                    T_(PS[0:L, h * P:(h + 1) * P], reg(PK + h * T2 + t0, L), P)
                for m in range(8):
                    last = T_(PS[0:L, 512 + m * P:512 + (m + 1) * P], reg(PVV + m * T2 + t0, L), P)
                last.then_inc(S["gla_tr"], 1)
                for h in range(GLH):
                    last = mm(PS[0:L, 1536 + h * GC:1536 + h * GC + L], reg(KIN + h * T2 + t0, L),
                              reg(QIN + h * T2 + t0, L), start=True, stop=True)
                last.then_inc(S["gla_sc"], 1)
                w_("sm", c + 1)
                w_("vtok", c + 1)
                w_("ktok", c + 1)
                w_("o_set", c)
                w_("st", 4 * c)
                for m in range(8):
                    h = m // 2
                    o = bank(4)[:, m * GC:m * GC + L]
                    last = mm(o, reg(VTOK + m * P, P, L), reg(SM + h * GC, L, L), start=True, stop=(c == 0))
                    if c:
                        last = mm(o, reg(ST + m * P, P), reg(PQ + h * T2 + t0, L), start=False, stop=True)
                last.then_inc(S["gla_o"], 1)
                if c < len(GCH) - 1:
                    for h in range(GLH):
                        last = mm(PS[:, 3072 + h * DV:3072 + (h + 1) * DV], reg(KTOK + h * P, P, L),
                                  reg(VTOK + h * DV, DV, L), start=True, stop=True)
                    last.then_inc(S["gla_st"], 1)
            w_("sq6", 1)
            w_("st", 32)
            for h in range(GLH):
                sumsq(QIN + 2 * h * T2, 2, T2, 2 * h, "ss6")
            w_("rt6", 4)
            stage_products(pe, "r2", tok(XN, T2))
            w_("o_ready", 8)
            stage_products(pe, "ogla", tok(PVV, T2))
            drained("ogla")

            swap = con("swap")
            with pe.Fori(0, 8) as i:
                pe.wait_ge(S["s5_WT"], S.base("s5_WT") + i + 1)
                for g in range(GP):
                    last = T_(bank(g // 4)[:, (g % 4) * P:(g % 4 + 1) * P], reg(WT + g * P, P), P)
                last.then_inc(S["s5_Wmm"], 1)
                pe.wait_ge(S["s5_V9"], S.base("s5_V9") + i + 1)
                for g in range(GP):
                    last = mm(bank(2 + g // 4, 512, 16)[:, (g % 4) * P:(g % 4 + 1) * P], reg(BBP + g * 16, 16),
                              reg(V9 + g * 144, P), start=True, stop=True)
                last.then_inc(S["s5_Kmm"], 1)
                pe.wait_ge(S["s5_W"], S.base("s5_W") + i * 2 + 2)
                pe.wait_ge(S["s5_y"], S.base("s5_y") + i)
                for g in range(GP):
                    last = mm(bank(4 + g // 4)[:, (g % 4) * NB:(g % 4 + 1) * NB], reg(WW + g * P, P),
                              A[:, bass.ds(i * 528 + (UALL + g * NB), NB)], start=True, stop=True)
                last.then_inc(S["s5_Smm"], 1)
                for n, (sem, src) in enumerate((("s5_S", SS), ("s5_w", S2))):
                    pe.wait_ge(S[sem], S.base(sem) + i + 1)
                    for h in range(2):
                        last = mm(bank(6 + h, 264), swap, reg(src + h * 264, 264), start=True, stop=True)
                    last.then_inc(S["s5_Zmm"], 1)
                pe.wait_ge(S["s5_H"], S.base("s5_H") + i + 1)
                pe.wait_ge(S["T_in"], S.base("T_in") + i * (16 * SB) + 16 * SB)
                for g in range(GP):
                    o = bank(4 + g // 4)[:, (g % 4) * NB:(g % 4 + 1) * NB]
                    mm(o, reg(TT_ + g * P, P), A[:, bass.ds(i * 528 + (UALL + g * NB), NB)], start=True, stop=False)
                    last = mm(o[:, 1:NB], reg(V9 + g * 144 + 16, P), reg(SS + g * NB, NB - 1), start=False, stop=True)
                last.then_inc(S["s5_ymm"], 1)
            w_("s5_y", 8)
            w_("gs", 8)
            stage_products(pe, "glu", tok(PU, T2))
            w_("mixed", 1)
            stage_products(pe, "out2", tok(PZG, T2))
            drained("out2")
            w_("sq7", 1)
            sumsq(XN, 8, T2, 6, "ss7")
            w_("sq8", 1)
            sumsq(XN, 8, T2, 6, "ss8")
            w_("hn_ready", 8)
            stage_products(pe, "ff1", tok(XN, T2))
            w_("ff1_out", 1)
            stage_products(pe, "ff2", tok(FF, T2))
            drained("ff2")
            w_("sq9", 1)
            sumsq(XN, 8, T2, 6, "ss9")

        @block.vector
        def _(dve):
            tn = Turn(dve, S, "dve_own")
            do, wait = tn.do, tn.wait
            v = nc.vector

            def tt(out, a, b, op, sem=None):
                do(v.tensor_tensor(out, a, b, op), sem)

            def ts(out, a, s1, s2, op0, op1=None, sem=None):
                do(v.tensor_scalar(out, a, s1, s2, op0, op1) if op1 is not None else
                   v.tensor_scalar(out, a, s1, s2, op0), sem)

            def stt(out, a, s, b, op0, op1, sem=None):
                do(v.scalar_tensor_tensor(out, a, s, b, op0, op1), sem)

            def three(off, a, b=None):
                return reg(off, a * b).rearrange("p (a b) -> p a b", a=a)

            v.memset(tick[:, 0:1], 0.0).then_inc(S["bank_free"], 4)
            v.memset(tick[:, 1:2], 0.0).then_inc(S["g_mm"], 2)
            v.memset(tick[:, 2:3], 0.0).then_inc(S["g_evac"], 2)
            v.memset(tick[:, 3:4], 0.0).then_inc(S["e_acc"], 4)
            tn.base["e_acc"] = 4

            for m in range(12):
                do(v.memset(reg(XRAW + m * XRW, 4), 0.0), "pads" if m == 11 else None)
            wait("small_in", 48)
            wait("cact", 1)

            def mod_row(n):
                wait(f"ada_in{n % 8}", 16 * (n // 8 + 1))
                do(v.tensor_tensor_reduce(out=reg(CACT + 1024, D), in0=reg(ADA + (n % 8) * 1024, D), in1=reg(CACT, D),
                                          scale=1.0, scalar=0.0, op0=ALU.mult, op1=ALU.add,
                                          accum_out=mod[:, n:n + 1]), "mod_done")
            for n in range(16):
                mod_row(n)
            b_ada = pr("b_ada")
            tt(mod[:, 0:16], mod[:, 0:16], b_ada[:, 0:16], ALU.add)
            stt(gsc[:, 0:8], mod[:, 8:16], 1.0, pr("norm_mix"), ALU.add, ALU.mult)
            wait("rt1", 1)
            do(v.reciprocal(RS[:, 0:T], RS[:, 0:T]))
            wait("ss1", 1)

            def modulated(out, src, shift0, sem):
                for k in range(KT):
                    stt(reg(out + k * T, T), reg(src + k * T, T), gsc[:, k:k + 1], RS[:, 0:T], ALU.mult, ALU.mult)
                    ts(reg(out + k * T, T), reg(out + k * T, T), mod[:, shift0 + k:shift0 + k + 1], None, ALU.add,
                       sem=sem)
            modulated(H, X, 0, "h_ready")
            for n in range(16, 48):
                mod_row(n)
            tt(mod[:, 16:48], mod[:, 16:48], b_ada[:, 16:48], ALU.add)
            for m in range(4):
                do(v.memset(reg(POOLU + m * PUW, 16), 0.0))
            for m in range(2):
                do(v.memset(reg(PTMP + m * PUW, 16), 0.0))

            for m in range(12):
                wait("bank_free", 4 + tiles["in"] + m + 1)
                cw = PAR["conv_w"][0] + 4 * m
                src = XRAW + m * XRW + 1
                out = reg(CONV + m * T, T)
                ts(out, reg(src, T), par[:, cw:cw + 1], None, ALU.mult)
                for k in range(1, 4):
                    stt(out, reg(src + k, T), par[:, cw + k:cw + k + 1], out, ALU.mult, ALU.add,
                        "conv_acc" if k == 3 else None)

            wait("bank_free", 4 + 24)
            for g in range(POOL_G):
                u0 = POOLU + g * PUW
                cur = u0
                for n in range(g + 1):
                    nxt = PTMP + (n % 2) * PUW
                    tt(reg(nxt + 16, T), reg(cur + 16, T), reg(cur + 16 - (1 << n), T), ALU.add)
                    cur = nxt
                w = 2 << g
                y = YMIX + g * T
                ic = CONST["invcnt"][0] + g * 16
                tt(reg(y, 16), reg(cur + 16, 16), cst[:, ic:ic + 16], ALU.mult)
                ts(reg(y + 16, T - 16), reg(cur + 32, T - 16), 1.0 / w, None, ALU.mult)
                tt(reg(y, T), reg(y, T), reg(u0 + 16, T), ALU.subtract, "pooled")

            dtx, dte, dt_ = (A[0:16, DTB + n * T:DTB + (n + 1) * T] for n in range(3))
            dacs = RS[0:16, 0:T]
            wait("sel_in", 32)
            wait("dt_raw", 1)
            ts(dtx, dtx, small[0:16, 320:321], None, ALU.add, sem="dt_x")
            wait("dt_e", 1)
            ts(dt_, dte, 2.0, None, ALU.add)
            do(v.reciprocal(dt_, dt_))
            tt(dt_, dt_, dte, ALU.mult)
            tt(dte, dt_, dt_, ALU.mult)
            ts(dacs, dte, 2.0 / 17, 2.0 / 15, ALU.mult, ALU.add)
            for n in (13, 11, 9, 7, 5, 3, 1):
                tt(dacs, dacs, dte, ALU.mult)
                ts(dacs, dacs, 2.0 / n, None, ALU.add)
            tt(dacs, dacs, dt_, ALU.mult)
            stt(dt_, dtx, 0.0, dacs, ALU.max, ALU.add)
            ts(small[0:16, 324:325], small[0:16, 323:324], -1.0, None, ALU.mult)
            ts(dtx, dt_, small[0:16, 324:325], None, ALU.mult)
            do(v.tensor_tensor_scan(dacs, con("mask128", 16), dtx, 0.0, ALU.mult, ALU.add), "acs")
            ends = dacs.rearrange("p (c l) -> p c l", c=NCH)[:, :, CH - 1:CH].rearrange("p c o -> p (c o)")
            tt(small[0:16, 0:64].rearrange("p (h c) -> p h c", h=16),
               bc(cst[0:16, 0:16].unsqueeze(2), [16, 16, NCH]), bc(ends.unsqueeze(1), [16, 16, NCH]), ALU.mult, "aend_x")
            wait("acol_mm", 1)
            do(v.tensor_copy(small[:, 0:192], bank(6)[:, 0:192]), "acol_set")
            def cols(ap16, w):
                return bc(ap16.unsqueeze(2), [P, ap16.shape[1], w])
            for c in range(NCH):
                for b in range(2):
                    wait("xs_mm", 2 * c + b + 1)
                    tt(reg(XDT + c * 1024 + b * 512, 512).rearrange("p (h d) -> p h d", h=8),
                       bank(b).rearrange("p (h d) -> p h d", h=8),
                       cols(dtcol[:, c * 16 + b * 8:c * 16 + b * 8 + 8], HD), ALU.mult, "xdt")
            ae = aend.rearrange("p (h c) -> p h c", h=16)
            for c in range(3):
                tt(dtecol, ae[:, :, c:c + 1].rearrange("p h c -> p (h c)"), acol[:, c * 16:(c + 1) * 16], ALU.subtract,
                   "dte_x")
                wait("dte", c + 1)
                tt(reg(XDTE + c * 1024, 1024).rearrange("p (h d) -> p h d", h=16),
                   reg(XDT + c * 1024, 1024).rearrange("p (h d) -> p h d", h=16), cols(dtecol, HD), ALU.mult, "xdte")
            for g in range(2):
                wait("cb_mm", g + 1)
                tt(three(CBM + g * 512, 4, P), bank(2 + g).rearrange("p (c l) -> p c l", c=4),
                   bc(causal.unsqueeze(1), [P, 4, P]), ALU.mult, "cbm")
            wait("cdec", 1)
            cd = cdec.rearrange("p (h c) -> p h c", h=16)
            for c in range(3):
                for g in range(2):
                    wait("st_mm", 2 * c + g + 1)
                    hs = reg(HST + c * 1024 + g * 512, 512)
                    if c == 0:
                        do(v.tensor_copy(hs, bank(4 + g)), "hst")
                    else:
                        dk = cd[:, g * 8:(g + 1) * 8, c:c + 1].rearrange("p h c -> p (h c)")
                        tt(hs.rearrange("p (h d) -> p h d", h=8),
                           reg(HST + (c - 1) * 1024 + g * 512, 512).rearrange("p (h d) -> p h d", h=8),
                           cols(dk, HD), ALU.mult)
                        tt(hs, hs, bank(4 + g), ALU.add, "hst")
            ac3 = acol.rearrange("p (c h) -> p c h", c=4)
            wait("eacs", 1)
            for g in range(2):
                for h in range(8 * g, 8 * g + 9):
                    if h < 8 * g + 8:
                        wait("row_mm", h + 1)
                        if h >= 2:
                            wait("diag_mm", h - 1)
                        m = reg(MB_ + (h % 2) * T, T).rearrange("p (c l) -> p c l", c=4)
                        tt(m, bank(h % 2).rearrange("p (c l) -> p c l", c=4),
                           bc(ac3[:, :, h:h + 1], [P, 4, P]), ALU.subtract, "seg")
                    if h > 8 * g:
                        wait("dec_e", h)
                        m = reg(MB_ + ((h - 1) % 2) * T, T)
                        tt(m, m, reg(CBM + g * 512, 512), ALU.mult, "mdec")
                wait("diag_mm", 8 * (g + 1))
                for c in range(NCH):
                    y = reg(YTOK + c * 512, 512)
                    if c == 0:
                        if g:
                            wait("yt_mm", 4)
                        do(v.tensor_copy(y, bank(2)), "ytok")
                    else:
                        wait("yoff_mm", 3 * g + c)
                        tt(y.rearrange("p (h d) -> p h d", h=8), bank(6).rearrange("p (h d) -> p h d", h=8),
                           cols(eacs[:, c * 16 + 8 * g:c * 16 + 8 * g + 8], HD), ALU.mult, "yoff")
                        tt(y, y, bank(2 + c), ALU.add, "ytok")
                for m in range(4):
                    k = 4 * g + m
                    wait("yt_mm", k + 1)
                    y = reg(YMIX + (4 + k) * T, T)
                    stt(y, reg(CONV + k * T, T), pr("d_skip", k), bank(m % 2), ALU.mult, ALU.add)
                    tt(y, y, reg(Z + k * T, T), ALU.mult, "yt_ready")
            wait("rt2", 1)
            do(v.reciprocal(RS[:, 0:T], RS[:, 0:T]))
            for k in range(KT):
                y = reg(YMIX + (4 + k) * T, T)
                stt(y, y, pr("ssd_norm", k), RS[:, 0:T], ALU.mult, ALU.mult, "ymix")
            for g in range(POOL_G):
                wait("pool_mm", g + 1)
                ts(reg(YMIX + g * T, T), bank(2 * (g % 2)), pr("pool_b", g), pr("pool_scale", g), ALU.add, ALU.mult,
                   "pool_out")
            ev(tn, "out", 0)
            evacuate(tn, "out", 0, 8, lambda j, i: stt(
                A[:, bass.ds(i * (4 * T) + (X + j * T), T)], bank(2 * j), mod[:, bass.ds(i * 4 + (16 + j), 1)],
                A[:, bass.ds(i * (4 * T) + (X + j * T), T)], ALU.mult, ALU.add, "bank_free"))
            do(v.memset(tick[:, 4:5], 0.0), "x1_ready")
            stt(gsc[:, 0:8], mod[:, 32:40], 1.0, pr("norm_ffn"), ALU.add, ALU.mult)
            wait("rt3", 1)
            do(v.reciprocal(RS[:, 0:T], RS[:, 0:T]))
            modulated(H, X, 24, "h2_ready")

            def top16(rows, vals, idx, sem):
                def each(f, sem=None):
                    for n, s in enumerate(rows):
                        v0, v1 = reg(vals + n * 16, 8), reg(vals + n * 16 + 8, 8)
                        u0, u1 = (reg(idx + n * 16 + m, 8).bitcast(U32) for m in (0, 8))
                        do(f(s, v0, v1, u0, u1), sem if n == len(rows) - 1 else FREE)
                each(lambda s, v0, v1, u0, u1: v.max(v0, s))
                each(lambda s, v0, v1, u0, u1: v.max_index(u0, v0, s))
                each(lambda s, v0, v1, u0, u1: v.match_replace(s, v0, s, -3.0e38))
                each(lambda s, v0, v1, u0, u1: v.max(v1, s))
                each(lambda s, v0, v1, u0, u1: v.max_index(u1, v1, s), sem)

            sg = reg(SELX, 128), reg(SELX + 128, 128), reg(SELX + 256, 128)
            for i in range(4):
                wait("sc_set", i * 4 + 4)
                top16([reg(SC + hh * P, P) for hh in range(16)], PV, PUI, "sc_free")
                do(v.tensor_copy(reg(PIF, 256), reg(PUI, 256).bitcast(U32)))
                V4 = reg(PV, 256).rearrange("p (h x k) -> p h x k", h=PH, x=2)
                for h in range(PH):
                    tt(three(CAND + h * 256, 16, 16), bc(V4[:, h, 0, :].unsqueeze(2), [P, 16, 16]),
                       bc(V4[:, h, 1, :].unsqueeze(1), [P, 16, 16]), ALU.add, None if h == PH - 1 else FREE)
                top16([reg(CAND + h * 256, 256) for h in range(PH)], TV, TU, None)
                wait("slots_mm", i)
                tv3 = three(TV, PH, 16)
                tt(sg[2].rearrange("p (h k) -> p h k", h=PH), tv3, bc(tv3[:, :, 0:1], [P, PH, 16]), ALU.subtract,
                   "gate_x")
                tu = reg(TU, 128).bitcast(U32)
                tr, tc_ = reg(TU + 128, 128).bitcast(U32), reg(TU + 256, 128).bitcast(U32)
                do(v.tensor_scalar(tr, tu, 4, None, ALU.logical_shift_right))
                do(v.tensor_scalar(tc_, tu, 15, None, ALU.bitwise_and))
                do(v.tensor_copy(reg(TF, 256), reg(TU + 128, 256).bitcast(U32)))
                I4 = reg(PIF, 256).rearrange("p (h x k) -> p h x k", h=PH, x=2)
                for x in range(2):
                    for h in range(PH):
                        oh = three(OH + h * 256, 16, 16)
                        tt(oh, bc(con("iota16").unsqueeze(1), [P, 16, 16]),
                           bc(reg(TF + x * 128 + h * 16, 16).unsqueeze(2), [P, 16, 16]), ALU.is_equal,
                           None if h == PH - 1 else FREE)
                    for h in range(PH):
                        oh = three(OH + h * 256, 16, 16)
                        tt(oh, oh, bc(I4[:, h, x, :].unsqueeze(1), [P, 16, 16]), ALU.mult, None if h == PH - 1 else FREE)
                    do(v.tensor_reduce(sg[x], three(OH, 128, 16), AX.X, ALU.add))
                wait("gate_e", i + 1)
                g3 = sg[2].rearrange("p (h k) -> p h k", h=PH)
                do(v.tensor_reduce(small[:, 0:8], g3, AX.X, ALU.add))
                do(v.reciprocal(small[:, 0:8], small[:, 0:8]))
                tt(g3, g3, bc(small[:, 0:8].unsqueeze(2), [P, PH, 16]), ALU.mult, "sel")

            wait("slots_T", 8)
            with tn.loop(64, b_hot=2) as i:
                for u_ in range(2):
                    wait("g_mm", i * 2 + (u_ + 1))
                    for out, src in ((OA, I1T), (OB, I2T)):
                        tt(three(out + u_ * 512, 4, P), bc(con("iota").unsqueeze(1), [P, 4, P]),
                           bc(A[:, bass.ds(i * 8 + (src + 4 * u_), 4)].unsqueeze(2), [P, 4, P]), ALU.is_equal,
                           "b_hot" if out == OB else FREE)
            wait("g_stored0", 32)
            wait("g_stored1", 32)
            for k in range(0, 8 * T, 2 * T):
                do(v.tensor_copy(rr(HHI + k, 2 * T), reg(H + k, 2 * T)))
                tt(rr(H + k, 2 * T), reg(H + k, 2 * T), rr(HHI + k, 2 * T).bitcast(F32), ALU.subtract,
                   "hsplit" if k == 6 * T else FREE)
            do(v.memset(reg(YACC, 8 * T), 0.0))
            with tn.loop(EROUNDS, dve_own=2 * ER, e_w=ER, e_acc=8) as i:
                for r in range(ER):
                    wait(f"g_in{r}", i * 16 + 16)
                    wait("e_g", i * ER + (r + 1))
                    if r == 0:
                        wait("e_y", i * 8)
                    a_ = reg(ACTB + r * T, T)
                    tt(a_, a_, reg(GRING + r * T, T), ALU.mult)
                    do(v.tensor_copy(rr(WHI + r * T, T), a_))
                    tt(rr(WLO + r * T, T), a_, rr(WHI + r * T, T).bitcast(F32), ALU.subtract, "e_w")
                for d in range(KT):
                    wait("e_y", i * 8 + (d + 1))
                    tt(reg(YACC + d * T, T), reg(YACC + d * T, T), bank(4 + d % 4), ALU.add, "e_acc")
            wait("unspilled", 16)
            for k in range(KT):
                y = reg(YACC + k * T, T)
                stt(y, y, mod[:, 40 + k:41 + k], reg(X + k * T, T), ALU.mult, ALU.add, "xf_ready")
            wait("rt4", 1)
            do(v.reciprocal(RS[:, 0:T], RS[:, 0:T]))
            for k in range(KT):
                stt(reg(X + k * T2 + META, T), reg(YACC + k * T, T), pr("norm_final", k), RS[:, 0:T], ALU.mult, ALU.mult,
                    "h2in")

            def norm2(src, gname, sem, rt, out=XN):
                wait(rt, 1)
                do(v.reciprocal(RS[:, 0:T2], RS[:, 0:T2]))
                for k in range(KT):
                    stt(reg(out + k * T2, T2), reg(src + k * T2, T2), pr(gname, k), RS[:, 0:T2], ALU.mult, ALU.mult, sem)
            wait("meta_in", 16)
            norm2(X, "g_mix_pre", "xn_ready", "rt5")
            for h in range(GLH):
                wait("gate_mm", h + 1)
                ts(halves(reg(LA + h * T2, T2)), pair(h), pr("b_gate", h), None, ALU.add, sem="gate_lin")
            wait("ln_e", 1)
            L4, D4, E4 = reg(LA, 4 * T2), reg(DD, 4 * T2), reg(EE, 4 * T2)
            stt(L4, L4, 0.0, E4, ALU.min, ALU.subtract)
            ts(L4, L4, 1.0 / 16, None, ALU.mult)
            for h in range(GLH):
                do(v.tensor_tensor_scan(reg(DD + h * T2, T2), con("mask64"), reg(LA + h * T2, T2), 0.0, ALU.mult, ALU.add))
            d4 = D4.rearrange("p (h t) -> p h t", h=GLH)
            l4 = L4.rearrange("p (h t) -> p h t", h=GLH)
            do(v.tensor_copy(l4[:, :, 0:META], d4[:, :, 0:META]))
            for h in range(GLH):
                dh = d4[:, h, META:T2].rearrange("p (c l) -> p c l", l=GC)
                lh = l4[:, h, META:T2].rearrange("p (c l) -> p c l", l=GC)
                tt(lh, dh, bc(dh[:, :, GC // 2:GC // 2 + 1], [P, 8, GC]), ALU.subtract, "gd" if h == 3 else None)
            Q4, K4 = reg(PQ, 4 * T2), reg(PK, 4 * T2)
            scale = float(P) ** -0.5
            wait("bank_free", 4 + tiles["in2"] + 8)
            wait("ge1", 1)
            ts(Q4, Q4, scale, None, ALU.mult)
            tt(reg(QIN, 4 * T2), Q4, E4, ALU.mult, "gq")
            wait("ge2", 1)
            tt(reg(KIN, 4 * T2), K4, E4, ALU.mult, "gq")
            dec = reg(DEC, 36).rearrange("p (h c) -> p h c", h=GLH)
            for h in range(GLH):
                dh = d4[:, h, META:T2].rearrange("p (c l) -> p c l", l=GC)
                lh = l4[:, h, META:T2].rearrange("p (c l) -> p c l", l=GC)
                tt(lh, bc(dh[:, :, GC - 1:GC], [P, 8, GC]), dh, ALU.subtract)
                do(v.tensor_copy(dec[:, h, 1:9].unsqueeze(2), dh[:, :, GC - 1:GC]))
            tt(l4[:, :, 0:META], bc(d4[:, :, META - 1:META], [P, GLH, META]), d4[:, :, 0:META], ALU.subtract)
            do(v.tensor_copy(dec[:, :, 0:1], d4[:, :, META - 1:META]))
            wait("ge3", 1)
            tt(Q4, Q4, E4, ALU.mult, "gq")
            wait("ge4", 1)
            tt(K4, K4, E4, ALU.mult, "gq")
            for c, (t0, L) in enumerate(GCH):
                wait("gla_tr", c + 1)
                do(v.tensor_copy(reg(KTOK, 512, L), PS[0:L, 0:512]), "ktok")
                wait("gla_sc", c + 1)
                tt(reg(SM, 256, L).rearrange("p (h l) -> p h l", h=4)[:, :, 0:L],
                   PS[0:L, 1536:1792].rearrange("p (h l) -> p h l", h=4)[:, :, 0:L],
                   bc(causal[0:L, 0:L].unsqueeze(1), [L, 4, L]), ALU.mult, "sm")
                if c < len(GCH) - 1:
                    wait("gla_st", c + 1)
                    for h in range(GLH):
                        st = reg(ST + h * DV, DV)
                        new = PS[:, 3072 + h * DV:3072 + (h + 1) * DV]
                        if c == 0:
                            do(v.tensor_copy(st, new), "st")
                        else:
                            stt(st, st, dec[:, h, c:c + 1], new, ALU.mult, ALU.add, "st")
            wait("o_set", 9)
            wait("rt6", 4)
            do(v.reciprocal(L4, L4))
            for m in range(8):
                o = reg(PVV + m * T2, T2)
                stt(o, o, pr("gla_norm", m), reg(LA + (m // 2) * T2, T2), ALU.mult, ALU.mult,
                    "gla_done" if m == 7 else None)
            wait("bank_free", 4 + tiles["r2"] + 8)
            for m in range(8):
                o = reg(PVV + m * T2, T2)
                tt(o, o, reg(RR + m * T2, T2), ALU.mult, "o_ready")
            ev(tn, "ogla", 0)
            evacuate(tn, "ogla", 0, 8, lambda j, i: tt(
                halves(A[:, bass.ds(i * (4 * T2) + (PZG + j * T2), T2)]), pair(j),
                halves(A[:, bass.ds(i * (4 * T2) + (PZG + j * T2), T2)]), ALU.mult, "bank_free"))
            do(v.memset(reg(TT_, 1024), 0.0), "ogla_out")

            def reduced(x, t, n):
                ts(t, x, 1.0 / TWO_PI, MAGIC, ALU.mult, ALU.add)
                ts(t, t, MAGIC, None, ALU.subtract)
                stt(x, t, -C1, x, ALU.mult, ALU.add)
                stt(x, t, -C2, x, ALU.mult, ALU.add)
                ts(x, x, -PI_IN, PI_IN, ALU.max, ALU.min)
            r = lambda off: reg(off, 64)
            ar, ai = r(S5A), r(S5A + 64)
            wait("s5_e", 1)
            tt(r(AR5), ar, r(DT5), ALU.mult)
            tt(r(TH5), ai, r(DT5), ALU.mult)
            t0_ = reg(T5, 64)
            ts(t0_, r(TH5), 1.0 / TWO_PI, MAGIC, ALU.mult, ALU.add)
            ts(t0_, t0_, MAGIC, None, ALU.subtract)
            stt(r(TH5), t0_, -C1, r(TH5), ALU.mult, ALU.add)
            stt(r(TH5), t0_, -C2, r(TH5), ALU.mult, ALU.add)
            ts(r(SN1), r(TH5), -PI_IN, PI_IN, ALU.max, ALU.min)
            ts(r(CS1), r(TH5), np.pi / 2, None, ALU.add)
            reduced(r(CS1), t0_, 64)
            ts(r(PH5), r(TH5), float(SB), None, ALU.mult)
            reduced(r(PH5), t0_, 64)
            do(v.memset(tick[:, 4:5], 0.0), "s5_x")
            kk = bc(con("kk").unsqueeze(1), [P, S5G, SB + 1])
            t3 = lambda off: three(off, S5G, SB + 1)
            tt(t3(LMG), kk, bc(r(AR5).unsqueeze(2), [P, S5G, SB + 1]), ALU.mult)
            tt(t3(LI), kk, bc(r(TH5).unsqueeze(2), [P, S5G, SB + 1]), ALU.mult)
            ts(reg(LR, 576), reg(LI, 576), np.pi / 2, None, ALU.add)
            reduced(reg(LI, 576), reg(T5, 576), 576)
            reduced(reg(LR, 576), reg(T5, 576), 576)
            do(v.memset(tick[:, 4:5], 0.0), "s5_x")
            wait("s5_e", 5)
            a1, a2, a3 = reg(T5, 64), reg(T5 + 64, 64), reg(T5 + 128, 64)
            tt(a1, r(MG1), r(CS1), ALU.mult)
            ts(a1, a1, 1.0, None, ALU.subtract)
            tt(a2, r(MG1), r(SN1), ALU.mult)
            tt(r(FR), a1, ar, ALU.mult)
            tt(a3, a2, ai, ALU.mult)
            tt(r(FR), r(FR), a3, ALU.add)
            tt(r(FI), a2, ar, ALU.mult)
            tt(a3, a1, ai, ALU.mult)
            tt(r(FI), r(FI), a3, ALU.subtract)
            tt(a1, ar, ar, ALU.mult)
            tt(a2, ai, ai, ALU.mult)
            tt(a1, a1, a2, ALU.add)
            do(v.reciprocal(a1, a1))
            tt(r(FR), r(FR), a1, ALU.mult)
            tt(r(FI), r(FI), a1, ALU.mult)
            wait("s5_e", 8)
            tt(reg(LR, 576), reg(LR, 576), reg(LMG, 576), ALU.mult)
            tt(reg(LI, 576), reg(LI, 576), reg(LMG, 576), ALU.mult)
            PB, QB, PC, QC = (S5P + 1024 * n for n in range(4))
            b3 = lambda off: three(off, S5G, S5H)
            f3 = lambda off: bc(r(off).unsqueeze(2), [P, S5G, S5H])
            ts(reg(QB, 1024), reg(QB, 1024), con("sgn"), None, ALU.mult)
            ts(reg(PC, 1024), reg(PC, 1024), con("nsgn"), None, ALU.mult)
            ts(reg(QC, 1024), reg(QC, 1024), -1.0, None, ALU.mult)
            tt(b3(WT), b3(PB), f3(FI), ALU.mult)
            tt(b3(V9), b3(QB), f3(FI), ALU.mult)
            tt(b3(PB), b3(PB), f3(FR), ALU.mult)
            tt(b3(QB), b3(QB), f3(FR), ALU.mult)
            tt(reg(PB, 1024), reg(PB, 1024), reg(V9, 1024), ALU.add)
            tt(reg(QB, 1024), reg(QB, 1024), reg(WT, 1024), ALU.subtract)

            def part(off, n, i, a):
                return A[:, bass.ds(i * n + off, n)].rearrange("p (g h) -> p g h", g=GP)
            wait("uall_in", 16 * SB)
            with tn.loop(8, dve_own=23, s5_WT=1, s5_ang=1, s5_V9=1, s5_w=1, s5_H=1) as i:
                lr, li = part(LR, 72, i, 9), part(LI, 72, i, 9)
                pb, qb, pc, qc = (part(o, 128, i, 16) for o in (PB, QB, PC, QC))
                wt = reg(WT, 1024).rearrange("p (g s h) -> p g s h", g=GP, s=SB)
                v9t = reg(V9, 1024).rearrange("p (g s h) -> p g s h", g=GP, s=SB)
                v9 = reg(V9, 1152).rearrange("p (g s h) -> p g s h", g=GP, s=SB + 1)
                vq = reg(WT, 1152).rearrange("p (g s h) -> p g s h", g=GP, s=SB + 1)

                def outer(out, l, b, n, sem=None):
                    for g in range(GP):
                        tt(out[:, g], bc(l[:, g, 0:n].unsqueeze(2), [P, n, S5H]), bc(b[:, g, :].unsqueeze(1), [P, n, S5H]),
                           ALU.mult, sem if g == GP - 1 else FREE)
                wait("s5_ymm", i)
                do(v.tensor_copy(reg(BBP, 128), A[:, bass.ds(i * 128 + PB, 128)]))
                outer(wt, lr, pb, SB)
                outer(v9t, li, qb, SB)
                tt(reg(WT, 1024), reg(WT, 1024), reg(V9, 1024), ALU.add, "s5_WT")
                a3_ = three(ANG, GP, NB)
                tt(a3_, bc(con("cidx").unsqueeze(1), [P, GP, NB]), bc(A[:, bass.ds(i * 8 + PH5, 8)].unsqueeze(2), [P, GP, NB]),
                   ALU.mult)
                ts(reg(ANG2, 528), reg(ANG, 528), np.pi / 2, None, ALU.add)
                reduced(reg(ANG, 528), reg(T5, 528), 528)
                reduced(reg(ANG2, 528), reg(T5, 528), 528)
                do(v.memset(tick[:, 4:5], 0.0), "s5_ang")
                wait("s5_Wmm", i + 1)
                outer(v9, lr, pc, SB + 1)
                outer(vq, li, qc, SB + 1)
                tt(reg(V9, 1152), reg(V9, 1152), reg(WT, 1152), ALU.add, "s5_V9")
                wait("s5_cs", i * 2 + 2)
                tt(three(ANG2, GP, NB), bc(con("cmask").unsqueeze(1), [P, GP, NB]),
                   bc(A[:, bass.ds(i * 8 + MG8, 8)].unsqueeze(2), [P, GP, NB]), ALU.mult)
                wait("s5_Zmm", i * 2 + 1)
                wait("s5_S", i + 1)
                tt(reg(SS, 528), reg(SS, 528), reg(COS, 528), ALU.mult)
                tt(halves(reg(S2, 528)), halves(reg(SIN, 528)), pair(3), ALU.mult)
                tt(reg(SS, 528), reg(SS, 528), reg(S2, 528), ALU.add)
                do(v.tensor_tensor_scan(reg(S2, 528), reg(ANG2, 528), reg(SS, 528), 0.0, ALU.mult, ALU.add), "s5_w")
                tt(reg(SS, 528), reg(S2, 528), reg(COS, 528), ALU.mult)
                wait("s5_Zmm", i * 2 + 2)
                tt(halves(reg(ANG, 528)), halves(reg(SIN, 528)), pair(3), ALU.mult)
                tt(reg(SS, 528), reg(SS, 528), reg(ANG, 528), ALU.subtract, "s5_H")
            wait("y8_in", 16)
            for m in range(8):
                y = reg(Y8 + m * T2, T2)
                stt(y, reg(PU + m * T2, T2), pr("d_skip_2", m), y, ALU.mult, ALU.add, "s5_out")
            wait("bank_free", 4 + tiles["glu"] + 16)
            tt(reg(Y8, XW), reg(Y8, XW), reg(YALL, XW), ALU.mult)
            tt(reg(Y8, XW), reg(Y8, XW), reg(PZS, XW), ALU.mult)
            tt(reg(PZG, XW), reg(PZG, XW), reg(Y8, XW), ALU.add, "mixed")

            def residual(src, gname, rt, sem):
                wait(rt, 1)
                do(v.reciprocal(RS[:, 0:T2], RS[:, 0:T2]))
                for k in range(KT):
                    s = reg(src + k * T2, T2)
                    stt(s, s, pr(gname, k), RS[:, 0:T2], ALU.mult, ALU.mult)
                    tt(reg(X + k * T2, T2), reg(X + k * T2, T2), s, ALU.add, sem)
            residual(MO, "g_mix_post", "rt7", "h_mid")
            norm2(X, "g_ffn_pre", "hn_ready", "rt8")
            with tn.loop(32, dve_own=1) as i:
                wait("bank_free", i + (5 + tiles["ff1"]))
                f = A[:, bass.ds(i * T2 + FF, T2)]
                tt(f, f, f, ALU.mult)
            do(v.memset(tick[:, 4:5], 0.0), "ff1_out")
            residual(MO, "g_ffn_post", "rt9", "h_end")
            do(v.memset(tick[:, 4:5], 0.0), "fin")

        pass


def constants():
    c = np.zeros((P, NCONST), np.float32)

    def put(name, a):
        o, w = CONST[name]
        c[:, o:o + w] = a
    n = np.arange(P)
    put("ident", np.eye(P))
    put("causal", n[:, None] <= n[None, :])
    put("ones", 1.0)
    sw = np.zeros((P, P))
    h = P // 2
    sw[h + np.arange(h), np.arange(h)] = 1.0
    sw[np.arange(h), h + np.arange(h)] = -1.0
    put("swap", sw)
    put("iota", n[None, :])
    put("iota16", np.arange(16)[None, :])
    put("mask64", (~np.isin(np.arange(T2), [t0 for t0, _ in GCH]))[None, :])
    put("mask128", (np.arange(T) % CH != 0)[None, :])
    t = np.arange(16)
    put("invcnt", np.concatenate([1.0 / np.minimum(t + 1, 2 << g) for g in range(POOL_G)])[None, :])
    put("cidx", np.arange(NB)[None, :])
    put("cmask", (np.arange(NB) > 0)[None, :])
    put("kk", np.arange(SB + 1)[None, :])
    put("sgn", np.where(n < h, -1.0, 1.0)[:, None])
    put("nsgn", np.where(n < h, 1.0, -1.0)[:, None])
    sel = np.zeros((16, 16, P), np.float32)
    sel[np.arange(16), np.arange(16), :] = 1.0
    return c, sel.reshape(16, 2048)


def tiled(w, kt=8):
    K, M = w.shape
    return np.ascontiguousarray(w.reshape(K // (kt * P), kt, P, M // P, P).transpose(3, 0, 2, 1, 4)
                                .reshape(M // P * (K // (kt * P)), P, kt * P))


def feat(v):
    return v.reshape(-1, P).T


def kernel(**inp):
    from concourse import bacc
    from concourse.bass_utils import run_bass_kernel_spmd

    i = {k: np.asarray(v) for k, v in inp.items()}
    s_z, s_x = 512, 1536
    s_dt = s_x + 1536
    w_in = i["w_in"][0]
    arr = {}
    arr["consts"], arr["sel"] = constants()
    arr["params"] = np.ascontiguousarray(np.concatenate([
        feat(i["norm_mix"][0]), feat(i["norm_ffn"][0]), feat(i["norm_final"]), feat(i["ssd_norm"][0]),
        feat(i["b_ada"][0]), feat(i["pool_b"][0].reshape(-1)), feat(i["pool_scale"][0].reshape(-1)),
        i["conv_w"][0].reshape(4, 12, P).transpose(2, 1, 0).reshape(P, 48), feat(i["conv_b"][0]),
        feat(np.repeat(i["d_skip"][0], HD)), feat(i["g_mix_pre_2"][0]), feat(i["g_mix_post_2"][0]),
        feat(i["g_ffn_pre_2"][0]), feat(i["g_ffn_post_2"][0]), feat(i["gla_norm_g_2"][0].reshape(-1)),
        feat(i["b_gate_2"][0]), feat(i["d_skip_2"][0]), feat(i["b_glu_2"][0])], axis=1))
    w2 = i["w_in_2"][0]
    q, k, v, r, al, u, g1 = 512, 1024, 2048, 3072, 3088, 4112, 5136
    lay16 = lambda w: w.reshape(8, P, 16).transpose(1, 0, 2).reshape(P, 128)
    arr["w16"] = np.ascontiguousarray(np.concatenate([lay16(w_in[:, s_dt:]), lay16(w2[:, r:al])], axis=1))
    arr["dtal"] = np.ascontiguousarray(np.stack([i["dt_bias"][0], i["a_log"][0]], axis=1))
    arr["xT"] = np.ascontiguousarray(i["x"][0].T)
    arr["c"] = np.ascontiguousarray(i["c"])
    arr["w_ada"] = np.ascontiguousarray(i["w_ada"][0].T.reshape(48, P, D))
    arr["w_in"] = tiled(np.concatenate([w_in[:, s_x:s_dt], w_in[:, s_z:s_x], w_in[:, :s_z]], axis=1))
    arr["w_out"] = tiled(i["w_out"][0], 12)
    arr["w_query"] = tiled(i["w_query"][0])
    arr["keys"] = np.ascontiguousarray(np.stack([i["sub_keys1"][0], i["sub_keys2"][0]], axis=1).transpose(3, 0, 1, 2)
                                       .reshape(P, 2048))
    arr["pool_w"] = np.ascontiguousarray(i["pool_w"][0])
    arr["down"] = np.ascontiguousarray(i["expert_down"][0].reshape(P, NKEY, KT, P).transpose(1, 3, 2, 0)
                                       .reshape(NKEY, P, D))
    arr["up"] = np.ascontiguousarray(i["expert_up"][0].reshape(P, NKEY, D).transpose(1, 0, 2))
    arr["metaT"] = np.ascontiguousarray(i["meta_tokens_2"].T)
    arr["w_gate_up"] = np.ascontiguousarray(i["w_gate_up_2"][0])
    arr["w_in2"] = tiled(np.concatenate([w2[:, :v], w2[:, al:]], axis=1))
    arr["w_r2"] = tiled(w2[:, v:r])
    arr["w_ogla"] = tiled(i["w_o_gla_2"][0])
    arr["w_glu"] = tiled(i["w_glu_2"][0])
    arr["w_out2"] = tiled(i["w_out_2"][0])
    arr["w_ff1"] = tiled(i["w_ff1_2"][0])
    arr["w_ff2"] = tiled(i["w_ff2_2"][0], 16)
    twice = lambda a, b: np.concatenate([a, b], axis=0)
    s = lambda name: i[name][0]
    arr["s5a"] = np.ascontiguousarray(np.concatenate([
        twice(s("a_re_2").T, s("a_re_2").T), twice(s("a_im_2").T, s("a_im_2").T),
        np.broadcast_to(s("log_step_2")[None], (P, S5G))], axis=1))
    bt = lambda name: s(name).transpose(1, 0, 2).reshape(S5N, S5G * S5H)
    ct = lambda name: s(name).transpose(2, 0, 1).reshape(S5N, S5G * S5H)
    arr["s5bc"] = np.ascontiguousarray(np.concatenate([
        twice(bt("b_re_2"), bt("b_im_2")), twice(bt("b_im_2"), bt("b_re_2")),
        twice(ct("c_re_2"), ct("c_im_2")), twice(ct("c_im_2"), ct("c_re_2"))], axis=1))

    nc = bacc.Bacc("TRN2", target_bir_lowering=False, num_devices=1)
    io = {n: nc.dram_tensor(f"in_{n}", a.shape, F32, kind="ExternalInput").ap() for n, a in arr.items()}
    io["out"] = nc.dram_tensor("out_0", (D, T), F32, kind="ExternalOutput").ap()
    for n, shape in (("gates", (NKEY, P, T)), ("spill", (P, KT * T)), ("u_d", (8, P, T2)), ("y_d", (8, P, T2))):
        io[n] = nc.dram_tensor(f"scratch_{n}", shape, F32, kind="Internal").ap()
    build(nc, io)
    res = run_bass_kernel_spmd(nc, [{f"in_{n}": a for n, a in arr.items()}], core_ids=[0])
    return np.ascontiguousarray(res.results[0]["out_0"].T)[None]
```

```python
import numpy as np
from contextlib import ExitStack, contextmanager

import concourse.bass as bass
from concourse import mybir

F32 = mybir.dt.float32
F32R = mybir.dt.float32r
U32 = mybir.dt.uint32
ALU = mybir.AluOpType
ACT = mybir.ActivationFunctionType
AX = mybir.AxisListType

P = 128
D, T = 1024, 512
KT = D // P
EPS = 1e-6

POOL_G = 4
HEADS, HD = 16, 64
CH = 128
NCH = T // CH
PH, TOPK, NKEY = 8, 16, 128
SLOTS = PH * TOPK

META = 16
T2 = T + META
GLH, DV = 4, 256
GC = 64
GCH = [(0, META)] + [(META + GC * c, GC) for c in range(T // GC)]
S5G, S5H, S5N = 64, 16, 64
SB = 8
NB = T2 // SB
GP = P // S5H

ER = 4
EROUNDS = NKEY // ER
SPLIT_ORDER = [("d", 0), ("d", 1), ("u", 0), ("u", 1), ("d", 2), ("u", 2), ("d", 3), ("u", 3)]

CONST = {}
_at = 0
for _n, _w in [("ident", P), ("causal", P), ("ones", P), ("swap", P), ("iota", P), ("iota16", 16), ("mask64", T2),
               ("mask128", T), ("invcnt", POOL_G * 16), ("cidx", NB), ("cmask", NB), ("kk", SB + 1), ("sgn", 1),
               ("nsgn", 1)]:
    CONST[_n] = (_at, _w)
    _at += _w
NCONST = _at

PAR = {}
_at = 0
for _n, _w in [("norm_mix", 8), ("norm_ffn", 8), ("norm_final", 8), ("ssd_norm", 8), ("b_ada", 48), ("pool_b", 4),
               ("pool_scale", 4), ("conv_w", 48), ("conv_b", 12), ("d_skip", 8), ("g_mix_pre", 8), ("g_mix_post", 8),
               ("g_ffn_pre", 8), ("g_ffn_post", 8), ("gla_norm", 8), ("b_gate", 4), ("d_skip_2", 8), ("b_glu", 16)]:
    PAR[_n] = (_at, _w)
    _at += _w
NPAR = _at

TWO_PI = 2.0 * np.pi
MAGIC = 12582912.0
C1 = 6.28125
C2 = float(np.float32(TWO_PI - 6.28125))
PI_IN = 3.1415925

STAGES = {
    "in": (24, 8, 1, T), "out": (8, 12, 1, T), "query": (16, 8, 1, T),
    "in2": (32, 8, 1, T2), "r2": (16, 8, 1, T2), "ogla": (8, 8, 1, T2), "glu": (16, 8, 1, T2),
    "out2": (8, 8, 1, T2), "ff1a": (16, 8, 1, T2), "ff2a": (8, 8, 2, T2), "ff1b": (16, 8, 1, T2), "ff2b": (8, 8, 2, T2),
}
SPLIT = ("in2", "r2", "ogla", "glu", "out2", "ff1a", "ff2a", "ff1b", "ff2b")
NSLOT, SLOT = 4, 2048


SHARED = {
    "act_events": [("cact", 1), ("sq1", 1), ("rt1", 1), ("dt_raw", 1), ("conv_out", 12), ("dt_e", 1), ("eacs", 1),
                   ("cdec", 1), ("dte", 3), ("btok", 2), ("dec_e", 16), ("sq2", 1), ("rt2", 1), ("sq3", 1), ("rt3", 1),
                   ("e_g", 128), ("sq4", 1), ("rt4", 1), ("sq5", 1), ("rt5", 1), ("alow", 1), ("ln_e", 1), ("ge1", 1),
                   ("ge2", 1), ("ge3", 1), ("ge4", 1), ("sq6", 1), ("rt6", 4), ("s5_e", 8), ("gs", 8), ("sq7", 1),
                   ("rt7", 1), ("sq8", 1), ("rt8", 1), ("sq9", 1), ("rt9", 1)],
    "act_1": [("sc_set", 16), ("s5_cs", 16)],
    "act_2": [("gate_e", 4), ("s5_W", 16)],
    "act_3": [("slots_T", 8), ("s5_K", 16)],
    "act_4": [("vtok", 9), ("s5_S", 8)],
    "act_5": [("o_set", 9), ("s5_y", 8)],
    "pe_events": [("ss1", 1), ("dt_mm", 1), ("btok_mm", 2), ("cb_mm", 2), ("xs_mm", 8), ("st_mm", 6),
                  ("ss2", 1), ("pool_mm", 4), ("ss3", 1), ("ss4", 1), ("ss5", 1), ("alow_mm", 1), ("gate_mm", 4),
                  ("ss6", 4), ("ss7", 1), ("ss8", 1), ("ss9", 1)],
    "pe_1": [("row_mm", 16), ("sc_mm", 4), ("gla_tr", 9), ("s5_Wmm", 8)],
    "pe_2": [("diag_mm", 16), ("slots_mm", 4), ("gla_sc", 9), ("s5_Kmm", 8)],
    "pe_3": [("yoff_mm", 6), ("e_u", 128), ("gla_o", 9), ("s5_Smm", 8)],
    "pe_4": [("yt_mm", 8), ("e_y", 256), ("gla_st", 8), ("s5_Zmm", 16)],
    "pe_5": [("acol_mm", 1), ("s5_ymm", 8)],
    "dma_1": [("g_stored0", 32), ("T_in", 1024)],
    "dve_events": [("pads", 1), ("h_ready", 8), ("conv_acc", 12), ("pooled", 4), ("dt_x", 1), ("acs", 1), ("aend_x", 1),
                   ("acol_set", 1), ("xdt", 8), ("cbm", 2), ("hst", 6), ("ymix", 8), ("pool_out", 4), ("x1_ready", 1),
                   ("h2_ready", 8), ("hsplit", 1), ("xf_ready", 8), ("h2in", 8), ("xn_ready", 8), ("xn_split", 1), ("gate_lin", 4), ("gd", 1),
                   ("gq", 4), ("xn_moved", 1), ("o_split", 1), ("ogla_out", 1), ("s5_x", 2), ("s5_out", 8),
                   ("gs_split", 1), ("mixed", 1), ("h_mid", 8), ("hn_split", 1), ("ff_split", 32), ("mo_sum", 1), ("h_end", 8), ("fin", 1)],
    "act_6": [("u_hi", 128), ("l_hi", 144)],
    "pool_1": [("u_lo", 128), ("l_lo", 144)],
    "dve_1": [("dte_x", 3), ("seg", 16), ("sc_free", 4), ("ktok", 9), ("s5_WT", 8)],
    "dve_2": [("xdte", 3), ("mdec", 16), ("gate_x", 4), ("sm", 9), ("s5_ang", 8)],
    "dve_3": [("yoff", 6), ("sel", 4), ("st", 32), ("s5_V9", 8)],
    "dve_4": [("ytok", 8), ("b_hot", 128), ("s5_w", 8)],
    "dve_5": [("yt_ready", 8), ("e_w", 128), ("s5_H", 8)],
}
PLACE = {}
for _s, _names in SHARED.items():
    _at = 0
    for _n, _w in _names:
        assert _n not in PLACE
        PLACE[_n] = (_s, _at)
        _at += _w


class Sems:

    def __init__(self, nc, ctx):
        self.nc, self.ctx, self.made = nc, ctx, {}

    def __getitem__(self, name):
        name = PLACE.get(name, (name, 0))[0]
        if name not in self.made:
            self.made[name] = self.ctx.enter_context(self.nc.semaphore(name))
        return self.made[name]

    def base(self, name):
        return PLACE.get(name, (name, 0))[1]


FREE = "free"


class Turn:

    def __init__(self, eng, sems, own):
        self.eng, self.sems, self.own = eng, sems, own
        self.base, self.k, self.per, self.i = {}, {}, {}, None

    def do(self, ins, sem=None):
        if sem == FREE:
            return
        sem = sem or self.own
        later, sem = sem[0] == "~", sem.lstrip("~")
        ins.then_inc(self.sems[sem], 1)
        if self.i is None:
            self.base[sem] = self.base.get(sem, 0) + 1
            if later:
                return
            self.eng.wait_ge(self.sems[sem], self.sems.base(sem) + self.base[sem])
        else:
            self.k[sem] = self.k.get(sem, 0) + 1
            if later:
                return
            self.eng.wait_ge(self.sems[sem], self.i * self.per[sem] + (self.sems.base(sem) + self.base.get(sem, 0) + self.k[sem]))

    def wait(self, sem, value):
        self.eng.wait_ge(self.sems[sem], self.sems.base(sem) + value)

    @contextmanager
    def loop(self, n, **per):
        with self.eng.Fori(0, n) as i:
            self.i, self.per, self.k = i, per, {}
            yield i
            assert self.k == per, (self.k, per)
        self.i = None
        for sem, m in per.items():
            self.base[sem] = self.base.get(sem, 0) + m * n


def build(nc, io):
    ctx = ExitStack()
    with ctx:
        def sb(name, shape, dt=F32):
            return ctx.enter_context(nc.sbuf_tensor(name, shape, dt))

        S = Sems(nc, ctx)

        ARENA = 49408
        at = (nc.sbuf_base + 31) // 32 * 32
        A = nc.alloc_sbuf_tensor_at("arena", [P, ARENA], F32, offset=at)
        sb("fence", [P, ARENA + 8])
        PS = ctx.enter_context(nc.psum_tensor("psum", [P, 4096], F32))
        cst = sb("cst", [P, NCONST])
        par = sb("par", [P, NPAR])
        mod = sb("mod", [P, 48])
        gsc = sb("gsc", [P, 16])
        RS = sb("rs", [P, T2])
        w16 = sb("w16", [P, 256])
        small = sb("small", [P, 336])
        tick = sb("tick", [P, 8])

        RING = 0
        X = NSLOT * SLOT
        XW = KT * T2
        H = X + XW
        R0 = H + XW

        def reg(off, n, parts=P):
            return A[0:parts, off:off + n]

        parts_r = {}

        def as_r(off, n, size, use="e"):
            for o in range(off, off + n, size):
                parts_r[use, o] = (size, nc.alloc_sbuf_tensor_at(f"{use}_r{o}", [P, size], F32R, offset=at + 4 * o))

        def rr(off, n, use="e"):
            o = max(o for w, o in parts_r if w == use and o <= off)
            assert off + n <= o + parts_r[use, o][0]
            return parts_r[use, o][1][:, off - o:off - o + n]

        def con(name, parts=P):
            a, w = CONST[name]
            return cst[0:parts, a:a + w]

        def pr(name, j=None):
            a, w = PAR[name]
            return par[:, a:a + w] if j is None else par[:, a + j:a + j + 1]

        def bank(b, w=512, parts=P):
            return PS[0:parts, b * 512:b * 512 + w]

        def pair(b, parts=P):
            return PS[0:parts, b * 1024:(b + 1) * 1024].rearrange("p (h x) -> p h x", h=2)[:, :, 0:T2 // 2]

        def halves(ap):
            return ap.rearrange("p (h x) -> p h x", h=2)

        def bc(ap, shape):
            return ap.broadcast_to(shape)

        ident = con("ident")
        ones = con("ones")
        causal = con("causal")

        XRAW = R0
        XRW = 4 + T
        CONV = XRAW + 12 * XRW
        Z = CONV + 12 * T
        YMIX = Z + 8 * T
        POOLU = YMIX + 12 * T
        PUW = 16 + T
        PTMP = POOLU + 4 * PUW
        SEL = PTMP + 2 * PUW
        XDTE = SEL + 2048
        CBM = XDTE + 3072
        assert CBM + 1024 <= ARENA
        XDT = XRAW
        MB_ = XRAW + 4096
        PWT = CBM + 1024
        assert PWT + 512 <= ARENA
        YTOK = POOLU
        HST = H
        BTOK = H + 3072
        ADA = POOLU
        CACT = YMIX
        DTB = YMIX + 4 * T
        QT = R0
        KEYS = QT + 16 * T
        SC = KEYS + 2048
        CAND = SC + 2048
        OH = CAND + 2048
        OH2 = OH + 2048
        PV = OH2 + 2048
        PUI = PV + 256
        PIF = PUI + 256
        TV = PIF + 256
        TU = TV + 128
        TF = TU + 3 * 128
        SELX = TF + 2 * 128
        GSTG = R0
        I1T, I2T, GT = X, X + T, X + 2 * T
        GB = 4
        OA, OB = RING + 4096, RING + 4096 + GB * 512
        YACC = R0
        GRING = YACC + 8 * T
        ACTB = GRING + ER * T
        WHI, WLO = ACTB + ER * T, ACTB + 2 * ER * T
        HHI = WLO + ER * T
        DHI, DLO = HHI + 8 * T, HHI + 8 * T + 2048
        UHI, ULO = DLO + 2048, DLO + 2048 + 4096
        assert ULO + 4096 <= ARENA
        for o_, n_, size_ in ((H, 8 * T, 2 * T), (WHI, 2 * ER * T, T), (HHI, 8 * T, 2 * T),
                              (DHI, 4096, 1024), (UHI, 8192, 1024)):
            as_r(o_, n_, size_)
        PROJ = R0
        PQ, PK, PVV, PU, PZG, PZS = (PROJ + T2 * n for n in (0, 4, 8, 16, 24, 32))
        TMP = PROJ + 40 * T2
        LA, DD, EE, QIN, KIN = (TMP + 4 * T2 * n for n in range(5))
        DEC = TMP + 20 * T2
        assert DEC + 36 <= ARENA
        KTOK, VTOK, ST, SM = DD, DD + 512, DD + 1536, LA
        RR = QIN
        UALL, YALL = PROJ, PROJ + 8 * T2
        Y8 = PROJ
        S5P = TMP
        WT, V9A, V9B, TT_, MSK = (S5P + 4096 + n for n in (0, 1152, 2304, 3456, 4480))
        WW, KALL = RING + 1024, RING + SLOT + 1024
        COS, SIN, SS, S2 = (S5P + 4096 + 5376 + 528 * n for n in range(4))
        RSX = COS
        assert S2 + 528 <= ARENA
        XN = H
        ANG, ANG2 = XN, XN + 528
        S5A = XN + 1056
        DT5, AR5, TH5, PH5, MG1, MG8, SN1, CS1, FR, FI = (S5A + 192 + 64 * n for n in range(10))
        BBP = S5A + 192 + 640
        LR, LI, LMG = BBP + 128, BBP + 128 + 576, RSX
        T5 = LI + 576
        assert T5 + 1056 <= XN + XW and ANG2 == ANG + 528
        FF, FFH = R0, R0 + 16 * T2
        ff = lambda m: (m % 4) * 4 * T2 + m // 4 * T2
        MO = R0 + 32 * T2
        XH1, XH2, XH3 = PZS, DD, R0 + 40 * T2
        for o_, size_, use_ in ((XN, T2, "l"), (XH3, T2, "l"), (XH1, T2, "p"), (XH2, XW, "p"), (PVV, T2, "p"),
                                (PU, T2, "p"), (PZG, T2, "p"), (FF, 4 * T2, "f")):
            as_r(o_, 32 * T2 if use_ == "f" else XW, size_, use_)
        for s_ in range(NSLOT):
            as_r(RING + s_ * SLOT + 1024, 1024, 1024, "l")
        MO2 = R0

        acol = small[:, 0:64]
        dtcol = small[:, 64:128]
        aend = small[:, 128:192]
        cdec = small[:, 192:256]
        eacs = small[:, 256:320]
        dtecol = small[:, 320:336]

        def wslot(s, kt, mcols=P):
            return reg(RING + s * SLOT, kt * mcols).rearrange("p (k m) -> p k m", k=kt)

        units, tiles, arr = {}, {}, {}
        u = t = 0
        a = [0] * NSLOT
        for name, (nt, kt, parts, w) in STAGES.items():
            units[name], tiles[name], arr[name] = u, t, list(a)
            u += nt * parts
            t += nt
            a = [x + nt * parts // NSLOT for x in a]
        su, SPLITS = {}, 0
        for name in SPLIT:
            su[name] = SPLITS
            SPLITS += STAGES[name][0] * STAGES[name][2]

        def hi_lo(q):
            return RING + 2 * (q % 2) * SLOT + 1024, RING + (2 * (q % 2) + 1) * SLOT + 1024

        def load_split(sp, names):
            for name in names:
                nt, kt, parts, w = STAGES[name]
                src = io["w_" + name]
                first = su[name] == 0
                if first:
                    for s in range(NSLOT):
                        sp.dma_start(reg(RING + s * SLOT, 1024), src[s]).then_inc(S[f"w_in{s}"], 16)
                with sp.Fori(1 if first else 0, nt * parts // NSLOT) as i:
                    for s in range(NSLOT):
                        sp.wait_ge(S["l_lo"], S.base("l_lo") + i * NSLOT + (su[name] + s - 3))
                        sp.dma_start(reg(RING + s * SLOT, 1024),
                                     src[bass.ds(i * NSLOT + s, 1)].rearrange("o p n -> (o p) n"))\
                          .then_inc(S[f"w_in{s}"], 16)

        def split_products(pe, name, rhs):
            nt, kt, parts, w = STAGES[name]
            with pe.Fori(0, nt // 4) as i:
                for j in range(4):
                    for p in range(parts):
                        v = j * parts + p
                        hi, lo = hi_lo(v)
                        pe.wait_ge(S["l_lo"], S.base("l_lo") + i * (4 * parts) + (su[name] + v + 1))
                        if p == 0:
                            pe.wait_ge(S["bank_free"], S.base("bank_free") + i * 4 + (tiles[name] + j + 1))
                        for k in range(kt):
                            xh, xl = rhs(p * kt + k)
                            for n, (w_, x_) in enumerate(((hi, xh), (hi, xl), (lo, xh))):
                                for h in range(2):
                                    last = nc.tensor.matmul(bank(2 * j + h, w // 2), rr(w_ + k * P, P, "l"),
                                                            x_[:, h * (w // 2):(h + 1) * (w // 2)],
                                                            start=(p == 0 and k == 0 and n == 0),
                                                            stop=(p == parts - 1 and k == kt - 1 and n == 2))
                        last.then_inc(S["unit_done"], 1)

        def rounds(i, m):
            return 0 if i is None else i * m

        def weights_hi(tn, name, i, v):
            parts = STAGES[name][2]
            s = v % NSLOT
            tn.wait(f"w_in{s}", rounds(i, 16 * parts) + 16 * (arr[name][s] + v // NSLOT + 1))
            tn.wait("unit_done", rounds(i, 4 * parts) + (units[name] + v - 1))
            tn.do(nc.scalar.activation(rr(hi_lo(v)[0], 1024, "l"), reg(RING + s * SLOT, 1024), ACT.Copy), "l_hi")

        def load_stage(sp, name):
            nt, kt, parts, w = STAGES[name]
            src = io["w_" + name]
            n = kt * P
            first = name == "in"
            if first:
                for s in range(NSLOT):
                    sp.dma_start(reg(RING + s * SLOT, n), src[s]).then_inc(S[f"w_in{s}"], 16)
            with sp.Fori(1 if first else 0, nt * parts // NSLOT) as i:
                for s in range(NSLOT):
                    sp.wait_ge(S["unit_done"], S.base("unit_done") + i * NSLOT + (units[name] + s - 3))
                    sp.dma_start(reg(RING + s * SLOT, n), src[bass.ds(i * NSLOT + s, 1)].rearrange("o p n -> (o p) n"))\
                      .then_inc(S[f"w_in{s}"], 16)

        def stage_products(pe, name, rhs):
            nt, kt, parts, w = STAGES[name]
            cols = [(0, w)] if w <= 512 else [(0, w // 2), (w // 2, w // 2)]
            with pe.Fori(0, nt // 4) as i:
                for j in range(4):
                    for p in range(parts):
                        v = j * parts + p
                        s = v % NSLOT
                        pe.wait_ge(S[f"w_in{s}"], S.base(f"w_in{s}") + i * (16 * parts) + 16 * (arr[name][s] + v // NSLOT + 1))
                        if p == 0:
                            pe.wait_ge(S["bank_free"], S.base("bank_free") + i * 4 + (tiles[name] + j + 1))
                        for k in range(kt):
                            for h, (c0, cw) in enumerate(cols):
                                last = nc.tensor.matmul(bank(2 * j + h, cw), wslot(s, kt)[:, k, :],
                                                        rhs(p * kt + k, c0, cw), start=(p == 0 and k == 0),
                                                        stop=(p == parts - 1 and k == kt - 1))
                        last.then_inc(S["unit_done"], 1)

        def evacuate(tn, name, first, n, op, ahead=False):
            parts = STAGES[name][2]
            with tn.loop(n // 4, bank_free=4, **({"l_hi": 4} if ahead else {})) as i:
                for j in range(4):
                    tn.wait("unit_done", i * (4 * parts) + (units[name] + parts * (first + j + 1)))
                    op(j, i)
                    if ahead:
                        weights_hi(tn, name, i, first + j + 2)

        def ev(tn, name, first):
            tn.base["bank_free"] = 4 + tiles[name] + first

        def s5_count(i, u, m, c=0):
            return m * u + c if i is None else i * (2 * m) + (m * u + c)

        def s5_at(i, u, off, n):
            return A[:, off + n * u:off + n * (u + 1)] if i is None else A[:, bass.ds(i * (2 * n) + (off + n * u), n)]

        block = ctx.enter_context(nc.Block())

        @block.sync
        def _(sp):
            load_stage(sp, "in")
            load_stage(sp, "out")
            load_stage(sp, "query")

            def tile(src, i, r):
                return src[r] if i is None else src[bass.ds(i * ER + r, 1)].rearrange("o p n -> (o p) n")

            def load_down(i):
                for r in range(ER):
                    if i is not None:
                        sp.wait_ge(S["d_lo"], S.base("d_lo") + i * ER + (r - 3))
                    sp.dma_start(reg(RING + r * 1024, 1024), tile(io["down"], i, r)).then_inc(S[f"down_in{r}"], 16)

            def load_gates(i):
                for r in range(ER):
                    if i is not None:
                        sp.wait_ge(S["e_w"], S.base("e_w") + i * ER + (r - 3))
                    sp.dma_start(reg(GRING + r * T, T), tile(io["gates"], i, r)).then_inc(S[f"g_in{r}"], 16)

            def load_up(i):
                for r in range(ER):
                    if i is not None:
                        sp.wait_ge(S["u_lo"], S.base("u_lo") + i * ER + (r - 3))
                    sp.dma_start(reg(RING + 4096 + r * 1024, 1024), tile(io["up"], i, r)).then_inc(S[f"up_in{r}"], 16)

            sp.wait_ge(S["unit_done"], S.base("unit_done") + units["query"] + 16)
            load_down(None)
            for tb in range(4):
                sp.wait_ge(S["g_evac"], S.base("g_evac") + GB + 32 * (tb + 1))
                sp.dma_start(io["gates"][:, :, tb * P:(tb + 1) * P].rearrange("j i t -> i j t"),
                             reg(GSTG + (tb % 2) * 16384, 16384).rearrange("p (j t) -> p j t", j=P))\
                  .then_inc(S[f"g_stored{tb % 2}"], 16)
            sp.wait_ge(S["g_stored0"], S.base("g_stored0") + 32)
            sp.wait_ge(S["g_stored1"], S.base("g_stored1") + 32)
            load_gates(None)
            load_up(None)
            with sp.Fori(1, EROUNDS) as i:
                load_down(i)
                load_gates(i)
                load_up(i)
            sp.wait_ge(S["e_y"], S.base("e_y") + EROUNDS * 8)
            load_split(sp, ("in2", "r2", "ogla"))
            with sp.Fori(0, 8) as i:
                sp.wait_ge(S["s5_K"], S.base("s5_K") + i * 2 + 2)
                for s in range(SB):
                    q = SB - 1 - s
                    sp.dma_start(
                        A[q * S5H:(q + 1) * S5H, TT_:TT_ + 1024].rearrange("p (g m) -> p g m", g=GP)[:, :, s * S5H:P],
                        A[0:S5H, KALL:KALL + 1024].rearrange("p (g m) -> p g m", g=GP)[:, :, 0:P - s * S5H])\
                        .then_inc(S["T_in"], 16)
            load_split(sp, ("glu", "out2", "ff1a", "ff2a", "ff1b", "ff2b"))

        @block.gpsimd
        def _(pool):
            def alone(sem, value):
                pool.wait_ge(S["small_in"], 48)
                pool.wait_ge(S[sem], S.base(sem) + value)

            pool.dma_start(cst[:, :], io["consts"]).then_inc(S["small_in"], 16)
            pool.dma_start(par[:, :], io["params"]).then_inc(S["small_in"], 16)
            pool.dma_start(reg(CACT, D), io["c"].broadcast_to([P, D])).then_inc(S["c_in"], 16)
            pool.dma_start(w16[:, :], io["w16"]).then_inc(S["small_in"], 16)
            pool.dma_start(reg(X, KT * T).rearrange("p (k t) -> p k t", k=KT), io["xT"].rearrange("(k p) t -> p k t", p=P))\
                .then_inc(S["x_in"], 16)
            for m in range(8):
                pool.dma_start(reg(ADA + m * 1024, 1024), io["w_ada"][m]).then_inc(S[f"ada_in{m}"], 16)
            with pool.Fori(1, 6) as i:
                for m in range(8):
                    alone("mod_done", i * 8 + (m - 7))
                    pool.dma_start(reg(ADA + m * 1024, 1024), io["w_ada"][bass.ds(i * 8 + m, 1)]
                                   .rearrange("o p n -> (o p) n")).then_inc(S[f"ada_in{m}"], 16)
            pool.wait_ge(S["mod_done"], S.base("mod_done") + 48)
            pool.dma_start(reg(SEL, 2048, 16), io["sel"]).then_inc(S["sel_in"], 16)
            pool.dma_start(small[0:16, 320:322], io["dtal"]).then_inc(S["sel_in"], 16)
            pool.dma_start(reg(PWT, 512).rearrange("p (g d) -> p g d", g=4), io["pool_w"].rearrange("g c d -> c g d"))\
                .then_inc(S["poolw_in"], 16)

            pool.wait_ge(S["h2_ready"], S.base("h2_ready") + 8)
            pool.dma_start(reg(KEYS, 2048), io["keys"]).then_inc(S["keys_in"], 16)
            pool.dma_start(io["spill"], reg(X, KT * T)).then_inc(S["spilled"], 16)
            with pool.Fori(0, 128 // GB) as i:
                for u_ in range(GB):
                    pool.wait_ge(S["b_hot"], S.base("b_hot") + i * GB + (u_ + 1))
                    b3 = reg(OB + u_ * 512, 512).rearrange("p (t i) -> p t i", t=4)
                    nc.gpsimd.tensor_tensor(b3, b3, bc(A[:, bass.ds(i * (4 * GB) + (GT + 4 * u_), 4)].unsqueeze(2), [P, 4, P]),
                                            ALU.mult).then_inc(S["b_gated"], 1)
            pool.wait_ge(S["g_mm"], S.base("g_mm") + GB + 128)
            pool.wait_ge(S["spilled"], S.base("spilled") + 16)
            pool.dma_start(reg(X, KT * T), io["spill"]).then_inc(S["unspilled"], 16)

            def low(raw, hi, lo, ready, done, i, r):
                pool.wait_ge(S[ready], S.base(ready) + i * ER + (r + 1))
                nc.gpsimd.tensor_tensor(rr(lo, 1024), reg(raw, 1024), rr(hi, 1024).bitcast(F32), ALU.subtract)\
                    .then_inc(S[done], 1)
            with pool.Fori(0, EROUNDS) as i:
                for kind, r in SPLIT_ORDER:
                    if kind == "d":
                        low(RING + r * 1024, DHI + (r % 2) * 1024, DLO + (r % 2) * 1024, "d_hi", "d_lo", i, r)
                    else:
                        low(RING + 4096 + r * 1024, UHI + r * 1024, ULO + r * 1024, "u_hi", "u_lo", i, r)

            pool.wait_ge(S["xf_ready"], S.base("xf_ready") + 8)
            pool.dma_start(A[:, X:X + XW].rearrange("p (k t) -> p k t", k=KT)[:, :, 0:META],
                           io["metaT"].rearrange("(k p) t -> p k t", p=P)).then_inc(S["meta_in"], 16)
            pool.dma_start(reg(DEC + 40, 512, 16), io["w_gate_up"]).then_inc(S["gate_in"], 16)

            def lows(q, n):
                def one(i, q):
                    hi, lo = hi_lo(q)
                    pool.wait_ge(S["l_hi"], S.base("l_hi") + rounds(i, NSLOT) + (q + 1))
                    nc.gpsimd.tensor_tensor(rr(lo, 1024, "l"), reg(RING + q % NSLOT * SLOT, 1024),
                                            rr(hi, 1024, "l").bitcast(F32), ALU.subtract).then_inc(S["l_lo"], 1)
                if n >= NSLOT:
                    with pool.Fori(0, n // NSLOT) as i:
                        for s in range(NSLOT):
                            one(i, q + s)
                for s in range(n // NSLOT * NSLOT, n):
                    one(None, q + s)
            lows(su["in2"], 34)
            pool.wait_ge(S["bank_free"], S.base("bank_free") + 4 + tiles["in2"] + 24)
            pool.dma_start(io["u_d"].rearrange("t p x -> p t x"),
                           reg(PU, 8 * T2).rearrange("p (t x) -> p t x", t=8)).then_inc(S["u_out"], 16)
            pool.wait_ge(S["u_out"], S.base("u_out") + 16)
            pool.wait_ge(S["o_set"], S.base("o_set") + 9)
            ud = io["u_d"].rearrange("t (m h) (s c) -> s h (t m) c", h=S5H, s=SB)
            for s in range(SB):
                q = SB - 1 - s
                pool.dma_start(A[q * S5H:(q + 1) * S5H, UALL:UALL + S5G * NB].rearrange("p (g c) -> p g c", g=S5G),
                               ud[s]).then_inc(S["uall_in"], 16)
            lows(su["r2"] + 2, 22)
            pool.wait_ge(S["ogla_out"], S.base("ogla_out") + 1)
            pool.dma_start(reg(S5P, 4096), io["s5bc"]).then_inc(S["s5p_in"], 16)
            pool.dma_start(reg(S5A, 192), io["s5a"]).then_inc(S["s5p_in"], 16)
            pool.wait_ge(S["s5_y"], S.base("s5_y") + 8)
            yd = io["y_d"].rearrange("t (m h) (s c) -> s h (t m) c", h=S5H, s=SB)
            for s in range(SB):
                pool.dma_start(yd[s], A[s * S5H:(s + 1) * S5H, YALL:YALL + S5G * NB]
                               .rearrange("p (g c) -> p g c", g=S5G)).then_inc(S["y_out"], 16)
            pool.wait_ge(S["y_out"], S.base("y_out") + 16 * SB)
            pool.dma_start(reg(Y8, 8 * T2).rearrange("p (t x) -> p t x", t=8),
                           io["y_d"].rearrange("t p x -> p t x")).then_inc(S["y8_in"], 16)
            lows(su["glu"], SPLITS - su["glu"])
            pool.wait_ge(S["fin"], S.base("fin") + 1)
            pool.dma_start(io["out"].rearrange("(k p) t -> p k t", p=P),
                           A[:, X:X + XW].rearrange("p (k t) -> p k t", k=KT)[:, :, META:T2]).then_inc(S["stored"], 16)
            pool.wait_ge(S["stored"], S.base("stored") + 16)

        @block.scalar
        def _(act):
            tn = Turn(act, S, "act_own")
            do, wait = tn.do, tn.wait
            sc = nc.scalar

            def act_(out, in_, f, sem=None, **kw):
                do(sc.activation(out, in_, f, **kw), sem)

            def norm_root(out, src_bank, sem, scale=1.0 / D):
                act_(out, src_bank, ACT.Sqrt, sem, scale=scale, bias=EPS)

            wait("small_in", 48)
            wait("c_in", 16)
            act_(reg(CACT, D), reg(CACT, D), ACT.Silu, "cact")
            wait("x_in", 16)
            act_(reg(H, KT * T), reg(X, KT * T), ACT.Square, "sq1")
            wait("ss1", 1)
            norm_root(RS[:, 0:T], bank(7), "rt1")

            wait("h_ready", 8)
            wait("pads", 1)
            wait("dt_mm", 1)
            act_(A[0:16, DTB:DTB + T], bank(7, 512, 16), ACT.Copy, "dt_raw")
            ev(tn, "in", 0)
            evacuate(tn, "in", 0, 12, lambda j, i: act_(
                A[:, bass.ds(i * (4 * XRW) + (XRAW + j * XRW + 4), T)], bank(2 * j), ACT.Copy, "bank_free"))
            evacuate(tn, "in", 12, 8, lambda j, i: act_(
                A[:, bass.ds(i * (4 * T) + (Z + j * T), T)], bank(2 * j), ACT.Silu, "bank_free"))
            for m in range(12):
                wait("conv_acc", m + 1)
                act_(reg(CONV + m * T, T), reg(CONV + m * T, T), ACT.Silu, "conv_out", bias=pr("conv_b", m))
            wait("mod_done", 48)
            evacuate(tn, "in", 20, 4, lambda j, i: act_(
                A[:, bass.ds(i * 0 + (POOLU + j * PUW + 16), T)], bank(2 * j), ACT.Copy, "bank_free"))

            wait("dt_x", 1)
            act_(A[0:16, DTB + T:DTB + 2 * T], A[0:16, DTB:DTB + T], ACT.Abs)
            act_(A[0:16, DTB + T:DTB + 2 * T], A[0:16, DTB + T:DTB + 2 * T], ACT.Exp, scale=-1.0)
            act_(small[0:16, 323:324], small[0:16, 321:322], ACT.Exp, "dt_e")

            wait("acol_set", 1)
            act_(eacs, acol, ACT.Exp, "eacs")
            act_(cdec, aend, ACT.Exp, "cdec")
            for c in range(3):
                wait("dte_x", c + 1)
                act_(dtecol, dtecol, ACT.Exp, "dte")
            wait("btok_mm", 2)
            act_(reg(BTOK, 512), bank(4), ACT.Copy, "btok")
            act_(reg(BTOK + 512, 512), bank(5), ACT.Copy, "btok")
            for h in range(HEADS):
                wait("seg", h + 1)
                m = reg(MB_ + (h % 2) * T, T)
                act_(m, m, ACT.Relu, scale=-1.0)
                act_(m, m, ACT.Exp, "dec_e", scale=-1.0)
            wait("yt_ready", 8)
            act_(reg(XRAW, 8 * T), reg(YMIX + 4 * T, 8 * T), ACT.Square, "sq2")
            wait("ss2", 1)
            norm_root(RS[:, 0:T], bank(7), "rt2")

            wait("x1_ready", 1)
            act_(reg(H, KT * T), reg(X, KT * T), ACT.Square, "sq3")
            wait("ss3", 1)
            norm_root(RS[:, 0:T], bank(7), "rt3")
            ev(tn, "query", 0)
            evacuate(tn, "query", 0, 16, lambda j, i: act_(
                A[:, bass.ds(i * (4 * T) + (QT + j * T), T)], bank(2 * j), ACT.Copy, "bank_free"))

            with tn.loop(4, act_own=1, sc_set=4, gate_e=1, slots_T=2) as i:
                wait("sc_mm", i + 1)
                wait("sc_free", i)
                for b in range(4):
                    act_(reg(SC + b * 512, 512), bank(b), ACT.Copy, "sc_set")
                wait("gate_x", i + 1)
                act_(reg(SELX + 256, 128), reg(SELX + 256, 128), ACT.Exp, "gate_e")
                wait("slots_mm", i + 1)
                wait("spilled", 16)
                act_(A[:, bass.ds(i * P + I1T, P)], bank(4)[:, 0:P], ACT.Copy)
                act_(A[:, bass.ds(i * P + I2T, P)], bank(4)[:, P:2 * P], ACT.Copy, "slots_T")
                act_(A[:, bass.ds(i * P + GT, P)], bank(4)[:, 2 * P:3 * P], ACT.Copy, "slots_T")

            tn.base["g_evac"] = GB
            for tb in range(4):
                if tb >= 2:
                    wait(f"g_stored{tb % 2}", 16)
                with tn.loop(32 // GB, g_evac=GB) as i:
                    for u_ in range(GB):
                        wait("g_mm", i * GB + (GB + tb * 32 + u_ + 1))
                        stg = reg(GSTG + (tb % 2) * 16384, 16384).rearrange("p (j t) -> p t j", j=P)
                        act_(stg[:, bass.ds(i * (4 * GB) + 4 * u_, 4), :],
                             bank(u_).rearrange("p (t j) -> p t j", t=4), ACT.Copy, "g_evac")

            wait("g_stored0", 32)
            wait("g_stored1", 32)
            with tn.loop(EROUNDS, e_g=ER, d_hi=ER, u_hi=ER) as i:
                def gelu(r):
                    wait("e_u", i * ER + (r + 1))
                    wait("e_w", i * ER)
                    act_(reg(ACTB + r * T, T), bank(r), ACT.Gelu, "e_g")
                n = 0
                for kind, r in SPLIT_ORDER:
                    if kind == "d":
                        wait(f"down_in{r}", i * 16 + 16)
                        wait("e_u", i * ER + (r - 1))
                        act_(rr(DHI + (r % 2) * 1024, 1024), reg(RING + r * 1024, 1024), ACT.Copy, "d_hi")
                    else:
                        wait(f"up_in{r}", i * 16 + 16)
                        wait("e_y", i * 8)
                        act_(rr(UHI + r * 1024, 1024), reg(RING + 4096 + r * 1024, 1024), ACT.Copy, "u_hi")
                        if r:
                            gelu(r - 1)
                gelu(3)

            wait("xf_ready", 8)
            act_(reg(H, KT * T), reg(YACC, KT * T), ACT.Square, "sq4")
            wait("ss4", 1)
            norm_root(RS[:, 0:T], bank(7), "rt4")

            for v_ in range(2):
                weights_hi(tn, "in2", None, v_)
            wait("h2in", 8)
            wait("meta_in", 16)
            act_(reg(XN, XW), reg(X, XW), ACT.Square, "sq5")
            wait("ss5", 1)
            norm_root(halves(RS[:, 0:T2]), pair(3), "rt5")
            wait("alow_mm", 1)
            act_(halves(A[0:16, EE:EE + T2]), pair(3, 16), ACT.Copy, "alow")
            E4, L4 = reg(EE, 4 * T2), reg(LA, 4 * T2)
            wait("gate_lin", 4)
            act_(E4, L4, ACT.Abs)
            act_(E4, E4, ACT.Exp, scale=-1.0)
            act_(E4, E4, ACT.Ln, "ln_e", bias=1.0)
            ev(tn, "in2", 0)
            evacuate(tn, "in2", 0, 16, lambda j, i: act_(
                halves(A[:, bass.ds(i * (4 * T2) + (PROJ + j * T2), T2)]), pair(j), ACT.Copy, "bank_free"), True)
            wait("gd", 1)
            act_(E4, L4, ACT.Exp, "ge1")
            wait("gq", 1)
            act_(E4, L4, ACT.Exp, "ge2", scale=-1.0)
            wait("gq", 2)
            act_(E4, reg(DD, 4 * T2), ACT.Exp, "ge3")
            wait("gq", 3)
            act_(E4, L4, ACT.Exp)
            act_(reg(DEC, 36), reg(DEC, 36), ACT.Exp, "ge4")

            def ev_u(j, i):
                dst = A[:, bass.ds(i * (4 * T2) + (PU + j * T2), T2)].rearrange("p (s c) -> p c s", s=SB)
                for h in range(2):
                    src = bank(2 * j + h, T2 // 2).rearrange("p (c s) -> p c s", s=SB)
                    act_(dst[:, h * NB // 2:(h + 1) * NB // 2, :], src, ACT.Copy, "bank_free" if h else None)
            with tn.loop(2, bank_free=4, act_own=4, l_hi=4) as i:
                for j in range(4):
                    wait("unit_done", i * 4 + (units["in2"] + 16 + j + 1))
                    ev_u(j, i)
                    weights_hi(tn, "in2", i, 16 + j + 2)
            evacuate(tn, "in2", 24, 8, lambda j, i: act_(
                halves(A[:, bass.ds(i * (4 * T2) + (PZG + j * T2), T2)]), pair(j), ACT.Sigmoid, "bank_free"), True)

            for c, (t0, L) in enumerate(GCH):
                wait("gla_tr", c + 1)
                act_(reg(VTOK, 1024, L), PS[0:L, 512:1536], ACT.Copy, "vtok")
                wait("gla_o", c + 1)
                o = A[:, PVV:PVV + 8 * T2].rearrange("p (m t) -> p m t", m=8)[:, :, t0:t0 + L]
                act_(o, bank(4).rearrange("p (m t) -> p m t", m=8)[:, :, 0:L], ACT.Copy, "o_set")
            act_(reg(QIN, 8 * T2), reg(PVV, 8 * T2), ACT.Square, "sq6")
            wait("ss6", 4)
            for h in range(GLH):
                norm_root(halves(reg(LA + h * T2, T2)), pair(h), "rt6", scale=1.0 / DV)
            ev(tn, "r2", 0)
            evacuate(tn, "r2", 0, 8, lambda j, i: act_(
                halves(A[:, bass.ds(i * (4 * T2) + (PZS + j * T2), T2)]), pair(j), ACT.Sigmoid, "bank_free"), True)
            evacuate(tn, "r2", 8, 8, lambda j, i: act_(
                halves(A[:, bass.ds(i * (4 * T2) + (RR + j * T2), T2)]), pair(j), ACT.Silu, "bank_free"), True)
            for v_ in range(2, 8):
                weights_hi(tn, "ogla", None, v_)

            wait("s5p_in", 32)
            act_(reg(DT5, 64), reg(S5A + 128, 64), ACT.Exp, "s5_e")
            wait("s5_x", 1)
            act_(reg(MG1, 64), reg(AR5, 64), ACT.Exp, "s5_e")
            act_(reg(MG8, 64), reg(AR5, 64), ACT.Exp, "s5_e", scale=float(SB))
            act_(reg(SN1, 64), reg(SN1, 64), ACT.Sin, "s5_e")
            act_(reg(CS1, 64), reg(CS1, 64), ACT.Sin, "s5_e")
            wait("s5_x", 2)
            act_(reg(LMG, 576), reg(LMG, 576), ACT.Exp, "s5_e")
            act_(reg(LR, 576), reg(LR, 576), ACT.Sin, "s5_e")
            act_(reg(LI, 576), reg(LI, 576), ACT.Sin, "s5_e")
            def s5_W():
                act_(reg(WW, 512), bank(0), ACT.Copy, "s5_W")
                act_(reg(WW + 512, 512), bank(1), ACT.Copy, "s5_W")

            def s5_part(i, u, more):
                wait("s5_Smm", s5_count(i, u, 1, 1))
                act_(halves(reg(SS, 528)), pair(3), ACT.Copy, "s5_S")
                wait("s5_Kmm", s5_count(i, u, 1, 1))
                wait("T_in", s5_count(i, u, 16 * SB))
                act_(reg(KALL, 512, 16), bank(2, 512, 16), ACT.Copy, "s5_K")
                act_(reg(KALL + 512, 512, 16), bank(3, 512, 16), ACT.Copy, "s5_K")
                wait("s5_ang", s5_count(i, u, 1, 1))
                act_(reg(SIN, 528), reg(ANG, 528), ACT.Sin, "s5_cs")
                act_(reg(COS, 528), reg(ANG2, 528), ACT.Sin, "s5_cs")
                if more:
                    wait("s5_Wmm", s5_count(i, u, 1, 2))
                    s5_W()
                wait("s5_ymm", s5_count(i, u, 1, 1))
                act_(halves(s5_at(i, u, YALL, 528)), pair(2), ACT.Copy, "s5_y")

            wait("s5_Wmm", 1)
            s5_W()
            with tn.loop(3, s5_cs=4, s5_W=4, s5_K=4, s5_S=2, s5_y=2) as i:
                s5_part(i, 0, True)
                s5_part(i, 1, True)
            s5_part(None, 6, True)
            s5_part(None, 7, False)
            for v_ in range(2):
                weights_hi(tn, "glu", None, v_)
            for m in range(8):
                wait("s5_out", m + 1)
                act_(reg(PU + m * T2, T2).rearrange("p (c s) -> p s c", s=SB),
                     reg(Y8 + m * T2, T2).rearrange("p (s c) -> p s c", s=SB), ACT.Gelu_apprx_tanh, "gs")
            ev(tn, "glu", 0)
            wait("gs", 8)
            evacuate(tn, "glu", 0, 8, lambda j, i: act_(
                halves(A[:, bass.ds(i * (4 * T2) + (YALL + j * T2), T2)]), pair(j), ACT.Identity, "bank_free",
                bias=par[:, bass.ds(i * 4 + (PAR["b_glu"][0] + j), 1)]), True)
            evacuate(tn, "glu", 8, 8, lambda j, i: act_(
                halves(A[:, bass.ds(i * (4 * T2) + (Y8 + j * T2), T2)]), pair(j), ACT.Sigmoid, "bank_free",
                bias=par[:, bass.ds(i * 4 + (PAR["b_glu"][0] + 8 + j), 1)]), True)
            ev(tn, "out2", 0)
            evacuate(tn, "out2", 0, 8, lambda j, i: act_(
                halves(A[:, bass.ds(i * (4 * T2) + (MO + j * T2), T2)]), pair(j), ACT.Copy, "bank_free"), True)
            act_(reg(XN, XW), reg(MO, XW), ACT.Square, "sq7")
            wait("ss7", 1)
            norm_root(halves(RS[:, 0:T2]), pair(3), "rt7")
            wait("h_mid", 8)
            act_(reg(XN, XW), reg(X, XW), ACT.Square, "sq8")
            wait("ss8", 1)
            norm_root(halves(RS[:, 0:T2]), pair(3), "rt8")
            def hidden(name, n=16):
                with tn.loop(n // 4, bank_free=4, l_hi=4) as i:
                    for j in range(4):
                        wait("unit_done", i * 4 + (units[name] + j + 1))
                        act_(halves(A[:, bass.ds(i * T2 + (FF + j * 4 * T2), T2)]), pair(j), ACT.Relu, "bank_free")
                        weights_hi(tn, name, i, j + 2)

            ev(tn, "ff1a", 0)
            hidden("ff1a")
            ev(tn, "ff2a", 0)
            with tn.loop(2, bank_free=4, l_hi=8) as i:
                for j in range(4):
                    wait("unit_done", i * 8 + (units["ff2a"] + 2 * j + 1))
                    weights_hi(tn, "ff2a", i, 2 * j + 2)
                    wait("unit_done", i * 8 + (units["ff2a"] + 2 * j + 2))
                    act_(halves(A[:, bass.ds(i * (4 * T2) + (MO + j * T2), T2)]), pair(j), ACT.Copy, "bank_free")
                    weights_hi(tn, "ff2a", i, 2 * j + 3)
            ev(tn, "ff1b", 0)
            hidden("ff1b")
            with tn.loop(1, l_hi=8) as i:
                for v_ in range(8):
                    weights_hi(tn, "ff2b", i, v_ + 2)
            for v_ in range(10, 16):
                weights_hi(tn, "ff2b", None, v_)
            wait("mo_sum", 1)
            act_(reg(XN, XW), reg(MO, XW), ACT.Square, "sq9")
            wait("ss9", 1)
            norm_root(halves(RS[:, 0:T2]), pair(3), "rt9")

        @block.tensor
        def _(pe):
            mm = nc.tensor.matmul

            def w_(sem, v):
                pe.wait_ge(S[sem], S.base(sem) + v)

            def tok(off, w=T):
                return lambda k, c0, cw: A[:, off + k * w + c0:off + k * w + c0 + cw]

            def sumsq(src, n, w, out, sem, start=True):
                cols = [(0, w)] if w <= 512 else [(0, w // 2), (w // 2, w // 2)]
                for h, (c0, cw) in enumerate(cols):
                    for k in range(n):
                        last = mm(bank(out + h, cw), ones, reg(src + k * w + c0, cw), start=(k == 0), stop=(k == n - 1))
                last.then_inc(S[sem], 1)

            def drained(name):
                w_("bank_free", 4 + tiles[name] + STAGES[name][0])

            def T_(out, in_, n):
                return nc.tensor.transpose(out, in_, cst[0:n, 0:n])

            w_("small_in", 48)

            def ssd_diag(h):
                w_("mdec", h + 1)
                w_("xdt", 8)
                for c in range(NCH):
                    last = mm(bank(2 + c)[:, (h % 8) * HD:(h % 8 + 1) * HD], reg(MB_ + (h % 2) * T + c * CH, CH),
                              reg(XDT + c * 1024 + h * HD, HD), start=True, stop=True)
                last.then_inc(S["diag_mm"], 1)

            w_("sq1", 1)
            sumsq(H, 8, T, 7, "ss1")
            w_("h_ready", 8)
            for k in range(KT):
                last = mm(bank(7, 512, 16), w16[:, k * 16:(k + 1) * 16], reg(H + k * T, T), start=(k == 0), stop=(k == 7))
            last.then_inc(S["dt_mm"], 1)
            stage_products(pe, "in", tok(H))
            drained("in")

            w_("acs", 1)
            for c in range(NCH):
                T_(bank(6)[:, c * 16:(c + 1) * 16], RS[0:16, c * CH:(c + 1) * CH], 16)
                T_(bank(6)[:, 64 + c * 16:80 + c * 16], A[0:16, DTB + 2 * T + c * CH:DTB + 2 * T + (c + 1) * CH], 16)
            w_("aend_x", 1)
            mm(bank(6)[:, 128:192], cst[0:16, CONST["ones"][0]:CONST["ones"][0] + P], small[0:16, 0:64], start=True,
               stop=True).then_inc(S["acol_mm"], 1)
            w_("conv_out", 12)
            for g in range(2):
                for c in range(NCH):
                    last = T_(bank(4 + g)[:, c * P:(c + 1) * P], reg(CONV + (8 + g) * T + c * CH, CH), P)
                last.then_inc(S["btok_mm"], 1)
            for g in range(2):
                for c in range(NCH):
                    last = mm(bank(2 + g)[:, c * P:(c + 1) * P], reg(CONV + (8 + g) * T + c * CH, CH),
                              reg(CONV + (10 + g) * T + c * CH, CH), start=True, stop=True)
                last.then_inc(S["cb_mm"], 1)
            for c in range(NCH):
                w_("xdt", 2 * c)
                for m in range(8):
                    last = T_(bank(m // 4)[:, (m % 4) * P:(m % 4 + 1) * P], reg(CONV + m * T + c * CH, CH), P)
                    if m % 4 == 3:
                        last.then_inc(S["xs_mm"], 1)
            w_("btok", 2)
            for c in range(3):
                w_("xdte", c + 1)
                w_("hst", 2 * c)
                for g in range(2):
                    mm(bank(4 + g), reg(BTOK + g * 512 + c * P, P), reg(XDTE + c * 1024 + g * 512, 512), start=True,
                       stop=True).then_inc(S["st_mm"], 1)
            w_("hst", 6)
            w_("cbm", 2)
            w_("sel_in", 32)
            for g in range(2):
                w_("yt_ready", 4 * g)
                for h in range(8 * g, 8 * g + 8):
                    if h >= 2:
                        w_("seg", h - 1)
                    mm(bank(h % 2), A[0:16, SEL + h * P:SEL + (h + 1) * P], RS[0:16, 0:T], start=True,
                       stop=True).then_inc(S["row_mm"], 1)
                    if h % 8:
                        ssd_diag(h - 1)
                ssd_diag(8 * g + 7)
                for c in range(1, NCH):
                    w_("yoff", g * 3 + c - 1)
                    mm(bank(6), reg(CONV + (10 + g) * T + c * CH, CH), reg(HST + (c - 1) * 1024 + g * 512, 512),
                       start=True, stop=True).then_inc(S["yoff_mm"], 1)
                for m in range(4):
                    w_("ytok", 4 * (g + 1))
                    if m >= 2:
                        w_("yt_ready", 4 * g + m - 1)
                    for c in range(NCH):
                        last = T_(bank(m % 2)[:, c * P:(c + 1) * P], reg(YTOK + c * 512 + m * P, P), P)
                    last.then_inc(S["yt_mm"], 1)
            w_("sq2", 1)
            sumsq(XRAW, 8, T, 7, "ss2")
            w_("poolw_in", 16)
            w_("pooled", 4)
            w_("yt_ready", 8)
            for g in range(POOL_G):
                if g >= 2:
                    w_("pool_out", g - 1)
                mm(bank(2 * (g % 2)), reg(PWT + g * P, P), reg(YMIX + g * T, T), start=True, stop=True)                    .then_inc(S["pool_mm"], 1)
            w_("pool_out", 4)
            w_("ymix", 8)
            stage_products(pe, "out", tok(YMIX))
            w_("sq3", 1)
            sumsq(H, 8, T, 7, "ss3")
            w_("h2_ready", 8)
            stage_products(pe, "query", tok(H))
            drained("query")

            w_("keys_in", 16)

            def scores(tb):
                w_("sc_set", 4 * tb)
                for hh in range(16):
                    last = mm(bank(hh // 4)[:, (hh % 4) * P:(hh % 4 + 1) * P], reg(QT + hh * T + tb * P, P),
                              reg(KEYS + hh * P, P), start=True, stop=True)
                last.then_inc(S["sc_mm"], 1)

            scores(0)
            for tb in range(4):
                if tb < 3:
                    scores(tb + 1)
                w_("sel", tb + 1)
                w_("slots_T", 2 * tb)
                for n in range(3):
                    last = T_(bank(4)[:, n * P:(n + 1) * P], reg(SELX + n * P, P), P)
                last.then_inc(S["slots_mm"], 1)
            w_("slots_T", 8)
            with pe.Fori(0, 128 // GB) as i:
                for u_ in range(GB):
                    pe.wait_ge(S["b_gated"], S.base("b_gated") + i * GB + (u_ + 1))
                    pe.wait_ge(S["g_evac"], S.base("g_evac") + i * GB + (u_ + 1))
                    for t in range(4):
                        last = mm(bank(u_)[:, t * P:(t + 1) * P], reg(OA + u_ * 512 + t * P, P),
                                  reg(OB + u_ * 512 + t * P, P), start=True, stop=True)
                    last.then_inc(S["g_mm"], 1)
            w_("g_evac", 128 + GB)

            w_("hsplit", 1)
            with pe.Fori(0, EROUNDS) as i:
                for r in range(ER):
                    w_("d_lo", i * ER + (r + 1))
                    w_("e_w", i * ER)
                    hi, lo = DHI + (r % 2) * 1024, DLO + (r % 2) * 1024
                    for k in range(KT):
                        for n, (a_, b_) in enumerate(((hi, HHI), (hi, H), (lo, HHI))):
                            last = mm(bank(r), rr(a_ + k * P, P), rr(b_ + k * T, T), start=(k == 0 and n == 0),
                                      stop=(k == 7 and n == 2))
                    last.then_inc(S["e_u"], 1)
                for d in range(KT):
                    w_("e_acc", i * 8 + (d + 1))
                    for r in range(ER):
                        if d == 0:
                            w_("u_lo", i * ER + (r + 1))
                            w_("e_w", i * ER + (r + 1))
                        for n, (a_, b_) in enumerate(((UHI, WHI), (UHI, WLO), (ULO, WHI))):
                            last = mm(bank(4 + d % 4), rr(a_ + r * 1024 + d * P, P), rr(b_ + r * T, T),
                                      start=(r == 0 and n == 0), stop=(r == ER - 1 and n == 2))
                    last.then_inc(S["e_y"], 1)

            w_("sq4", 1)
            w_("e_acc", 4 + 8 * EROUNDS)
            sumsq(H, 8, T, 7, "ss4")

            w_("sq5", 1)
            sumsq(XN, 8, T2, 6, "ss5")
            w_("xn_ready", 8)
            for h in range(2):
                for k in range(KT):
                    last = mm(bank(6 + h, 264, 16), w16[:, 128 + k * 16:144 + k * 16],
                              reg(XN + k * T2 + h * 264, 264), start=(k == 0), stop=(k == 7))
            last.then_inc(S["alow_mm"], 1)
            w_("alow", 1)
            w_("gate_in", 16)
            for m in range(GLH):
                for h in range(2):
                    last = mm(bank(2 * m + h, 264), A[0:16, DEC + 40 + m * P:DEC + 40 + (m + 1) * P],
                              A[0:16, EE + h * 264:EE + (h + 1) * 264], start=True, stop=True)
                last.then_inc(S["gate_mm"], 1)
            w_("gate_lin", 4)
            w_("xn_split", 1)
            xl = lambda k: rr(XN + k * T2, T2, "l")
            split_products(pe, "in2", lambda k: (rr(XH1 + k * T2, T2, "p"), xl(k)))
            drained("in2")

            w_("gq", 4)
            for c, (t0, L) in enumerate(GCH):
                w_("ktok", c)
                w_("vtok", c)
                for h in range(GLH):
                    T_(PS[0:L, h * P:(h + 1) * P], reg(PK + h * T2 + t0, L), P)
                for m in range(8):
                    last = T_(PS[0:L, 512 + m * P:512 + (m + 1) * P], reg(PVV + m * T2 + t0, L), P)
                last.then_inc(S["gla_tr"], 1)
                for h in range(GLH):
                    last = mm(PS[0:L, 1536 + h * GC:1536 + h * GC + L], reg(KIN + h * T2 + t0, L),
                              reg(QIN + h * T2 + t0, L), start=True, stop=True)
                last.then_inc(S["gla_sc"], 1)
                w_("sm", c + 1)
                w_("vtok", c + 1)
                w_("ktok", c + 1)
                w_("o_set", c)
                w_("st", 4 * c)
                for m in range(8):
                    h = m // 2
                    o = bank(4)[:, m * GC:m * GC + L]
                    last = mm(o, reg(VTOK + m * P, P, L), reg(SM + h * GC, L, L), start=True, stop=(c == 0))
                    if c:
                        last = mm(o, reg(ST + m * P, P), reg(PQ + h * T2 + t0, L), start=False, stop=True)
                last.then_inc(S["gla_o"], 1)
                if c < len(GCH) - 1:
                    for h in range(GLH):
                        last = mm(PS[:, 3072 + h * DV:3072 + (h + 1) * DV], reg(KTOK + h * P, P, L),
                                  reg(VTOK + h * DV, DV, L), start=True, stop=True)
                    last.then_inc(S["gla_st"], 1)
            w_("sq6", 1)
            w_("st", 32)
            for h in range(GLH):
                sumsq(QIN + 2 * h * T2, 2, T2, 2 * h, "ss6")
            w_("rt6", 4)
            w_("xn_moved", 1)
            xh2 = lambda k: rr(XH2 + k * T2, T2, "p")
            split_products(pe, "r2", lambda k: (xh2(k), xl(k)))
            w_("o_split", 1)
            split_products(pe, "ogla", lambda k: (xh2(k), rr(PVV + k * T2, T2, "p")))
            drained("ogla")

            swap = con("swap")
            def s5_W():
                for g in range(GP):
                    last = T_(bank(g // 4)[:, (g % 4) * P:(g % 4 + 1) * P], reg(WT + g * P, P), P)
                last.then_inc(S["s5_Wmm"], 1)

            def s5_part(i, u, more):
                pe.wait_ge(S["s5_W"], S.base("s5_W") + s5_count(i, u, 2, 2))
                for g in range(GP):
                    uc = s5_at(i, u, UALL, GP * NB)[:, g * NB:(g + 1) * NB]
                    last = mm(bank(6 + g // 4)[:, (g % 4) * NB:(g % 4 + 1) * NB], reg(WW + g * P, P), uc,
                              start=True, stop=True)
                last.then_inc(S["s5_Smm"], 1)
                pe.wait_ge(S["s5_S"], S.base("s5_S") + s5_count(i, u, 1, 1))
                for h in range(2):
                    last = mm(bank(6 + h, 264), swap, reg(SS + h * 264, 264), start=True, stop=True)
                last.then_inc(S["s5_Zmm"], 1)
                v9 = (V9A, V9B)[u % 2]
                pe.wait_ge(S["s5_V9"], S.base("s5_V9") + s5_count(i, u, 1, 1))
                for g in range(GP):
                    last = mm(bank(2 + g // 4, 512, 16)[:, (g % 4) * P:(g % 4 + 1) * P], reg(BBP + g * 16, 16),
                              reg(v9 + g * 144, P), start=True, stop=True)
                last.then_inc(S["s5_Kmm"], 1)
                pe.wait_ge(S["s5_w"], S.base("s5_w") + s5_count(i, u, 1, 1))
                for h in range(2):
                    last = mm(bank(6 + h, 264), swap, reg(S2 + h * 264, 264), start=True, stop=True)
                last.then_inc(S["s5_Zmm"], 1)
                if more:
                    pe.wait_ge(S["s5_WT"], S.base("s5_WT") + s5_count(i, u, 1, 2))
                    s5_W()
                pe.wait_ge(S["s5_y"], S.base("s5_y") + s5_count(i, u, 1))
                pe.wait_ge(S["s5_H"], S.base("s5_H") + s5_count(i, u, 1, 1))
                pe.wait_ge(S["T_in"], S.base("T_in") + s5_count(i, u, 16 * SB, 16 * SB))
                for g in range(GP):
                    o = bank(4 + g // 4)[:, (g % 4) * NB:(g % 4 + 1) * NB]
                    uc = s5_at(i, u, UALL, GP * NB)[:, g * NB:(g + 1) * NB]
                    mm(o, reg(TT_ + g * P, P), uc, start=True, stop=False)
                    last = mm(o[:, 1:NB], reg(v9 + g * 144 + 16, P), reg(SS + g * NB, NB - 1), start=False, stop=True)
                last.then_inc(S["s5_ymm"], 1)

            w_("s5_WT", 1)
            s5_W()
            w_("uall_in", 16 * SB)
            with pe.Fori(0, 3) as i:
                s5_part(i, 0, True)
                s5_part(i, 1, True)
            s5_part(None, 6, True)
            s5_part(None, 7, False)
            w_("s5_y", 8)
            w_("gs_split", 1)
            xh3 = lambda k: rr(XH3 + k * T2, T2, "l")
            split_products(pe, "glu", lambda k: (xh3(k), rr(PU + k * T2, T2, "p")))
            w_("mixed", 1)
            split_products(pe, "out2", lambda k: (xh3(k), rr(PZG + k * T2, T2, "p")))
            drained("out2")
            w_("sq7", 1)
            sumsq(XN, 8, T2, 6, "ss7")
            w_("sq8", 1)
            sumsq(XN, 8, T2, 6, "ss8")
            w_("hn_split", 1)
            for n, half in enumerate("ab"):
                split_products(pe, "ff1" + half, lambda k: (xh3(k), xl(k)))
                w_("ff_split", 16 * (n + 1))
                split_products(pe, "ff2" + half, lambda k: (rr(FFH + ff(k), T2, "f"), rr(FF + ff(k), T2, "f")))
            drained("ff2b")
            w_("sq9", 1)
            sumsq(XN, 8, T2, 6, "ss9")

        @block.vector
        def _(dve):
            tn = Turn(dve, S, "dve_own")
            do, wait = tn.do, tn.wait
            v = nc.vector

            def tt(out, a, b, op, sem=None):
                do(v.tensor_tensor(out, a, b, op), sem)

            def ts(out, a, s1, s2, op0, op1=None, sem=None):
                do(v.tensor_scalar(out, a, s1, s2, op0, op1) if op1 is not None else
                   v.tensor_scalar(out, a, s1, s2, op0), sem)

            def stt(out, a, s, b, op0, op1, sem=None):
                do(v.scalar_tensor_tensor(out, a, s, b, op0, op1), sem)

            def three(off, a, b=None):
                return reg(off, a * b).rearrange("p (a b) -> p a b", a=a)

            v.memset(tick[:, 0:1], 0.0).then_inc(S["bank_free"], 4)
            v.memset(tick[:, 1:2], 0.0).then_inc(S["g_mm"], GB)
            v.memset(tick[:, 2:3], 0.0).then_inc(S["g_evac"], GB)
            v.memset(tick[:, 3:4], 0.0).then_inc(S["e_acc"], 4)
            tn.base["e_acc"] = 4

            for m in range(12):
                do(v.memset(reg(XRAW + m * XRW, 4), 0.0), "pads" if m == 11 else None)
            wait("small_in", 48)
            wait("cact", 1)

            def mod_row(n):
                wait(f"ada_in{n % 8}", 16 * (n // 8 + 1))
                do(v.tensor_tensor_reduce(out=reg(CACT + 1024, D), in0=reg(ADA + (n % 8) * 1024, D), in1=reg(CACT, D),
                                          scale=1.0, scalar=0.0, op0=ALU.mult, op1=ALU.add,
                                          accum_out=mod[:, n:n + 1]), "mod_done")
            for n in range(16):
                mod_row(n)
            b_ada = pr("b_ada")
            tt(mod[:, 0:16], mod[:, 0:16], b_ada[:, 0:16], ALU.add)
            stt(gsc[:, 0:8], mod[:, 8:16], 1.0, pr("norm_mix"), ALU.add, ALU.mult)
            wait("rt1", 1)
            do(v.reciprocal(RS[:, 0:T], RS[:, 0:T]))
            wait("ss1", 1)

            def modulated(out, src, shift0, sem):
                for k in range(KT):
                    stt(reg(out + k * T, T), reg(src + k * T, T), gsc[:, k:k + 1], RS[:, 0:T], ALU.mult, ALU.mult,
                        FREE if k % 2 == 0 else None)
                    if k % 2 == 0:
                        continue
                    for k in (k - 1, k):
                        ts(reg(out + k * T, T), reg(out + k * T, T), mod[:, shift0 + k:shift0 + k + 1], None, ALU.add,
                           sem=sem if k == 7 else "~" + sem)
            modulated(H, X, 0, "h_ready")
            for n in range(16, 48):
                mod_row(n)
            tt(mod[:, 16:48], mod[:, 16:48], b_ada[:, 16:48], ALU.add)
            for m in range(4):
                do(v.memset(reg(POOLU + m * PUW, 16), 0.0))
            for m in range(2):
                do(v.memset(reg(PTMP + m * PUW, 16), 0.0))

            for m in range(12):
                wait("bank_free", 4 + tiles["in"] + m + 1)
                cw = PAR["conv_w"][0] + 4 * m
                src = XRAW + m * XRW + 1
                out = reg(CONV + m * T, T)
                ts(out, reg(src, T), par[:, cw:cw + 1], None, ALU.mult)
                for k in range(1, 4):
                    stt(out, reg(src + k, T), par[:, cw + k:cw + k + 1], out, ALU.mult, ALU.add,
                        "conv_acc" if k == 3 else None)

            wait("bank_free", 4 + 24)
            for g in range(POOL_G):
                u0 = POOLU + g * PUW
                cur = u0
                for n in range(g + 1):
                    nxt = PTMP + (n % 2) * PUW
                    tt(reg(nxt + 16, T), reg(cur + 16, T), reg(cur + 16 - (1 << n), T), ALU.add)
                    cur = nxt
                w = 2 << g
                y = YMIX + g * T
                ic = CONST["invcnt"][0] + g * 16
                tt(reg(y, 16), reg(cur + 16, 16), cst[:, ic:ic + 16], ALU.mult)
                ts(reg(y + 16, T - 16), reg(cur + 32, T - 16), 1.0 / w, None, ALU.mult)
                tt(reg(y, T), reg(y, T), reg(u0 + 16, T), ALU.subtract, "pooled")

            dtx, dte, dt_ = (A[0:16, DTB + n * T:DTB + (n + 1) * T] for n in range(3))
            dacs = RS[0:16, 0:T]
            wait("sel_in", 32)
            wait("dt_raw", 1)
            ts(dtx, dtx, small[0:16, 320:321], None, ALU.add, sem="dt_x")
            wait("dt_e", 1)
            ts(dt_, dte, 2.0, None, ALU.add)
            do(v.reciprocal(dt_, dt_))
            tt(dt_, dt_, dte, ALU.mult)
            tt(dte, dt_, dt_, ALU.mult)
            ts(dacs, dte, 2.0 / 17, 2.0 / 15, ALU.mult, ALU.add)
            for n in (13, 11, 9, 7, 5, 3, 1):
                tt(dacs, dacs, dte, ALU.mult)
                ts(dacs, dacs, 2.0 / n, None, ALU.add)
            tt(dacs, dacs, dt_, ALU.mult)
            stt(dt_, dtx, 0.0, dacs, ALU.max, ALU.add)
            ts(small[0:16, 324:325], small[0:16, 323:324], -1.0, None, ALU.mult)
            ts(dtx, dt_, small[0:16, 324:325], None, ALU.mult)
            do(v.tensor_tensor_scan(dacs, con("mask128", 16), dtx, 0.0, ALU.mult, ALU.add), "acs")
            ends = dacs.rearrange("p (c l) -> p c l", c=NCH)[:, :, CH - 1:CH].rearrange("p c o -> p (c o)")
            tt(small[0:16, 0:64].rearrange("p (h c) -> p h c", h=16),
               bc(cst[0:16, 0:16].unsqueeze(2), [16, 16, NCH]), bc(ends.unsqueeze(1), [16, 16, NCH]), ALU.mult, "aend_x")
            wait("acol_mm", 1)
            do(v.tensor_copy(small[:, 0:192], bank(6)[:, 0:192]), "acol_set")
            def cols(ap16, w):
                return bc(ap16.unsqueeze(2), [P, ap16.shape[1], w])
            for c in range(NCH):
                for b in range(2):
                    wait("xs_mm", 2 * c + b + 1)
                    tt(reg(XDT + c * 1024 + b * 512, 512).rearrange("p (h d) -> p h d", h=8),
                       bank(b).rearrange("p (h d) -> p h d", h=8),
                       cols(dtcol[:, c * 16 + b * 8:c * 16 + b * 8 + 8], HD), ALU.mult, "~xdt" if 2 * c + b < 7 else "xdt")
            ae = aend.rearrange("p (h c) -> p h c", h=16)
            for c in range(3):
                tt(dtecol, ae[:, :, c:c + 1].rearrange("p h c -> p (h c)"), acol[:, c * 16:(c + 1) * 16], ALU.subtract,
                   "dte_x")
                wait("dte", c + 1)
                tt(reg(XDTE + c * 1024, 1024).rearrange("p (h d) -> p h d", h=16),
                   reg(XDT + c * 1024, 1024).rearrange("p (h d) -> p h d", h=16), cols(dtecol, HD), ALU.mult, "xdte")
            for g in range(2):
                wait("cb_mm", g + 1)
                tt(three(CBM + g * 512, 4, P), bank(2 + g).rearrange("p (c l) -> p c l", c=4),
                   bc(causal.unsqueeze(1), [P, 4, P]), ALU.mult, "~cbm")
            wait("cdec", 1)
            cd = cdec.rearrange("p (h c) -> p h c", h=16)
            for c in range(3):
                for g in range(2):
                    wait("st_mm", 2 * c + g + 1)
                    hs = reg(HST + c * 1024 + g * 512, 512)
                    if c == 0:
                        do(v.tensor_copy(hs, bank(4 + g)), "hst")
                    else:
                        dk = cd[:, g * 8:(g + 1) * 8, c:c + 1].rearrange("p h c -> p (h c)")
                        tt(hs.rearrange("p (h d) -> p h d", h=8),
                           reg(HST + (c - 1) * 1024 + g * 512, 512).rearrange("p (h d) -> p h d", h=8),
                           cols(dk, HD), ALU.mult)
                        tt(hs, hs, bank(4 + g), ALU.add, "hst")
            ac3 = acol.rearrange("p (c h) -> p c h", c=4)
            wait("eacs", 1)
            for g in range(2):
                for h in range(8 * g, 8 * g + 9):
                    if h < 8 * g + 8:
                        wait("row_mm", h + 1)
                        if h >= 2:
                            wait("diag_mm", h - 1)
                        m = reg(MB_ + (h % 2) * T, T).rearrange("p (c l) -> p c l", c=4)
                        tt(m, bank(h % 2).rearrange("p (c l) -> p c l", c=4),
                           bc(ac3[:, :, h:h + 1], [P, 4, P]), ALU.subtract, "~seg")
                    if h > 8 * g:
                        wait("dec_e", h)
                        m = reg(MB_ + ((h - 1) % 2) * T, T)
                        tt(m, m, reg(CBM + g * 512, 512), ALU.mult, "~mdec")
                wait("diag_mm", 8 * (g + 1))
                for c in range(NCH):
                    y = reg(YTOK + c * 512, 512)
                    if c == 0:
                        if g:
                            wait("yt_mm", 4)
                        do(v.tensor_copy(y, bank(2)), "~ytok")
                    else:
                        wait("yoff_mm", 3 * g + c)
                        tt(y.rearrange("p (h d) -> p h d", h=8), bank(6).rearrange("p (h d) -> p h d", h=8),
                           cols(eacs[:, c * 16 + 8 * g:c * 16 + 8 * g + 8], HD), ALU.mult, "yoff")
                        tt(y, y, bank(2 + c), ALU.add, "~ytok")
                for m in range(4):
                    k = 4 * g + m
                    wait("yt_mm", k + 1)
                    y = reg(YMIX + (4 + k) * T, T)
                    stt(y, reg(CONV + k * T, T), pr("d_skip", k), bank(m % 2), ALU.mult, ALU.add)
                    tt(y, y, reg(Z + k * T, T), ALU.mult, "~yt_ready" if k < 7 else "yt_ready")
            wait("rt2", 1)
            do(v.reciprocal(RS[:, 0:T], RS[:, 0:T]))
            for k in range(KT):
                y = reg(YMIX + (4 + k) * T, T)
                stt(y, y, pr("ssd_norm", k), RS[:, 0:T], ALU.mult, ALU.mult, "~ymix" if k < 7 else "ymix")
            for g in range(POOL_G):
                wait("pool_mm", g + 1)
                ts(reg(YMIX + g * T, T), bank(2 * (g % 2)), pr("pool_b", g), pr("pool_scale", g), ALU.add, ALU.mult,
                   "pool_out")
            ev(tn, "out", 0)
            evacuate(tn, "out", 0, 8, lambda j, i: stt(
                A[:, bass.ds(i * (4 * T) + (X + j * T), T)], bank(2 * j), mod[:, bass.ds(i * 4 + (16 + j), 1)],
                A[:, bass.ds(i * (4 * T) + (X + j * T), T)], ALU.mult, ALU.add, "bank_free"))
            do(v.memset(tick[:, 4:5], 0.0), "x1_ready")
            stt(gsc[:, 0:8], mod[:, 32:40], 1.0, pr("norm_ffn"), ALU.add, ALU.mult)
            wait("rt3", 1)
            do(v.reciprocal(RS[:, 0:T], RS[:, 0:T]))
            modulated(H, X, 24, "h2_ready")

            def top16(rows, vals, idx, sem):
                def each(f, sem=None):
                    for n, s in enumerate(rows):
                        v0, v1 = reg(vals + n * 16, 8), reg(vals + n * 16 + 8, 8)
                        u0, u1 = (reg(idx + n * 16 + m, 8).bitcast(U32) for m in (0, 8))
                        do(f(s, v0, v1, u0, u1), sem if n == len(rows) - 1 else FREE)
                each(lambda s, v0, v1, u0, u1: v.max(v0, s))
                each(lambda s, v0, v1, u0, u1: v.max_index(u0, v0, s))
                each(lambda s, v0, v1, u0, u1: v.match_replace(s, v0, s, -3.0e38))
                each(lambda s, v0, v1, u0, u1: v.max(v1, s))
                each(lambda s, v0, v1, u0, u1: v.max_index(u1, v1, s), sem)

            sg = reg(SELX, 128), reg(SELX + 128, 128), reg(SELX + 256, 128)
            for i in range(4):
                wait("sc_set", i * 4 + 4)
                top16([reg(SC + hh * P, P) for hh in range(16)], PV, PUI, "sc_free")
                do(v.tensor_copy(reg(PIF, 256), reg(PUI, 256).bitcast(U32)))
                V4 = reg(PV, 256).rearrange("p (h x k) -> p h x k", h=PH, x=2)
                for h in range(PH):
                    tt(three(CAND + h * 256, 16, 16), bc(V4[:, h, 0, :].unsqueeze(2), [P, 16, 16]),
                       bc(V4[:, h, 1, :].unsqueeze(1), [P, 16, 16]), ALU.add, None if h == PH - 1 else FREE)
                top16([reg(CAND + h * 256, 256) for h in range(PH)], TV, TU, None)
                wait("slots_mm", i)
                tv3 = three(TV, PH, 16)
                tt(sg[2].rearrange("p (h k) -> p h k", h=PH), tv3, bc(tv3[:, :, 0:1], [P, PH, 16]), ALU.subtract,
                   "gate_x")
                tu = reg(TU, 128).bitcast(U32)
                tr, tc_ = reg(TU + 128, 128).bitcast(U32), reg(TU + 256, 128).bitcast(U32)
                do(v.tensor_scalar(tr, tu, 4, None, ALU.logical_shift_right))
                do(v.tensor_scalar(tc_, tu, 15, None, ALU.bitwise_and))
                do(v.tensor_copy(reg(TF, 256), reg(TU + 128, 256).bitcast(U32)))
                I4 = reg(PIF, 256).rearrange("p (h x k) -> p h x k", h=PH, x=2)
                for x in range(2):
                    for h in range(PH):
                        oh = three(OH + h * 256, 16, 16)
                        tt(oh, bc(con("iota16").unsqueeze(1), [P, 16, 16]),
                           bc(reg(TF + x * 128 + h * 16, 16).unsqueeze(2), [P, 16, 16]), ALU.is_equal,
                           None if h == PH - 1 else FREE)
                    for h in range(PH):
                        oh = three(OH + h * 256, 16, 16)
                        tt(oh, oh, bc(I4[:, h, x, :].unsqueeze(1), [P, 16, 16]), ALU.mult, None if h == PH - 1 else FREE)
                    do(v.tensor_reduce(sg[x], three(OH, 128, 16), AX.X, ALU.add))
                wait("gate_e", i + 1)
                g3 = sg[2].rearrange("p (h k) -> p h k", h=PH)
                do(v.tensor_reduce(small[:, 0:8], g3, AX.X, ALU.add))
                do(v.reciprocal(small[:, 0:8], small[:, 0:8]))
                tt(g3, g3, bc(small[:, 0:8].unsqueeze(2), [P, PH, 16]), ALU.mult, "sel")

            wait("slots_T", 8)
            with tn.loop(128 // GB, b_hot=GB) as i:
                for u_ in range(GB):
                    wait("g_mm", i * GB + (u_ + 1))
                    for out, src in ((OA, I1T), (OB, I2T)):
                        tt(three(out + u_ * 512, 4, P), bc(con("iota").unsqueeze(1), [P, 4, P]),
                           bc(A[:, bass.ds(i * (4 * GB) + (src + 4 * u_), 4)].unsqueeze(2), [P, 4, P]), ALU.is_equal,
                           "~b_hot" if out == OB else FREE)
            wait("g_stored0", 32)
            wait("g_stored1", 32)
            for k in range(0, 8 * T, 2 * T):
                do(v.tensor_copy(rr(HHI + k, 2 * T), reg(H + k, 2 * T)))
                tt(rr(H + k, 2 * T), reg(H + k, 2 * T), rr(HHI + k, 2 * T).bitcast(F32), ALU.subtract,
                   "hsplit" if k == 6 * T else FREE)
            do(v.memset(reg(YACC, 8 * T), 0.0))
            with tn.loop(EROUNDS, dve_own=2 * ER, e_w=ER, e_acc=8) as i:
                for r in range(ER):
                    wait(f"g_in{r}", i * 16 + 16)
                    wait("e_g", i * ER + (r + 1))
                    if r == 0:
                        wait("e_y", i * 8)
                    a_ = reg(ACTB + r * T, T)
                    tt(a_, a_, reg(GRING + r * T, T), ALU.mult)
                    do(v.tensor_copy(rr(WHI + r * T, T), a_))
                    tt(rr(WLO + r * T, T), a_, rr(WHI + r * T, T).bitcast(F32), ALU.subtract, "e_w")
                for d in range(KT):
                    wait("e_y", i * 8 + (d + 1))
                    tt(reg(YACC + d * T, T), reg(YACC + d * T, T), bank(4 + d % 4), ALU.add, "~e_acc" if d < 7 else "e_acc")
            wait("unspilled", 16)
            for k in range(KT):
                y = reg(YACC + k * T, T)
                stt(y, y, mod[:, 40 + k:41 + k], reg(X + k * T, T), ALU.mult, ALU.add,
                    "~xf_ready" if k < 7 else "xf_ready")
            wait("rt4", 1)
            do(v.reciprocal(RS[:, 0:T], RS[:, 0:T]))
            for k in range(KT):
                stt(reg(X + k * T2 + META, T), reg(YACC + k * T, T), pr("norm_final", k), RS[:, 0:T], ALU.mult, ALU.mult,
                    "~h2in" if k < 7 else "h2in")

            def norm2(src, gname, sem, rt, out=XN):
                wait(rt, 1)
                do(v.reciprocal(RS[:, 0:T2], RS[:, 0:T2]))
                for k in range(KT):
                    stt(reg(out + k * T2, T2), reg(src + k * T2, T2), pr(gname, k), RS[:, 0:T2], ALU.mult, ALU.mult,
                        ("~" + sem if k < 7 else sem) if sem else (FREE if k < 7 else None))
            wait("meta_in", 16)
            norm2(X, "g_mix_pre", "xn_ready", "rt5")

            def in_parts(src, hi, sem, use="p", use_hi="l", before=None):
                for k in range(KT):
                    do(v.tensor_copy(rr(hi + k * T2, T2, use_hi), reg(src + k * T2, T2)), FREE if k < 7 else None)
                if before:
                    wait(before, 1)
                for k in range(KT):
                    tt(rr(src + k * T2, T2, use), reg(src + k * T2, T2), rr(hi + k * T2, T2, use_hi).bitcast(F32),
                       ALU.subtract, FREE if k < 7 else sem)
            in_parts(XN, XH1, "xn_split", "l", "p", before="alow_mm")
            for h in range(GLH):
                wait("gate_mm", h + 1)
                ts(halves(reg(LA + h * T2, T2)), pair(h), pr("b_gate", h), None, ALU.add,
                   sem="~gate_lin" if h < 3 else "gate_lin")
            wait("ln_e", 1)
            L4, D4, E4 = reg(LA, 4 * T2), reg(DD, 4 * T2), reg(EE, 4 * T2)
            stt(L4, L4, 0.0, E4, ALU.min, ALU.subtract)
            ts(L4, L4, 1.0 / 16, None, ALU.mult)
            for h in range(GLH):
                do(v.tensor_tensor_scan(reg(DD + h * T2, T2), con("mask64"), reg(LA + h * T2, T2), 0.0, ALU.mult, ALU.add))
            d4 = D4.rearrange("p (h t) -> p h t", h=GLH)
            l4 = L4.rearrange("p (h t) -> p h t", h=GLH)
            do(v.tensor_copy(l4[:, :, 0:META], d4[:, :, 0:META]))
            for h in range(GLH):
                dh = d4[:, h, META:T2].rearrange("p (c l) -> p c l", l=GC)
                lh = l4[:, h, META:T2].rearrange("p (c l) -> p c l", l=GC)
                tt(lh, dh, bc(dh[:, :, GC // 2:GC // 2 + 1], [P, 8, GC]), ALU.subtract, "gd" if h == 3 else None)
            Q4, K4 = reg(PQ, 4 * T2), reg(PK, 4 * T2)
            scale = float(P) ** -0.5
            wait("bank_free", 4 + tiles["in2"] + 8)
            wait("ge1", 1)
            ts(Q4, Q4, scale, None, ALU.mult)
            tt(reg(QIN, 4 * T2), Q4, E4, ALU.mult, "gq")
            wait("ge2", 1)
            tt(reg(KIN, 4 * T2), K4, E4, ALU.mult, "gq")
            dec = reg(DEC, 36).rearrange("p (h c) -> p h c", h=GLH)
            for h in range(GLH):
                dh = d4[:, h, META:T2].rearrange("p (c l) -> p c l", l=GC)
                lh = l4[:, h, META:T2].rearrange("p (c l) -> p c l", l=GC)
                tt(lh, bc(dh[:, :, GC - 1:GC], [P, 8, GC]), dh, ALU.subtract)
                do(v.tensor_copy(dec[:, h, 1:9].unsqueeze(2), dh[:, :, GC - 1:GC]))
            tt(l4[:, :, 0:META], bc(d4[:, :, META - 1:META], [P, GLH, META]), d4[:, :, 0:META], ALU.subtract)
            do(v.tensor_copy(dec[:, :, 0:1], d4[:, :, META - 1:META]))
            wait("ge3", 1)
            tt(Q4, Q4, E4, ALU.mult, "gq")
            wait("ge4", 1)
            tt(K4, K4, E4, ALU.mult, "gq")
            for c, (t0, L) in enumerate(GCH):
                wait("gla_tr", c + 1)
                do(v.tensor_copy(reg(KTOK, 512, L), PS[0:L, 0:512]), "ktok")
                wait("gla_sc", c + 1)
                tt(reg(SM, 256, L).rearrange("p (h l) -> p h l", h=4)[:, :, 0:L],
                   PS[0:L, 1536:1792].rearrange("p (h l) -> p h l", h=4)[:, :, 0:L],
                   bc(causal[0:L, 0:L].unsqueeze(1), [L, 4, L]), ALU.mult, "sm")
                if c < len(GCH) - 1:
                    wait("gla_st", c + 1)
                    for h in range(GLH):
                        st = reg(ST + h * DV, DV)
                        new = PS[:, 3072 + h * DV:3072 + (h + 1) * DV]
                        if c == 0:
                            do(v.tensor_copy(st, new), "st")
                        else:
                            stt(st, st, dec[:, h, c:c + 1], new, ALU.mult, ALU.add, "st")
            wait("o_set", 9)
            for k in range(KT):
                do(v.tensor_copy(rr(XH2 + k * T2, T2, "p"), rr(XH1 + k * T2, T2, "p")), FREE if k < 7 else "xn_moved")
            wait("rt6", 4)
            do(v.reciprocal(L4, L4))
            for m in range(8):
                o = reg(PVV + m * T2, T2)
                stt(o, o, pr("gla_norm", m), reg(LA + (m // 2) * T2, T2), ALU.mult, ALU.mult, FREE if m < 7 else None)
            wait("bank_free", 4 + tiles["r2"] + 16)
            for m in range(8):
                o = reg(PVV + m * T2, T2)
                tt(o, o, reg(RR + m * T2, T2), ALU.mult, FREE if m < 7 else None)
            in_parts(PVV, XH2, "o_split", use_hi="p")
            ev(tn, "ogla", 0)
            evacuate(tn, "ogla", 0, 8, lambda j, i: tt(
                halves(A[:, bass.ds(i * (4 * T2) + (PZG + j * T2), T2)]), pair(j),
                halves(A[:, bass.ds(i * (4 * T2) + (PZG + j * T2), T2)]), ALU.mult, "bank_free"))
            do(v.memset(reg(TT_, 1024), 0.0), "ogla_out")

            def reduced(x, t, n):
                ts(t, x, 1.0 / TWO_PI, MAGIC, ALU.mult, ALU.add)
                ts(t, t, MAGIC, None, ALU.subtract)
                stt(x, t, -C1, x, ALU.mult, ALU.add)
                stt(x, t, -C2, x, ALU.mult, ALU.add)
                ts(x, x, -PI_IN, PI_IN, ALU.max, ALU.min)
            r = lambda off: reg(off, 64)
            ar, ai = r(S5A), r(S5A + 64)
            wait("s5_e", 1)
            tt(r(AR5), ar, r(DT5), ALU.mult)
            tt(r(TH5), ai, r(DT5), ALU.mult)
            t0_ = reg(T5, 64)
            ts(t0_, r(TH5), 1.0 / TWO_PI, MAGIC, ALU.mult, ALU.add)
            ts(t0_, t0_, MAGIC, None, ALU.subtract)
            stt(r(TH5), t0_, -C1, r(TH5), ALU.mult, ALU.add)
            stt(r(TH5), t0_, -C2, r(TH5), ALU.mult, ALU.add)
            ts(r(SN1), r(TH5), -PI_IN, PI_IN, ALU.max, ALU.min)
            ts(r(CS1), r(TH5), np.pi / 2, None, ALU.add)
            reduced(r(CS1), t0_, 64)
            ts(r(PH5), r(TH5), float(SB), None, ALU.mult)
            reduced(r(PH5), t0_, 64)
            do(v.memset(tick[:, 4:5], 0.0), "s5_x")
            kk = bc(con("kk").unsqueeze(1), [P, S5G, SB + 1])
            t3 = lambda off: three(off, S5G, SB + 1)
            tt(t3(LMG), kk, bc(r(AR5).unsqueeze(2), [P, S5G, SB + 1]), ALU.mult)
            tt(t3(LI), kk, bc(r(TH5).unsqueeze(2), [P, S5G, SB + 1]), ALU.mult)
            ts(reg(LR, 576), reg(LI, 576), np.pi / 2, None, ALU.add)
            reduced(reg(LI, 576), reg(T5, 576), 576)
            reduced(reg(LR, 576), reg(T5, 576), 576)
            do(v.memset(tick[:, 4:5], 0.0), "s5_x")
            wait("s5_e", 5)
            a1, a2, a3 = reg(T5, 64), reg(T5 + 64, 64), reg(T5 + 128, 64)
            tt(a1, r(MG1), r(CS1), ALU.mult)
            ts(a1, a1, 1.0, None, ALU.subtract)
            tt(a2, r(MG1), r(SN1), ALU.mult)
            tt(r(FR), a1, ar, ALU.mult)
            tt(a3, a2, ai, ALU.mult)
            tt(r(FR), r(FR), a3, ALU.add)
            tt(r(FI), a2, ar, ALU.mult)
            tt(a3, a1, ai, ALU.mult)
            tt(r(FI), r(FI), a3, ALU.subtract)
            tt(a1, ar, ar, ALU.mult)
            tt(a2, ai, ai, ALU.mult)
            tt(a1, a1, a2, ALU.add)
            do(v.reciprocal(a1, a1))
            tt(r(FR), r(FR), a1, ALU.mult)
            tt(r(FI), r(FI), a1, ALU.mult)
            wait("s5_e", 8)
            tt(reg(LR, 576), reg(LR, 576), reg(LMG, 576), ALU.mult)
            tt(reg(LI, 576), reg(LI, 576), reg(LMG, 576), ALU.mult)
            PB, QB, PC, QC = (S5P + 1024 * n for n in range(4))
            b3 = lambda off: three(off, S5G, S5H)
            f3 = lambda off: bc(r(off).unsqueeze(2), [P, S5G, S5H])
            ts(reg(QB, 1024), reg(QB, 1024), con("sgn"), None, ALU.mult)
            ts(reg(PC, 1024), reg(PC, 1024), con("nsgn"), None, ALU.mult)
            ts(reg(QC, 1024), reg(QC, 1024), -1.0, None, ALU.mult)
            tt(b3(WT), b3(PB), f3(FI), ALU.mult)
            tt(b3(V9A), b3(QB), f3(FI), ALU.mult)
            tt(b3(PB), b3(PB), f3(FR), ALU.mult)
            tt(b3(QB), b3(QB), f3(FR), ALU.mult)
            tt(reg(PB, 1024), reg(PB, 1024), reg(V9A, 1024), ALU.add)
            tt(reg(QB, 1024), reg(QB, 1024), reg(WT, 1024), ALU.subtract)

            def outer(out, l, b, n, sem=None):
                for g in range(GP):
                    tt(out[:, g], bc(l[:, g, 0:n].unsqueeze(2), [P, n, S5H]), bc(b[:, g, :].unsqueeze(1), [P, n, S5H]),
                       ALU.mult, sem if g == GP - 1 else FREE)

            def part(i, u, off, n):
                return s5_at(i, u, off, n).rearrange("p (g h) -> p g h", g=GP)

            def gsh(off, n):
                return reg(off, n * P).rearrange("p (g s h) -> p g s h", g=GP, s=n)

            def s5_WT(i, u):
                tmp = (V9A, V9B)[u % 2]
                outer(gsh(WT, SB), part(i, u, LR, 72), part(i, u, PB, 128), SB, FREE)
                outer(gsh(tmp, SB), part(i, u, LI, 72), part(i, u, QB, 128), SB)
                tt(reg(WT, 1024), reg(WT, 1024), reg(tmp, 1024), ALU.add, "s5_WT")

            def s5_tables(i, u):
                v9 = (V9A, V9B)[u % 2]
                wait("s5_Wmm", s5_count(i, u, 1, 1))
                outer(gsh(v9, SB + 1), part(i, u, LR, 72), part(i, u, PC, 128), SB + 1, FREE)
                do(v.tensor_copy(reg(BBP, 128), s5_at(i, u, PB, 128)), FREE)
                outer(gsh(WT, SB + 1), part(i, u, LI, 72), part(i, u, QC, 128), SB + 1)
                tt(reg(v9, 1152), reg(v9, 1152), reg(WT, 1152), ALU.add, "s5_V9")
                tt(three(ANG, GP, NB), bc(con("cidx").unsqueeze(1), [P, GP, NB]),
                   bc(s5_at(i, u, PH5, 8).unsqueeze(2), [P, GP, NB]), ALU.mult)
                ts(reg(ANG2, 528), reg(ANG, 528), np.pi / 2, None, ALU.add)
                reduced(reg(ANG, 1056), reg(T5, 1056), 1056)
                do(v.memset(tick[:, 4:5], 0.0), "s5_ang")
                tt(three(MSK, GP, NB), bc(con("cmask").unsqueeze(1), [P, GP, NB]),
                   bc(s5_at(i, u, MG8, 8).unsqueeze(2), [P, GP, NB]), ALU.mult)

            def s5_part(i, u, more):
                wait("s5_cs", s5_count(i, u, 2, 2))
                wait("s5_S", s5_count(i, u, 1, 1))
                wait("s5_Zmm", s5_count(i, u, 2, 1))
                tt(reg(SS, 528), reg(SS, 528), reg(COS, 528), ALU.mult, FREE)
                tt(halves(reg(S2, 528)), halves(reg(SIN, 528)), pair(3), ALU.mult)
                tt(reg(SS, 528), reg(SS, 528), reg(S2, 528), ALU.add)
                do(v.tensor_tensor_scan(reg(S2, 528), reg(MSK, 528), reg(SS, 528), 0.0, ALU.mult, ALU.add), "s5_w")
                if more:
                    s5_WT(i, u + 1)
                wait("s5_Zmm", s5_count(i, u, 2, 2))
                tt(reg(SS, 528), reg(S2, 528), reg(COS, 528), ALU.mult, FREE)
                tt(halves(reg(T5, 528)), halves(reg(SIN, 528)), pair(3), ALU.mult)
                tt(reg(SS, 528), reg(SS, 528), reg(T5, 528), ALU.subtract, "s5_H")
                if more:
                    s5_tables(i, u + 1)

            s5_WT(None, 0)
            s5_tables(None, 0)
            with tn.loop(3, dve_own=26, s5_WT=2, s5_ang=2, s5_V9=2, s5_w=2, s5_H=2) as i:
                s5_part(i, 0, True)
                s5_part(i, 1, True)
            s5_part(None, 6, True)
            s5_part(None, 7, False)
            wait("y8_in", 16)
            for m in range(8):
                y = reg(Y8 + m * T2, T2)
                stt(y, reg(PU + m * T2, T2), pr("d_skip_2", m), y, ALU.mult, ALU.add, "~s5_out")
            wait("gs", 8)
            in_parts(PU, XH3, "gs_split")
            wait("bank_free", 4 + tiles["glu"] + 16)
            tt(reg(Y8, XW), reg(Y8, XW), reg(YALL, XW), ALU.mult)
            tt(reg(Y8, XW), reg(Y8, XW), reg(PZS, XW), ALU.mult)
            tt(reg(PZG, XW), reg(PZG, XW), reg(Y8, XW), ALU.add)
            in_parts(PZG, XH3, "mixed")

            def residual(src, gname, rt, sem):
                wait(rt, 1)
                do(v.reciprocal(RS[:, 0:T2], RS[:, 0:T2]))
                for k in range(KT):
                    s = reg(src + k * T2, T2)
                    stt(s, s, pr(gname, k), RS[:, 0:T2], ALU.mult, ALU.mult, FREE if k < 7 else None)
                for k in range(KT):
                    tt(reg(X + k * T2, T2), reg(X + k * T2, T2), reg(src + k * T2, T2), ALU.add, "~" + sem if k < 7 else sem)
            residual(MO, "g_mix_post", "rt7", "h_mid")
            norm2(X, "g_ffn_pre", None, "rt8")
            in_parts(XN, XH3, "hn_split", "l")
            for half in "ab":
                with tn.loop(4, dve_own=8, ff_split=4) as i:
                    for j in range(4):
                        wait("bank_free", i * 4 + (5 + tiles["ff1" + half] + j))
                        f = A[:, bass.ds(i * T2 + (FF + j * 4 * T2), T2)]
                        fh = parts_r["f", FFH + j * 4 * T2][1][:, bass.ds(i * T2, T2)]
                        fl = parts_r["f", FF + j * 4 * T2][1][:, bass.ds(i * T2, T2)]
                        tt(f, f, f, ALU.mult)
                        do(v.tensor_copy(fh, f))
                        tt(fl, f, fh.bitcast(F32), ALU.subtract, "ff_split")
            ev(tn, "ff2b", 0)
            def add_mo(j, i):
                o = halves(A[:, bass.ds(i * (4 * T2) + (MO + j * T2), T2)])
                tt(o, o, pair(j), ALU.add, "bank_free")
            evacuate(tn, "ff2b", 0, 8, add_mo)
            do(v.memset(tick[:, 4:5], 0.0), "mo_sum")
            residual(MO, "g_ffn_post", "rt9", "h_end")
            do(v.memset(tick[:, 4:5], 0.0), "fin")


def constants():
    c = np.zeros((P, NCONST), np.float32)

    def put(name, a):
        o, w = CONST[name]
        c[:, o:o + w] = a
    n = np.arange(P)
    put("ident", np.eye(P))
    put("causal", n[:, None] <= n[None, :])
    put("ones", 1.0)
    sw = np.zeros((P, P))
    h = P // 2
    sw[h + np.arange(h), np.arange(h)] = 1.0
    sw[np.arange(h), h + np.arange(h)] = -1.0
    put("swap", sw)
    put("iota", n[None, :])
    put("iota16", np.arange(16)[None, :])
    put("mask64", (~np.isin(np.arange(T2), [t0 for t0, _ in GCH]))[None, :])
    put("mask128", (np.arange(T) % CH != 0)[None, :])
    t = np.arange(16)
    put("invcnt", np.concatenate([1.0 / np.minimum(t + 1, 2 << g) for g in range(POOL_G)])[None, :])
    put("cidx", np.arange(NB)[None, :])
    put("cmask", (np.arange(NB) > 0)[None, :])
    put("kk", np.arange(SB + 1)[None, :])
    put("sgn", np.where(n < h, -1.0, 1.0)[:, None])
    put("nsgn", np.where(n < h, 1.0, -1.0)[:, None])
    sel = np.zeros((16, 16, P), np.float32)
    sel[np.arange(16), np.arange(16), :] = 1.0
    return c, sel.reshape(16, 2048)


def tiled(w, kt=8):
    K, M = w.shape
    return np.ascontiguousarray(w.reshape(K // (kt * P), kt, P, M // P, P).transpose(3, 0, 2, 1, 4)
                                .reshape(M // P * (K // (kt * P)), P, kt * P))


def feat(v):
    return v.reshape(-1, P).T


def kernel(**inp):
    from concourse import bacc
    from concourse.bass_utils import run_bass_kernel_spmd

    i = {k: np.asarray(v) for k, v in inp.items()}
    s_z, s_x = 512, 1536
    s_dt = s_x + 1536
    w_in = i["w_in"][0]
    arr = {}
    arr["consts"], arr["sel"] = constants()
    arr["params"] = np.ascontiguousarray(np.concatenate([
        feat(i["norm_mix"][0]), feat(i["norm_ffn"][0]), feat(i["norm_final"]), feat(i["ssd_norm"][0]),
        feat(i["b_ada"][0]), feat(i["pool_b"][0].reshape(-1)), feat(i["pool_scale"][0].reshape(-1)),
        i["conv_w"][0].reshape(4, 12, P).transpose(2, 1, 0).reshape(P, 48), feat(i["conv_b"][0]),
        feat(np.repeat(i["d_skip"][0], HD)), feat(i["g_mix_pre_2"][0]), feat(i["g_mix_post_2"][0]),
        feat(i["g_ffn_pre_2"][0]), feat(i["g_ffn_post_2"][0]), feat(i["gla_norm_g_2"][0].reshape(-1)),
        feat(i["b_gate_2"][0]), feat(i["d_skip_2"][0]), feat(i["b_glu_2"][0])], axis=1))
    w2 = i["w_in_2"][0]
    q, k, v, r, al, u, g1 = 512, 1024, 2048, 3072, 3088, 4112, 5136
    lay16 = lambda w: w.reshape(8, P, 16).transpose(1, 0, 2).reshape(P, 128)
    arr["w16"] = np.ascontiguousarray(np.concatenate([lay16(w_in[:, s_dt:]), lay16(w2[:, r:al])], axis=1))
    arr["dtal"] = np.ascontiguousarray(np.stack([i["dt_bias"][0], i["a_log"][0]], axis=1))
    arr["xT"] = np.ascontiguousarray(i["x"][0].T)
    arr["c"] = np.ascontiguousarray(i["c"])
    arr["w_ada"] = np.ascontiguousarray(i["w_ada"][0].T.reshape(48, P, D))
    arr["w_in"] = tiled(np.concatenate([w_in[:, s_x:s_dt], w_in[:, s_z:s_x], w_in[:, :s_z]], axis=1))
    arr["w_out"] = tiled(i["w_out"][0], 12)
    arr["w_query"] = tiled(i["w_query"][0])
    arr["keys"] = np.ascontiguousarray(np.stack([i["sub_keys1"][0], i["sub_keys2"][0]], axis=1).transpose(3, 0, 1, 2)
                                       .reshape(P, 2048))
    arr["pool_w"] = np.ascontiguousarray(i["pool_w"][0])
    arr["down"] = np.ascontiguousarray(i["expert_down"][0].reshape(P, NKEY, KT, P).transpose(1, 3, 2, 0)
                                       .reshape(NKEY, P, D))
    arr["up"] = np.ascontiguousarray(i["expert_up"][0].reshape(P, NKEY, D).transpose(1, 0, 2))
    arr["metaT"] = np.ascontiguousarray(i["meta_tokens_2"].T)
    arr["w_gate_up"] = np.ascontiguousarray(i["w_gate_up_2"][0])
    arr["w_in2"] = tiled(np.concatenate([w2[:, :v], w2[:, al:g1]], axis=1))
    arr["w_r2"] = tiled(np.concatenate([w2[:, g1:], w2[:, v:r]], axis=1))
    arr["w_ogla"] = tiled(i["w_o_gla_2"][0])
    arr["w_glu"] = tiled(i["w_glu_2"][0])
    arr["w_out2"] = tiled(i["w_out_2"][0])
    for half, o in (("a", 0), ("b", 2048)):
        arr["w_ff1" + half] = tiled(i["w_ff1_2"][0][:, o:o + 2048])
        arr["w_ff2" + half] = tiled(i["w_ff2_2"][0][o:o + 2048])
    twice = lambda a, b: np.concatenate([a, b], axis=0)
    s = lambda name: i[name][0]
    arr["s5a"] = np.ascontiguousarray(np.concatenate([
        twice(s("a_re_2").T, s("a_re_2").T), twice(s("a_im_2").T, s("a_im_2").T),
        np.broadcast_to(s("log_step_2")[None], (P, S5G))], axis=1))
    bt = lambda name: s(name).transpose(1, 0, 2).reshape(S5N, S5G * S5H)
    ct = lambda name: s(name).transpose(2, 0, 1).reshape(S5N, S5G * S5H)
    arr["s5bc"] = np.ascontiguousarray(np.concatenate([
        twice(bt("b_re_2"), bt("b_im_2")), twice(bt("b_im_2"), bt("b_re_2")),
        twice(ct("c_re_2"), ct("c_im_2")), twice(ct("c_im_2"), ct("c_re_2"))], axis=1))

    nc = bacc.Bacc("TRN2", target_bir_lowering=False, num_devices=1)
    io = {n: nc.dram_tensor(f"in_{n}", a.shape, F32, kind="ExternalInput").ap() for n, a in arr.items()}
    io["out"] = nc.dram_tensor("out_0", (D, T), F32, kind="ExternalOutput").ap()
    for n, shape in (("gates", (NKEY, P, T)), ("spill", (P, KT * T)), ("u_d", (8, P, T2)), ("y_d", (8, P, T2))):
        io[n] = nc.dram_tensor(f"scratch_{n}", shape, F32, kind="Internal").ap()
    build(nc, io)
    res = run_bass_kernel_spmd(nc, [{f"in_{n}": a for n, a in arr.items()}], core_ids=[0])
    return np.ascontiguousarray(res.results[0]["out_0"].T)[None]
```
